# Optimizing a Trainium2 kernel written in Bass

```python
import jax, jax.numpy as jnp
from jax import lax
import numpy as np

D_MODEL = 1024
BATCH = 1
SEQ = 512
DEPTH = 1

GRID_W = 64
NA_HEADS = 8
NA_HEAD_DIM = 64
NA_WIDTH = NA_HEADS * NA_HEAD_DIM
WIN_H_MAX = 8
WIN_W = 16
GLA_HEADS = 4
GLA_DK = 64
GLA_DV = 128
GLA_KEY_WIDTH = GLA_HEADS * GLA_DK
GLA_VAL_WIDTH = GLA_HEADS * GLA_DV
GLA_GATE_RANK = 16
GLA_GATE_NORMALIZER = 16.0
GLA_CHUNK = 64
MIX_WIDTH = NA_WIDTH + GLA_VAL_WIDTH
IN_SIZES = (NA_WIDTH, NA_WIDTH, NA_WIDTH, GLA_KEY_WIDTH, GLA_KEY_WIDTH, GLA_VAL_WIDTH, GLA_VAL_WIDTH, GLA_GATE_RANK, GLA_GATE_RANK)
IN_PROJ_WIDTH = sum(IN_SIZES)
N_GROUPS = 4
EXPERTS_PER_GROUP = 8
N_EXPERTS = N_GROUPS * EXPERTS_PER_GROUP
TOP_K_IN_GROUP = 2
D_FF_EXPERT = 512
RMS_EPS = 1e-6

kernel_name = 'hybrid_na_gla_hiermoe_encoder'

def rmsnorm(x, g):
    xf = x.astype(jnp.float32)
    y = xf * lax.rsqrt(jnp.mean(xf * xf, axis=-1, keepdims=True) + RMS_EPS)
    return (y * g.astype(jnp.float32)).astype(x.dtype)

def neighbourhood_attention(q, k, v, rpb):
    B, T, H, dh = q.shape
    rows = T // GRID_W
    kh = min(WIN_H_MAX, rows)
    r = jnp.arange(rows)
    row_idx = jnp.clip(r - kh // 2, 0, rows - kh)[:, None] + jnp.arange(kh)[None, :]
    c = jnp.arange(GRID_W)
    col_idx = jnp.clip(c - WIN_W // 2, 0, GRID_W - WIN_W)[:, None] + jnp.arange(WIN_W)[None, :]
    qg = q.reshape(B, rows, GRID_W, H, dh) * (dh ** -0.5)
    kg = k.reshape(B, rows, GRID_W, H, dh)
    vg = v.reshape(B, rows, GRID_W, H, dh)
    k_rows = kg[:, row_idx]
    v_rows = vg[:, row_idx]
    s_rows = jnp.einsum('brwhd,brixhd->bhrwix', qg, k_rows)
    sel = (col_idx[:, :, None] == jnp.arange(GRID_W)[None, None, :]).astype(q.dtype)
    s_win = jnp.einsum('bhrwix,wjx->bhrwij', s_rows, sel)
    roff = row_idx - r[:, None] + (WIN_H_MAX - 1)
    coff = col_idx - c[:, None] + (WIN_W - 1)
    bias = rpb[:, roff[:, None, :, None], coff[None, :, None, :]]
    logits = s_win.astype(jnp.float32) + bias[None].astype(jnp.float32)
    p = jax.nn.softmax(logits.reshape(B, H, rows, GRID_W, kh * WIN_W), axis=-1)
    p = p.reshape(B, H, rows, GRID_W, kh, WIN_W).astype(v.dtype)
    p_rows = jnp.einsum('bhrwij,wjx->bhrwix', p, sel)
    out = jnp.einsum('bhrwix,brixhd->brwhd', p_rows, v_rows)
    return out.reshape(B, T, H * dh)

def gla_chunked(q, k, v, g, strict):
    B, H, T, dk = q.shape
    dv = v.shape[-1]
    n = T // GLA_CHUNK
    q = q.reshape(B, H, n, GLA_CHUNK, dk)
    k = k.reshape(B, H, n, GLA_CHUNK, dk)
    v = v.reshape(B, H, n, GLA_CHUNK, dv)
    g = g.reshape(B, H, n, GLA_CHUNK, dk)
    b = jnp.cumsum(g, axis=3)
    b_ref = b[:, :, :, GLA_CHUNK // 2 - 1:GLA_CHUNK // 2, :]
    q_rel = q * jnp.exp(b - b_ref)
    k_rel = k * jnp.exp(b_ref - b)
    mask = jnp.tril(jnp.ones((GLA_CHUNK, GLA_CHUNK), dtype=bool), -1 if strict else 0)
    scores = jnp.where(mask, jnp.einsum('bhnik,bhnjk->bhnij', q_rel, k_rel), 0.0)
    o_intra = jnp.einsum('bhnij,bhnjv->bhniv', scores, v)
    b_last = b[:, :, :, -1:, :]
    chunk_state = jnp.einsum('bhnjk,bhnjv->bhnkv', k * jnp.exp(b_last - b), v)
    chunk_decay = jnp.exp(b_last[:, :, :, 0, :])

    def step(S, inp):
        dec, st = inp
        return dec[..., None] * S + st, S

    S0 = jnp.zeros((B, H, dk, dv), jnp.float32)
    _, S_prev = lax.scan(step, S0, (jnp.moveaxis(chunk_decay, 2, 0), jnp.moveaxis(chunk_state, 2, 0)))
    S_prev = jnp.moveaxis(S_prev, 0, 2)
    o_inter = jnp.einsum('bhnik,bhnkv->bhniv', q * jnp.exp(b), S_prev)
    return (o_intra + o_inter).reshape(B, H, T, dv)

def gla_mixer(q, k, v, r, glr_f, glr_b, w_g2_f, b_g_f, w_g2_b, b_g_b, norm_g):
    B, T, _ = q.shape
    f32 = jnp.float32
    heads = lambda a, d: a.astype(f32).reshape(B, T, GLA_HEADS, d).transpose(0, 2, 1, 3)
    qh = heads(q, GLA_DK) * (GLA_DK ** -0.5)
    kh = heads(k, GLA_DK)
    vh = heads(v, GLA_DV)
    g_f = heads(jax.nn.log_sigmoid(glr_f.astype(f32) @ w_g2_f.astype(f32) + b_g_f.astype(f32)) / GLA_GATE_NORMALIZER, GLA_DK)
    g_b = heads(jax.nn.log_sigmoid(glr_b.astype(f32) @ w_g2_b.astype(f32) + b_g_b.astype(f32)) / GLA_GATE_NORMALIZER, GLA_DK)
    o_fwd = gla_chunked(qh, kh, vh, g_f, strict=False)
    flip = lambda a: jnp.flip(a, axis=2)
    o_bwd = flip(gla_chunked(flip(qh), flip(kh), flip(vh), flip(g_b), strict=True))
    o = o_fwd + o_bwd
    o = o * lax.rsqrt(jnp.mean(o * o, axis=-1, keepdims=True) + RMS_EPS) * norm_g.astype(f32)
    o = o.transpose(0, 2, 1, 3).reshape(B, T, GLA_VAL_WIDTH).astype(r.dtype)
    return o * jax.nn.silu(r)

def hybrid_mixer(h, w_in, w_g2_f, b_g_f, w_g2_b, b_g_b, gla_norm_g, rpb, w_out):
    B, T, _ = h.shape
    proj = h @ w_in
    cuts = [int(c) for c in np.cumsum(IN_SIZES)[:-1]]
    na_q, na_k, na_v, g_q, g_k, g_v, g_r, g_lf, g_lb = jnp.split(proj, cuts, axis=-1)
    nh = lambda a: a.reshape(B, T, NA_HEADS, NA_HEAD_DIM)
    y_na = neighbourhood_attention(nh(na_q), nh(na_k), nh(na_v), rpb)
    y_gla = gla_mixer(g_q, g_k, g_v, g_r, g_lf, g_lb, w_g2_f, b_g_f, w_g2_b, b_g_b, gla_norm_g)
    return jnp.concatenate([y_na, y_gla], axis=-1) @ w_out

def hierarchical_moe(h, w_grp, b_grp, w_exp, b_exp, w_gate, w_up, w_down):
    B, T, D = h.shape
    x = h.reshape(B * T, D)
    f32 = jnp.float32
    grp_logits = (x @ w_grp + b_grp).astype(f32)
    grp_prob = jax.nn.softmax(grp_logits, axis=-1)
    g_sel = jnp.argmax(grp_logits, axis=-1)
    grp_w = jnp.take_along_axis(grp_prob, g_sel[:, None], axis=-1)
    exp_logits = (x @ w_exp + b_exp).astype(f32).reshape(B * T, N_GROUPS, EXPERTS_PER_GROUP)
    in_grp = jnp.take_along_axis(exp_logits, g_sel[:, None, None], axis=1)[:, 0]
    top_v, top_i = lax.top_k(in_grp, TOP_K_IN_GROUP)
    top_w = jax.nn.softmax(top_v, axis=-1) * grp_w
    expert_id = g_sel[:, None] * EXPERTS_PER_GROUP + top_i
    combine = jnp.sum(jax.nn.one_hot(expert_id, N_EXPERTS, dtype=f32) * top_w[..., None], axis=1).astype(x.dtype)
    y = jnp.zeros_like(x)
    for e in range(N_EXPERTS):
        hid = jax.nn.silu(x @ w_gate[e]) * (x @ w_up[e])
        y = y + combine[:, e:e + 1] * (hid @ w_down[e])
    return y.reshape(B, T, D)

def setup_inputs(seed: int = 0) -> dict:
    key = jax.random.key(seed)
    ks = jax.random.split(key, 20)
    nrm = lambda k, shape, scale: jax.random.normal(k, shape, jnp.float32) * scale
    L = DEPTH
    return {
        'x': nrm(ks[0], (BATCH, SEQ, D_MODEL), 1.0),
        'norm_mix_g': 1.0 + nrm(ks[1], (L, D_MODEL), 0.01),
        'w_in': nrm(ks[2], (L, D_MODEL, IN_PROJ_WIDTH), D_MODEL ** -0.5),
        'w_g2_f': nrm(ks[3], (L, GLA_GATE_RANK, GLA_KEY_WIDTH), GLA_GATE_RANK ** -0.5),
        'b_g_f': nrm(ks[4], (L, GLA_KEY_WIDTH), 0.1),
        'w_g2_b': nrm(ks[5], (L, GLA_GATE_RANK, GLA_KEY_WIDTH), GLA_GATE_RANK ** -0.5),
        'b_g_b': nrm(ks[6], (L, GLA_KEY_WIDTH), 0.1),
        'gla_norm_g': 1.0 + nrm(ks[7], (L, GLA_DV), 0.01),
        'rpb': nrm(ks[8], (L, NA_HEADS, 2 * WIN_H_MAX - 1, 2 * WIN_W - 1), 0.02),
        'w_out': nrm(ks[9], (L, MIX_WIDTH, D_MODEL), MIX_WIDTH ** -0.5),
        'norm_ffn_g': 1.0 + nrm(ks[10], (L, D_MODEL), 0.01),
        'w_grp': nrm(ks[11], (L, D_MODEL, N_GROUPS), D_MODEL ** -0.5),
        'b_grp': nrm(ks[12], (L, N_GROUPS), 0.01),
        'w_exp': nrm(ks[13], (L, D_MODEL, N_EXPERTS), D_MODEL ** -0.5),
        'b_exp': nrm(ks[14], (L, N_EXPERTS), 0.01),
        'w_gate': nrm(ks[15], (L, N_EXPERTS, D_MODEL, D_FF_EXPERT), D_MODEL ** -0.5),
        'w_up': nrm(ks[16], (L, N_EXPERTS, D_MODEL, D_FF_EXPERT), D_MODEL ** -0.5),
        'w_down': nrm(ks[17], (L, N_EXPERTS, D_FF_EXPERT, D_MODEL), D_FF_EXPERT ** -0.5),
        'final_norm_g': 1.0 + nrm(ks[18], (D_MODEL,), 0.01),
    }

def reference(x, norm_mix_g, w_in, w_g2_f, b_g_f, w_g2_b, b_g_b, gla_norm_g, rpb, w_out,
              norm_ffn_g, w_grp, b_grp, w_exp, b_exp, w_gate, w_up, w_down, final_norm_g):
    for l in range(DEPTH):
        h = rmsnorm(x, norm_mix_g[l])
        x = x + hybrid_mixer(h, w_in[l], w_g2_f[l], b_g_f[l], w_g2_b[l], b_g_b[l], gla_norm_g[l], rpb[l], w_out[l])
        h = rmsnorm(x, norm_ffn_g[l])
        x = x + hierarchical_moe(h, w_grp[l], b_grp[l], w_exp[l], b_exp[l], w_gate[l], w_up[l], w_down[l])
    return rmsnorm(x, final_norm_g)


_drawn_inputs = setup_inputs


def setup_inputs(seed=0):
    import zlib

    import numpy as np

    out = dict(_drawn_inputs(seed))
    spreads = {}
    factors = {'norm_mix_g': 2.865,
     'b_g_f': 2.755,
     'gla_norm_g': 6.659,
     'rpb': 8.0,
     'norm_ffn_g': 3.817,
     'b_grp': 5.223,
     'b_exp': 5.499,
     'final_norm_g': 5.814}
    for name, (base, spread) in spreads.items():
        noise = np.random.default_rng([zlib.crc32(name.encode()), seed]).standard_normal(out[name].shape)
        drawn = base * np.exp(spread * noise) if base else spread * noise
        out[name] = __import__('jax').numpy.asarray(drawn.astype(out[name].dtype))
    for name, factor in factors.items():
        out[name] = (out[name] * factor).astype(out[name].dtype)
    return out
```

```python
from contextlib import ExitStack

import concourse.bass as bass
from concourse import mybir

ALU = mybir.AluOpType
ACT = mybir.ActivationFunctionType
AX = mybir.AxisListType
F32 = mybir.dt.float32
U32 = mybir.dt.uint32
I32 = mybir.dt.int32

P = 128
D = 1024
T = 512
TT = T // P
KC = D // P
GRID_W = 64
ROWS = T // GRID_W
WIN_W = 16
NA_HEADS, NA_DIM = 8, 64
PAIRS = NA_HEADS // 2
BLK_W = P // ROWS
BLOCKS = GRID_W // BLK_W
KEY_W = 2 * BLK_W
NKEY = KEY_W * ROWS
KEY_START = [min(max(b * BLK_W - WIN_W // 2, 0), GRID_W - KEY_W) for b in range(BLOCKS)]
BIAS_VAR = [0, 1, 1, 2]
RPB_H, RPB_W = 2 * ROWS - 1, 2 * WIN_W - 1
RPB_RUN = RPB_W * (ROWS - 1) + KEY_W + WIN_W
RPB_PAD = WIN_W
GLA_HEADS, DK, DV = 4, 64, 128
CHUNK = 64
NCH = T // CHUNK
HP = GLA_HEADS // 2
RANK = 16
GROUPS, PER_GROUP = 4, 8
EXPERTS = GROUPS * PER_GROUP
FF = 512
FC = FF // P
SLOTS = 64
DUMP = EXPERTS * SLOTS
HROWS = DUMP + P
RING = 3
EPS = 1e-6
NEG = -1e30
LOWEST = -3e38
UNIT_BANKS = 2

IN_NQ, IN_NK, IN_NV, IN_GQK, IN_GV, IN_GR, IN_LR = 0, 512, 1024, 1536, 2048, 2560, 3072


def words(kib):
    return int(kib * 256)


def mixer_and_moe(nc, x, rpb, w_in, w_g2, b_g, gla_g, g_mix, w_out, g_ffn, w_r, b_r, w_gate, w_up, w_down, g_fin,
                  c_small, c_mask, c_scan, out, limit=SLOTS):
    with ExitStack() as ctx:
        arena = ctx.enter_context(nc.sbuf_tensor("arena", [P, words(207.75)], F32))
        pbank = [ctx.enter_context(nc.psum_tensor(f"bank{i}", [P, 512], F32)) for i in range(8)]
        rows_in = nc.dram_tensor("rows_in", [HROWS, D], F32).ap()
        rows_out = nc.dram_tensor("rows_out", [HROWS, D], F32).ap()

        def sem(name):
            return ctx.enter_context(nc.semaphore(name))

        def at(kib, *shape):
            n = 1
            for s in shape:
                n *= s
            v = arena[:, words(kib):words(kib) + n]
            if len(shape) == 2:
                return v.rearrange("p (a b) -> p a b", b=shape[1])
            if len(shape) == 3:
                return v.rearrange("p (a b c) -> p a b c", b=shape[1], c=shape[2])
            return v

        hT = at(0, KC, T)
        w_buf = [at(16, KC, 512), at(32, KC, 512)]
        bias = at(48, NA_HEADS, 3, NKEY)
        na_v = at(72, 2 * BLOCKS - 1, 512)
        gz = at(78, 4, T)
        r_exp = at(78, TT, 512)
        gd = at(86, 4, T)
        na_q = at(86, PAIRS, T)
        gE = at(94, 4, T)
        na_k = at(94, PAIRS, T)
        xs = at(102, TT, D)
        gb = at(102, 4, T)
        k_rows = at(102, 4, TT, P)
        q_rel = at(110, 4, T)
        rpb_run = at(118, NA_HEADS, RPB_RUN)
        k_rel = at(118, 4, T)
        o_junk = at(118, 16, DV)
        vT = at(110, PAIRS, T)
        k_dec = at(126, 4, T)
        o_rows = at(126, TT, 512)
        w_o = at(102, KC, D)
        q_exp = at(134, 4, T)
        scan_keep = at(140, T)
        probs = [at(134 + 2 * i, 2, NKEY) for i in range(4)]
        hT2 = [at(134 + 4 * i, KC, P) for i in range(2)]
        lr = at(142, T)
        probsT = [at(142, 4, P), at(195, 4, P)]
        x1 = at(144, TT, D)
        zeros = at(163, 512)
        s_prev = at(163, 4, NCH, DV)
        yT = at(163, KC, T)
        gv = at(179, TT, 512)
        rg = at(187, TT, 512)
        junk = at(179, TT, D)
        h2 = at(179, TT, D)
        gq = at(195, HP, T)
        gk = at(199, HP, T)
        st = at(195, 16, P)
        mask = at(203, 3, NKEY)
        w_lr = at(206, KC, 2 * RANK)
        gla_gb = at(207, DV)
        g2b = at(195, D)
        gfb = at(175, D)
        wr_sb = at(203, KC, GROUPS + EXPERTS)

        small = at(160, 768)
        pos = [0]

        def take(n):
            v = small[:, pos[0]:pos[0] + n]
            pos[0] += n
            return v

        ident, upper, causal, iota = take(128), take(128), take(64), take(32)
        dump_row, gmix, bg = take(1), take(8), take(4)
        b_r_sb = take(GROUPS + EXPERTS)
        ssq, root, rstd = take(TT), take(TT), take(TT)
        dec = take(4 * NCH).rearrange("p (m n) -> p m n", m=4)
        oss, oroot, orstd = (take(16).rearrange("p (t h) -> p t h", t=TT) for _ in range(3))
        nmax, psum_, rsum = (take(32).rearrange("p (u h) -> p u h", h=2) for _ in range(3))
        ssq2, root2, rstd2 = take(TT), take(TT), take(TT)
        ssq3, root3, rstd3 = take(TT), take(TT), take(TT)
        comb = take(2 * TT).rearrange("p (t k) -> p t k", k=2)
        slot = take(2 * TT).rearrange("p (t k) -> p t k", k=2).bitcast(U32)
        most = take(1).bitcast(I32)
        assert pos[0] <= 768

        rt = at(204.25, 890)
        rpos = [0]

        def rtake(*shape):
            n = 1
            for s in shape:
                n *= s
            v = rt[:, rpos[0]:rpos[0] + n]
            rpos[0] += n
            if len(shape) == 2:
                v = v.rearrange("p (a b) -> p a b", b=shape[1])
            return v

        lg = rtake(TT, 8 + EXPERTS)
        gtop, itop8, ing = rtake(TT, 8), rtake(TT, 8).bitcast(U32), rtake(TT, 8)
        gidx, ghot, gexp = rtake(TT, 1), rtake(TT, GROUPS), rtake(TT, GROUPS)
        etop, eidx = rtake(TT, 8), rtake(TT, 8).bitcast(U32)
        gsum, ediff, eexp, eden = rtake(TT, 1), rtake(TT, 1), rtake(TT, 1), rtake(TT, 1)
        eid = rtake(TT, 2)
        hot = [rtake(TT, EXPERTS), rtake(TT, EXPERTS)]
        both = rtake(TT, EXPERTS)
        rank, fits, slotf = rtake(TT, 2), rtake(TT, 2), rtake(TT, 2)
        ones = at(202, P)
        prod = at(199, TT, EXPERTS)

        x_in = [at(179 + 4 * i, D) for i in range(RING)]
        xT = [at(191 + 2 * i, KC, SLOTS) for i in range(RING)]
        sil = [at(197 + i, 256) for i in range(RING)]
        hid = [at(200 + i, 256) for i in range(RING)]
        hidT = [at(163 + 2 * i, 2, 2, SLOTS) for i in range(RING)]
        y_sb = [at(169 + 2 * i, 512) for i in range(RING)]
        wg_sb = [at(48 * i, 2, KC, FF) for i in range(RING)]
        wd_sb = [at(48 * i + 32, FC, D) for i in range(RING)]
        got = [[at(4 * (2 * t + k), D) for k in range(2)] for t in range(TT)]
        res = at(32, TT, D)
        x2 = at(96, TT, D)
        junk3 = at(112, TT, D)

        g_rows = at(48, TT, D)
        g_hT = [at(64 + 4 * t, KC, P) for t in range(TT)]
        g_sil = at(128, FF)
        g_hid = at(130, FF)
        g_hidT = at(132, FC, P)
        g_cw = at(134, TT, EXPERTS)
        g_col = at(135, TT, 1)
        g_gain = at(138, D)

        x_in_sb = [sem(f"x_in_sb{t}") for t in range(TT)]
        late_in = sem("late_in")
        consts_in, scan_in, mask_in, rpb_in = sem("consts_in"), sem("scan_in"), sem("mask_in"), sem("rpb_in")
        win_in = [sem(f"win_in{g}") for g in range(7)]
        zeroed, zero_ready = sem("zeroed"), sem("zero_ready")
        sumsq_done, ms_done, root_done, rstd_done = sem("sumsq_done"), sem("ms_done"), sem("root_done"), sem("rstd_done")
        xs_vec, xs_pool = sem("xs_vec"), sem("xs_pool")
        xT_done, hT_act, hT_vec = sem("xT_done"), sem("hT_act"), sem("hT_vec")
        unit_done, unit_evicted = sem("unit_done"), sem("unit_evicted")
        gates_done, z_done, abs_done, expa_done = sem("gates_done"), sem("z_done"), sem("abs_done"), sem("expa_done")
        softp_done, g_done, scan_done, d1_done = sem("softp_done"), sem("g_done"), sem("scan_done"), sem("d1_done")
        e12_done, q_rel_done, k_rel_done, d3_done = sem("e12_done"), sem("q_rel_done"), sem("k_rel_done"), sem("d3_done")
        e3_done, dec_done, e4_done = sem("e3_done"), sem("dec_done"), sem("e4_done")
        k_dec_done, q_exp_done = sem("k_dec_done"), sem("q_exp_done")
        r_step, rg_done, bias_done = sem("r_step"), sem("rg_done"), sem("bias_done")
        kT_done, k_rows_done, scores_done = sem("kT_done"), sem("k_rows_done"), sem("scores_done")
        st_zero, sb_copied, st_done = sem("st_zero"), sem("sb_copied"), sem("st_done")
        state_done, state_used = sem("state_done"), sem("state_used")
        o_done, oss_done, oms_done, oroot_done = sem("o_done"), sem("oss_done"), sem("oms_done"), sem("oroot_done")
        orstd_done, y_done, yg_done, yg_evicted = sem("orstd_done"), sem("y_done"), sem("yg_done"), sem("yg_evicted")
        v_done, v_evicted = sem("v_done"), sem("v_evicted")
        s_done, s_added, nmax_done = sem("s_done"), sem("s_added"), sem("nmax_done")
        exp_done, rsum_done, p_done = sem("exp_done"), sem("rsum_done"), sem("p_done")
        pT_done, pT_evicted, pv_done, yn_evicted = sem("pT_done"), sem("pT_evicted"), sem("pv_done"), sem("yn_evicted")
        wout_in, g2_in, gf_in = sem("wout_in"), sem("g2_in"), sem("gf_in")
        wo_done, x1_done, sumsq2_done, ms2_done = sem("wo_done"), sem("x1_done"), sem("sumsq2_done"), sem("ms2_done")
        root2_done, rstd2_done, h2_done = sem("root2_done"), sem("rstd2_done"), sem("h2_done")
        h2T_done, h2T_act, h2T_vec, lg_done = sem("h2T_done"), sem("h2T_act"), sem("h2T_vec"), sem("lg_done")
        route_step, gdiff_done, gexp_done, ediff_done = sem("route_step"), sem("gdiff_done"), sem("gexp_done"), sem("ediff_done")
        eexp_done, both_done, rank_mm_done, slots_done = sem("eexp_done"), sem("both_done"), sem("rank_mm_done"), sem("slots_done")
        most_done, scattered = sem("most_done"), sem("scattered")
        wgu_in = [sem(f"wgu_in{i}") for i in range(RING)]
        wd_in = [sem(f"wd_in{i}") for i in range(RING)]
        rows_in_sb = [sem(f"rows_in_sb{i}") for i in range(RING)]
        y_stored = [sem(f"y_stored{i}") for i in range(RING)]
        xt_done, xt_evicted, gu_done, sil_done = sem("xt_done"), sem("xt_evicted"), sem("gu_done"), sem("sil_done")
        hid_done, ht_done, ht_evicted, d_done, y_evicted = (sem("hid_done"), sem("ht_done"), sem("ht_evicted"),
                                                            sem("d_done"), sem("y_evicted"))
        gathered = [sem(f"gathered{t}") for t in range(TT)]
        x2_half, x2_done, sumsq3_done, ms3_done = sem("x2_half"), sem("x2_done"), sem("sumsq3_done"), sem("ms3_done")
        root3_done, rstd3_done, res_done, out_stored = sem("root3_done"), sem("rstd3_done"), sem("res_done"), sem("out_stored")
        a_g2, a_col = sem("a_g2"), sem("a_col")
        a_h2, a_T, a_hT, a_w, a_gu, a_sil, a_hid, a_ht, a_hte, a_d, a_acc, a_cw = (
            sem("a_h2"), sem("a_T"), sem("a_hT"), sem("a_w"), sem("a_gu"), sem("a_sil"), sem("a_hid"), sem("a_ht"),
            sem("a_hte"), sem("a_d"), sem("a_acc"), sem("a_cw"))

        x_d = x.rearrange("b (t p) d -> (b t) p d", p=P)
        out_d = out.rearrange("b (t p) d -> (b t) p d", p=P)
        win_d = w_in.rearrange("l (k p) n -> (l p) k n", p=P)
        wout_d = w_out.rearrange("l (k p) n -> (l p) k n", p=P)
        wg_d = w_gate.rearrange("l e (p k) f -> (l e) p k f", k=KC)
        wu_d = w_up.rearrange("l e (p k) f -> (l e) p k f", k=KC)
        wd_d = w_down.rearrange("l e (k p) d -> (l e) p k d", p=P)
        rows_out_d = rows_out[0:DUMP].rearrange("(e t) (h d) -> e h t d", t=SLOTS, h=2)
        rows_in_d = rows_in[0:DUMP].rearrange("(e t) d -> e t d", t=SLOTS)

        block = ctx.enter_context(nc.Block())

        groups = [("lr", None, IN_LR), ("gqk", 0, IN_GQK), ("gv", 1, IN_GV), ("gr", 0, IN_GR),
                  ("nq", 1, IN_NQ), ("nk", 0, IN_NK), ("nv", 1, IN_NV)]

        @block.sync
        def _(sp):
            for t in range(TT):
                sp.dma_start(x1[:, t], x_d[t]).then_inc(x_in_sb[t], 16)
                if t == 0:
                    sp.dma_start(small[:, 0:353], c_small).then_inc(consts_in, 16)
            sp.dma_start(gmix, g_mix).then_inc(consts_in, 16)
            sp.dma_start(bg, b_g).then_inc(consts_in, 16)
            sp.dma_start(w_lr, win_d[:, :, IN_LR:IN_LR + 2 * RANK]).then_inc(win_in[0], 16)
            sp.dma_start(gE[0:2 * RANK, 0, :], w_g2).then_inc(consts_in, 16)
            for g in (1, 2):
                sp.dma_start(w_buf[groups[g][1]], win_d[:, :, groups[g][2]:groups[g][2] + 512]).then_inc(win_in[g], 16)
            for h in range(NA_HEADS):
                run = bass.AP(rpb.tensor, h * RPB_H * RPB_W, [[1, BLK_W], [RPB_W, ROWS], [1, RPB_RUN]])
                sp.dma_start(rpb_run[:, h], run).then_inc(rpb_in, 16)
            sp.dma_start(mask.rearrange("p a b -> p (a b)"), c_mask).then_inc(mask_in, 16)
            sp.dma_start(scan_keep, c_scan).then_inc(scan_in, 16)
            sp.dma_start(gla_gb, gla_g.broadcast_to((P, DV))).then_inc(late_in, 16)
            sp.dma_start(b_r_sb, b_r.broadcast_to((P, GROUPS + EXPERTS))).then_inc(late_in, 16)
            sp.wait_ge(zero_ready, 1)
            per = HROWS // P
            zsrc = zeros.unsqueeze(1).broadcast_to((P, per * 2, 512))
            sp.dma_start(rows_in.rearrange("(p r) (h d) -> p (r h) d", p=P, h=2), zsrc).then_inc(zeroed, 16)
            sp.dma_start(rows_out[DUMP:HROWS].rearrange("p (h d) -> p h d", h=2),
                         zeros.unsqueeze(1).broadcast_to((P, 2, 512))).then_inc(zeroed, 16)
            for g in range(3, 7):
                sp.wait_ge(unit_done, 1 + 4 * (g - 2))
                sp.dma_start(w_buf[groups[g][1]], win_d[:, :, groups[g][2]:groups[g][2] + 512]).then_inc(win_in[g], 16)
            sp.wait_ge(yg_done, GLA_HEADS)
            sp.dma_start(w_o, wout_d).then_inc(wout_in, 16)
            def load_gu(e, s):
                sp.dma_start(wg_sb[s][:, 0], wg_d[e]).then_inc(wgu_in[s], 16)
                sp.dma_start(wg_sb[s][:, 1], wu_d[e]).then_inc(wgu_in[s], 16)

            def load_d(e, s):
                sp.dma_start(wd_sb[s], wd_d[e]).then_inc(wd_in[s], 16)

            sp.wait_ge(unit_done, 25)
            load_gu(0, 0)
            load_d(0, 0)
            sp.wait_ge(pv_done, 4 * PAIRS)
            load_gu(1, 1)
            load_d(1, 1)
            sp.dma_start(g2b, g_ffn.broadcast_to((P, D))).then_inc(g2_in, 16)
            sp.dma_start(wr_sb, w_r).then_inc(g2_in, 16)
            sp.wait_ge(wo_done, TT)
            load_gu(2, 2)
            sp.wait_ge(lg_done, TT)
            load_d(2, 2)
            sp.dma_start(gfb, g_fin.broadcast_to((P, D))).then_inc(gf_in, 16)

            def step(e, c, s):
                sp.wait_ge(gu_done, c - 2)
                load_gu(e, s)
                sp.wait_ge(d_done, c - 2)
                load_d(e, s)

            with sp.Fori(1, EXPERTS // RING) as i:
                for j in range(RING):
                    step(RING * i + j, RING * i + j, j)
            for e in range(EXPERTS // RING * RING, EXPERTS):
                step(e, e, e % RING)

            sp.wait_ge(most_done, 1)
            general = sp.value_load(most[0:1, 0:1], min_val=0, max_val=T)
            with sp.If(general > limit):
                sp.wait_ge(d_done, EXPERTS)
                sp.dma_start(g_gain, g_ffn.broadcast_to((P, D))).then_inc(a_g2, 16)
                with sp.Fori(0, EXPERTS) as e:
                    sp.wait_ge(a_acc, TT * 2 * e + 1)
                    sp.dma_start(wg_sb[0][:, 0], wg_d[e]).then_inc(a_w, 16)
                    sp.dma_start(wg_sb[0][:, 1], wu_d[e]).then_inc(a_w, 16)
                    sp.dma_start(wd_sb[0], wd_d[e]).then_inc(a_w, 16)

            for t in range(TT):
                sp.wait_ge(res_done, t + 1)
                sp.dma_start(out_d[t], res[:, t]).then_inc(out_stored, 16)
            sp.wait_ge(out_stored, 16 * TT)

        @block.tensor
        def _(pe):
            pe.wait_ge(consts_in, 16 * 4)
            for t in range(TT):
                if t < 2:
                    pe.wait_ge(xs_vec, t + 1)
                else:
                    pe.wait_ge(xs_pool, t - 1)
                for k in range(KC):
                    m = pe.transpose(pbank[k][:, t * P:(t + 1) * P], xs[:, t, k * P:(k + 1) * P], ident)
                    if t == TT - 1:
                        m.then_inc(xT_done, 1)
            pe.wait_ge(hT_act, KC // 2)
            pe.wait_ge(hT_vec, KC // 2)
            count = [0]

            def unit(m_cols, lhs, rhs):
                n = count[0]
                if n >= UNIT_BANKS:
                    pe.wait_ge(unit_evicted, n - UNIT_BANKS + 1)
                for k in range(KC):
                    m = pe.matmul(pbank[n % UNIT_BANKS][0:m_cols], lhs(k), rhs(k), start=(k == 0), stop=(k == KC - 1))
                m.then_inc(unit_done, 1)
                count[0] += 1

            def weights_stationary(g, m):
                w = w_buf[groups[g][1]]
                unit(P, lambda k: w[:, k, m * P:(m + 1) * P], lambda k: hT[:, k])

            def tokens_stationary(g, t):
                w = w_buf[groups[g][1]]
                unit(P, lambda k: hT[:, k, t * P:(t + 1) * P], lambda k: w[:, k])

            pe.wait_ge(win_in[0], 16)
            unit(2 * RANK, lambda k: w_lr[:, k], lambda k: hT[:, k])
            pe.wait_ge(win_in[1], 16)
            weights_stationary(1, 0)
            pe.wait_ge(unit_evicted, 1)
            for m in range(4):
                pe.matmul(pbank[2 + m][:], gE[0:2 * RANK, 0, m * P:(m + 1) * P], lr[0:2 * RANK],
                          start=True, stop=True).then_inc(gates_done, 1)
            for m in range(1, 4):
                weights_stationary(1, m)
            for g in (2, 3):
                pe.wait_ge(win_in[g], 16)
                for t in range(TT):
                    tokens_stationary(g, t)

            pe.wait_ge(k_dec_done, 1)
            for m in range(4):
                if m >= 2:
                    pe.wait_ge(k_rows_done, m - 1)
                for t in range(TT):
                    mm = pe.transpose(pbank[6 + m % 2][:, t * P:(t + 1) * P], k_dec[:, m, t * P:(t + 1) * P], ident)
                mm.then_inc(kT_done, 1)
            pe.wait_ge(q_rel_done, 1)
            pe.wait_ge(k_rel_done, 1)
            for d in range(2):
                for n in range(NCH):
                    for hp in range(HP):
                        for par in range(2):
                            rows = slice(64 * par, 64 * par + 64)
                            c = (hp * (NCH // 2) + n // 2) * CHUNK
                            mm = pe.matmul(pbank[2 + 2 * d + par][64 * (n % 2):64 * (n % 2) + 64, c:c + CHUNK],
                                           k_rel[rows, 2 * d + hp, n * CHUNK:(n + 1) * CHUNK],
                                           q_rel[rows, 2 * d + hp, n * CHUNK:(n + 1) * CHUNK], start=True, stop=True)
                mm.then_inc(scores_done, 1)

            pe.wait_ge(win_in[4], 16)
            for s2 in range(4):
                weights_stationary(4, s2)
                if s2 == 0:
                    pe.wait_ge(k_rows_done, 4)
                else:
                    pe.wait_ge(state_used, 8 * s2)
                for s in (2 * s2, 2 * s2 + 1):
                    if s == NCH - 1:
                        continue
                    for d in range(2):
                        n = s if d == 0 else NCH - 1 - s
                        rows = slice(64 * (n % 2), 64 * (n % 2) + 64)
                        for hp in range(HP):
                            for par in range(2):
                                h = 2 * hp + par
                                mm = pe.matmul(
                                    pbank[6 + n % 2][64 * par:64 * par + 64, d * 256 + hp * DV:d * 256 + (hp + 1) * DV],
                                    k_rows[rows, 2 * d + hp, n // 2, par * DK:(par + 1) * DK],
                                    gv[rows, n // 2, h * DV:(h + 1) * DV], start=True, stop=True)
                    mm.then_inc(state_done, 1)
            pe.wait_ge(win_in[5], 16)
            for m in range(4):
                weights_stationary(5, m)
            pe.wait_ge(st_done, 4)
            pe.wait_ge(state_used, 28)
            pe.wait_ge(q_exp_done, 1)
            for t in range(TT):
                for hp in range(HP):
                    for par in range(2):
                        h = 2 * hp + par
                        rows = slice(64 * par, 64 * par + 64)
                        c0 = (t % 2) * 256 + hp * DV
                        bank = pbank[2 + 2 * par + t // 2]
                        pe.matmul(bank[:, c0:c0 + DV], st[:, par * 8 + hp * 4 + t], gv[:, t, h * DV:(h + 1) * DV],
                                  start=True, stop=False)
                        for c in range(2):
                            n = 2 * t + c
                            dirs = [d for d in range(2) if not (d == 0 and n == 0) and not (d == 1 and n == NCH - 1)]
                            for d in dirs:
                                mm = pe.matmul(bank[64 * c:64 * c + 64, c0:c0 + DV],
                                               q_exp[rows, 2 * d + hp, n * CHUNK:(n + 1) * CHUNK],
                                               s_prev[rows, 2 * d + hp, n], start=False, stop=(d == dirs[-1]))
                mm.then_inc(o_done, 1)
            pe.wait_ge(win_in[6], 16)
            for m in range(4):
                weights_stationary(6, m)
            pe.wait_ge(unit_evicted, 25)
            for i in range(2 * BLOCKS - 1):
                if i >= 2:
                    pe.wait_ge(v_evicted, i - 1)
                for m in range(PAIRS):
                    mm = pe.transpose(pbank[6 + i % 2][:, m * P:(m + 1) * P], vT[:, m, i * 64:i * 64 + P], ident)
                mm.then_inc(v_done, 1)
            pe.wait_ge(v_evicted, 2 * BLOCKS - 1)
            pe.wait_ge(y_done, 16)
            for h in range(GLA_HEADS):
                if h >= 2:
                    pe.wait_ge(yg_evicted, h - 1)
                for t in range(TT):
                    mm = pe.transpose(pbank[6 + h % 2][:, t * P:(t + 1) * P], o_rows[:, t, h * DV:(h + 1) * DV], ident)
                mm.then_inc(yg_done, 1)

            NU = PAIRS * BLOCKS
            for i in range(NU + 3):
                if i < NU:
                    pair, b = divmod(i, BLOCKS)
                    if i >= 2:
                        pe.wait_ge(s_added, 2 * (i - 1))
                    for par in range(2):
                        rows = slice(64 * par, 64 * par + 64)
                        k0 = KEY_START[b] * ROWS
                        mm = pe.matmul(pbank[2 * (i % 2) + par][:, 0:NKEY], na_q[rows, pair, b * P:(b + 1) * P],
                                       na_k[rows, pair, k0:k0 + NKEY], start=True, stop=True)
                    mm.then_inc(s_done, 1)
                if 0 <= i - 2 < NU:
                    u = i - 2
                    pe.wait_ge(p_done, 2 * (u + 1))
                    if u >= 2:
                        pe.wait_ge(pT_evicted, u - 1)
                    for par in range(2):
                        for c in range(2):
                            a = 2 * par + c
                            mm = pe.transpose(pbank[4 + u % 2][:, a * P:(a + 1) * P],
                                              probs[u % 4][:, par, c * P:(c + 1) * P], ident)
                    mm.then_inc(pT_done, 1)
                if i >= 3:
                    u = i - 3
                    pair, b = divmod(u, BLOCKS)
                    pe.wait_ge(pT_evicted, u + 1)
                    if u == 0:
                        pe.wait_ge(yg_evicted, GLA_HEADS)
                    if b == 0 and pair >= 2:
                        pe.wait_ge(yn_evicted, pair - 1)
                    v0 = KEY_START[b] * ROWS // 64
                    for par in range(2):
                        h = 2 * pair + par
                        for c in range(2):
                            mm = pe.matmul(pbank[6 + pair % 2][64 * par:64 * par + 64, b * P:(b + 1) * P],
                                           na_v[:, v0 + 2 * c, h * NA_DIM:(h + 1) * NA_DIM],
                                           probsT[u % 2][:, 2 * par + c], start=(c == 0), stop=(c == 1))
                    mm.then_inc(pv_done, 1)

            def out_proj(t):
                if t >= 2:
                    pe.wait_ge(x1_done, 2 * (t - 1))
                for half in range(2):
                    for k in range(KC):
                        mm = pe.matmul(pbank[2 * (t % 2) + half][:], yT[:, k, t * P:(t + 1) * P],
                                       w_o[:, k, half * 512:(half + 1) * 512], start=(k == 0), stop=(k == KC - 1))
                mm.then_inc(wo_done, 1)

            def router(t):
                pe.wait_ge(h2_done, t + 1)
                if t >= 1:
                    pe.wait_ge(h2T_act, t)
                    pe.wait_ge(h2T_vec, t)
                for k in range(KC):
                    mm = pe.transpose(pbank[4 + k // 4][:, (k % 4) * P:(k % 4 + 1) * P], h2[:, t, k * P:(k + 1) * P],
                                      ident)
                mm.then_inc(h2T_done, 1)
                pe.wait_ge(h2T_act, t + 1)
                pe.wait_ge(h2T_vec, t + 1)
                for k in range(KC):
                    mm = pe.matmul(pbank[6][:, t * 64:t * 64 + GROUPS + EXPERTS], hT2[t % 2][:, k], wr_sb[:, k],
                                   start=(k == 0), stop=(k == KC - 1))
                mm.then_inc(lg_done, 1)

            pe.wait_ge(yn_evicted, PAIRS)
            pe.wait_ge(wout_in, 16)
            pe.wait_ge(g2_in, 32)
            out_proj(0)
            out_proj(1)
            router(0)
            out_proj(2)
            router(1)
            out_proj(3)
            router(2)
            router(3)
            pe.wait_ge(both_done, 1)
            for t in range(TT + 1):
                for s in range(min(t + 1, TT)):
                    mm = pe.matmul(pbank[7][:, t * EXPERTS:(t + 1) * EXPERTS], upper if s == t else ones, both[:, s],
                                   start=(s == 0), stop=(s == min(t, TT - 1)))
            mm.then_inc(rank_mm_done, 1)

            def rows_T(s, q):
                pe.wait_ge(rows_in_sb[s], 16 * q + 16)
                pe.nop(nofuse=True)
                for k in range(KC):
                    mm = pe.transpose(pbank[3][:, k * SLOTS:(k + 1) * SLOTS], x_in[s][0:SLOTS, k::KC], ident[0:SLOTS, 0:SLOTS])
                mm.then_inc(xt_done, 1)

            def gate_up(s, q, c):
                pe.wait_ge(xt_evicted, c + 1)
                pe.wait_ge(wgu_in[s], 32 * q + 32)
                for k in range(KC):
                    for half in range(2):
                        mm = pe.matmul(pbank[s][64 * half:64 * half + 64, :].rearrange("p (g f) -> p g f", g=2),
                                       xT[s][:, k], wg_sb[s][:, :, k, half * 256:(half + 1) * 256],
                                       start=(k == 0), stop=(k == KC - 1))
                mm.then_inc(gu_done, 1)

            def hidden_T(s, c):
                pe.wait_ge(hid_done, c + 1)
                pe.nop(nofuse=True)
                for cc in range(2):
                    mm = pe.transpose(pbank[4][:, cc * P:(cc + 1) * P], hid[s][:, cc * P:(cc + 1) * P], ident)
                mm.then_inc(ht_done, 1)

            def down(s, q, c):
                pe.wait_ge(ht_evicted, c + 1)
                pe.wait_ge(wd_in[s], 16 * q + 16)
                for kc in range(FC):
                    for half in range(2):
                        mm = pe.matmul(pbank[5 + s][64 * half:64 * half + 64, :], hidT[s][:, kc % 2, kc // 2],
                                       wd_sb[s][:, kc, half * 512:(half + 1) * 512],
                                       start=(kc == 0), stop=(kc == FC - 1))
                mm.then_inc(d_done, 1)

            rows_T(0, 0)
            gate_up(0, 0, 0)
            rows_T(1, 0)
            with pe.Fori(0, (EXPERTS - 2) // RING) as i:
                for j in range(RING):
                    e = RING * i + 1 + j
                    gate_up((1 + j) % RING, i + (1 + j) // RING, e)
                    hidden_T(j, e - 1)
                    rows_T((2 + j) % RING, i + (2 + j) // RING)
                    down(j, i, e - 1)
            last = EXPERTS - 1
            gate_up(last % RING, last // RING, last)
            hidden_T((last - 1) % RING, last - 1)
            down((last - 1) % RING, (last - 1) // RING, last - 1)
            hidden_T(last % RING, last)
            down(last % RING, last // RING, last)

            pe.wait_ge(most_done, 1)
            general = pe.value_load(most[0:1, 0:1], min_val=0, max_val=T)
            with pe.If(general > limit):
                for t in range(TT):
                    pe.wait_ge(a_h2, t + 1)
                    for g in range(2):
                        if 2 * t + g >= 1:
                            pe.wait_ge(a_hT, 2 * t + g)
                        for k in range(4):
                            mm = pe.transpose(pbank[0][:, k * P:(k + 1) * P],
                                              g_rows[:, t, (4 * g + k)::KC], ident)
                        mm.then_inc(a_T, 1)
                pe.wait_ge(a_hT, 2 * TT)
                with pe.Fori(0, EXPERTS) as e:
                    pe.wait_ge(a_w, 48 * e + 48)
                    for t in range(TT):
                        c = TT * e + t
                        for g in range(2):
                            for k in range(KC):
                                mm = pe.matmul(pbank[1 + g][:], g_hT[t][:, k], wg_sb[0][:, g, k],
                                               start=(k == 0), stop=(k == KC - 1))
                        mm.then_inc(a_gu, 1)
                        pe.wait_ge(a_hid, c + 1)
                        pe.nop(nofuse=True)
                        for k in range(FC):
                            mm = pe.transpose(pbank[3][:, k * P:(k + 1) * P], g_hid[:, k * P:(k + 1) * P], ident)
                        mm.then_inc(a_ht, 1)
                        pe.wait_ge(a_hte, c + 1)
                        for half in range(2):
                            for k in range(FC):
                                mm = pe.matmul(pbank[4 + half][:], g_hidT[:, k], wd_sb[0][:, k, half * 512:(half + 1) * 512],
                                               start=(k == 0), stop=(k == FC - 1))
                        mm.then_inc(a_d, 1)
                        pe.wait_ge(a_acc, 2 * c + 3)

        @block.scalar
        def _(act):
            def scaled_copy(dst, src, scale):
                return nc.scalar.activation(dst, src, ACT.Identity, scale=scale)

            for t in range(TT):
                act.wait_ge(x_in_sb[t], 16)
                nc.scalar.activation(junk[:, t], x1[:, t], ACT.Square, accum_out=ssq[:, t:t + 1]).then_inc(sumsq_done, 1)
            act.wait_ge(ms_done, 1)
            nc.scalar.activation(root, ssq, ACT.Sqrt).then_inc(root_done, 1)
            act.wait_ge(consts_in, 64)
            for k in range(1, KC, 2):
                act.wait_ge(xT_done, k + 1)
                scaled_copy(hT[:, k], pbank[k][:], gmix[:, k:k + 1]).then_inc(hT_act, 1)

            def gla_q_evict(n, m):
                act.wait_ge(unit_done, n + 1)
                dst = gq[:, m] if m < HP else gk[:, m - HP]
                scaled_copy(dst, pbank[n % 2][:], DK ** -0.5 if m < HP else 1.0).then_inc(unit_evicted, 1)

            def gv_evict(n, t):
                act.wait_ge(unit_done, n + 1)
                nc.scalar.copy(gv[:, t], pbank[n % 2][:]).then_inc(unit_evicted, 1)

            act.wait_ge(sumsq_done, TT)
            act.wait_ge(unit_done, 1)
            nc.scalar.copy(lr[0:2 * RANK], pbank[0][0:2 * RANK]).then_inc(unit_evicted, 1)
            gla_q_evict(1, 0)
            for m in range(4):
                act.wait_ge(gates_done, m + 1)
                nc.scalar.activation(gz[:, m], pbank[2 + m][:], ACT.Identity, bias=bg[:, m:m + 1]).then_inc(z_done, 1)
            for m in range(1, 4):
                gla_q_evict(1 + m, m)
            act.wait_ge(z_done, 4)
            nc.scalar.activation(gd, gz, ACT.Abs).then_inc(abs_done, 1)
            act.wait_ge(abs_done, 1)
            nc.scalar.activation(gE, gd, ACT.Exp, scale=-1.0).then_inc(expa_done, 1)
            act.wait_ge(expa_done, 1)
            nc.scalar.activation(gd, gE, ACT.Ln, bias=1.0).then_inc(softp_done, 1)
            gv_evict(5, 0)
            act.wait_ge(d1_done, 2)
            nc.scalar.activation(gE, gd, ACT.Exp, scale=1.0 / 16).then_inc(e12_done, 1)
            nc.scalar.activation(gz, gd, ACT.Exp, scale=-1.0 / 16).then_inc(e12_done, 1)
            gv_evict(6, 1)
            act.wait_ge(d3_done, 2)
            act.wait_ge(q_rel_done, 1)
            nc.scalar.activation(gE, gd, ACT.Exp, scale=1.0 / 16).then_inc(e3_done, 1)
            gbn = gb.rearrange("p m (n i) -> p m n i", i=CHUNK)
            nc.scalar.activation(dec[:, 0:2], gbn[:, 0:2, :, CHUNK - 1], ACT.Exp, scale=1.0 / 16).then_inc(dec_done, 1)
            nc.scalar.activation(dec[:, 2:4], gbn[:, 2:4, :, 0], ACT.Exp, scale=1.0 / 16).then_inc(dec_done, 1)
            act.wait_ge(k_rel_done, 1)
            nc.scalar.activation(gz, gb, ACT.Exp, scale=1.0 / 16).then_inc(e4_done, 1)
            gv_evict(7, 2)
            gv_evict(8, 3)
            act.wait_ge(q_exp_done, 1)
            for t in range(TT):
                act.wait_ge(unit_done, 10 + t)
                nc.scalar.copy(rg[:, t], pbank[(9 + t) % 2][:])
                nc.scalar.activation(r_exp[:, t], pbank[(9 + t) % 2][:], ACT.Exp, scale=-1.0).then_inc(unit_evicted, 1)
            act.wait_ge(scores_done, 2)
            act.wait_ge(st_zero, 1)
            for par in range(2):
                for c in range(2):
                    nc.scalar.copy(st[64 * c:64 * c + 64, par * 8:par * 8 + 8, 64 * c:64 * c + 64],
                                   pbank[4 + par][64 * c:64 * c + 64, :].rearrange("p (a i) -> p a i", i=CHUNK)
                                   ).then_inc(sb_copied, 1)
            for m in range(4):
                act.wait_ge(unit_done, 14 + m)
                nc.scalar.activation(na_q[:, m].rearrange("p (w r) -> p w r", r=ROWS),
                                     pbank[(13 + m) % 2][:].rearrange("p (r w) -> p w r", w=GRID_W),
                                     ACT.Identity, scale=NA_DIM ** -0.5).then_inc(unit_evicted, 1)
            act.wait_ge(k_dec_done, 1)
            for m in range(4):
                act.wait_ge(unit_done, 18 + m)
                nc.scalar.copy(na_k[:, m].rearrange("p (w r) -> p w r", r=ROWS),
                               pbank[(17 + m) % 2][:].rearrange("p (r w) -> p w r", w=GRID_W)).then_inc(unit_evicted, 1)

            def o_slice(t, h):
                hp, par = divmod(h, 2)
                c0 = (t % 2) * 256 + hp * DV
                return pbank[2 + 2 * par + t // 2][:, c0:c0 + DV]

            for t in range(TT):
                act.wait_ge(o_done, t // 2 * 2 + 2)
                for h in range(GLA_HEADS):
                    nc.scalar.activation(o_junk[:, 4 * t + h], o_slice(t, h), ACT.Square,
                                         accum_out=oss[:, t, h:h + 1]).then_inc(oss_done, 1)
            act.wait_ge(oms_done, 1)
            nc.scalar.activation(oroot, oss, ACT.Sqrt).then_inc(oroot_done, 1)
            for m in range(4):
                act.wait_ge(unit_done, 22 + m)
                nc.scalar.copy(vT[:, m].rearrange("p (w r) -> p w r", r=ROWS),
                               pbank[(21 + m) % 2][:].rearrange("p (r w) -> p w r", w=GRID_W)).then_inc(unit_evicted, 1)
            act.wait_ge(rg_done, TT)
            for i in range(2 * BLOCKS - 1):
                act.wait_ge(v_done, i + 1)
                nc.scalar.copy(na_v[:, i], pbank[6 + i % 2][:]).then_inc(v_evicted, 1)
            for h in range(GLA_HEADS):
                act.wait_ge(yg_done, h + 1)
                nc.scalar.copy(yT[:, 4 + h], pbank[6 + h % 2][:]).then_inc(yg_evicted, 1)

            NU = PAIRS * BLOCKS
            for i in range(NU + 4):
                if i < NU:
                    act.wait_ge(nmax_done, i + 1)
                    for par in range(2):
                        nc.scalar.activation(probs[i % 4][:, par], probs[i % 4][:, par], ACT.Exp,
                                             bias=nmax[:, i, par:par + 1],
                                             accum_out=psum_[:, i, par:par + 1]).then_inc(exp_done, 1)
                if 0 <= i - 2 < NU:
                    u = i - 2
                    act.wait_ge(pT_done, u + 1)
                    if u >= 2:
                        act.wait_ge(pv_done, u - 1)
                    nc.scalar.copy(probsT[u % 2].rearrange("p a b -> p (a b)"), pbank[4 + u % 2][:]).then_inc(pT_evicted, 1)
                if i >= 3 and (i - 3) % BLOCKS == BLOCKS - 1:
                    pair = (i - 3) // BLOCKS
                    act.wait_ge(pv_done, i - 2)
                    nc.scalar.copy(yT[:, pair].rearrange("p (r w) -> p w r", w=GRID_W),
                                   pbank[6 + pair % 2][:].rearrange("p (w r) -> p w r", r=ROWS)).then_inc(yn_evicted, 1)

            for t in range(TT):
                act.wait_ge(x1_done, 2 * (t + 1))
                nc.scalar.activation(h2[:, t], x1[:, t], ACT.Square, accum_out=ssq2[:, t:t + 1]).then_inc(sumsq2_done, 1)
                act.wait_ge(ms2_done, t + 1)
                nc.scalar.activation(root2[:, t:t + 1], ssq2[:, t:t + 1], ACT.Sqrt).then_inc(root2_done, 1)
                act.wait_ge(h2T_done, t + 1)
                if t >= 2:
                    act.wait_ge(lg_done, t - 1)
                nc.scalar.copy(hT2[t % 2][:, 0:4].rearrange("p a b -> p (a b)"), pbank[4][:]).then_inc(h2T_act, 1)
            act.wait_ge(gdiff_done, 1)
            nc.scalar.activation(gexp, gexp, ACT.Exp).then_inc(gexp_done, 1)
            act.wait_ge(ediff_done, 1)
            nc.scalar.activation(eexp, ediff, ACT.Exp).then_inc(eexp_done, 1)

            def silu(s, c):
                act.wait_ge(gu_done, c + 1)
                nc.scalar.activation(sil[s], pbank[s][:, 0:256], ACT.Silu).then_inc(sil_done, 1)

            def hidden_T_evict(s, c):
                act.wait_ge(ht_done, c + 1)
                nc.scalar.copy(hidT[s].rearrange("p c h t -> p (c h t)"), pbank[4][:, 0:256]).then_inc(ht_evicted, 1)

            silu(0, 0)
            with act.Fori(0, (EXPERTS - 2) // RING) as i:
                for j in range(RING):
                    e = RING * i + 1 + j
                    silu((1 + j) % RING, e)
                    hidden_T_evict(j, e - 1)
            last = EXPERTS - 1
            silu(last % RING, last)
            hidden_T_evict((last - 1) % RING, last - 1)
            hidden_T_evict(last % RING, last)

            act.wait_ge(most_done, 1)
            general = act.value_load(most[0:1, 0:1], min_val=0, max_val=T)
            with act.If(general > limit):
                for c in range(2 * TT):
                    act.wait_ge(a_T, c + 1)
                    nc.scalar.copy(g_hT[c // 2][:, 4 * (c % 2):4 * (c % 2) + 4].rearrange("p a b -> p (a b)"),
                                   pbank[0][:]).then_inc(a_hT, 1)
                with act.Fori(0, EXPERTS) as e:
                    for t in range(TT):
                        c = TT * e + t
                        act.wait_ge(a_gu, c + 1)
                        nc.scalar.activation(g_sil, pbank[1][:], ACT.Silu).then_inc(a_sil, 1)
                        act.wait_ge(a_ht, c + 1)
                        nc.scalar.copy(g_hidT.rearrange("p a b -> p (a b)"), pbank[3][:]).then_inc(a_hte, 1)

            for t in range(TT):
                act.wait_ge(x2_done, t + 1)
                nc.scalar.activation(junk3[:, t], x2[:, t], ACT.Square, accum_out=ssq3[:, t:t + 1]).then_inc(sumsq3_done, 1)
                act.wait_ge(ms3_done, t + 1)
                nc.scalar.activation(root3[:, t:t + 1], ssq3[:, t:t + 1], ACT.Sqrt).then_inc(root3_done, 1)

        @block.vector
        def _(dve):
            def tt(out_, a, b, op):
                return nc.vector.tensor_tensor(out_, a, b, op)

            dve.wait_ge(sumsq_done, TT)
            nc.vector.tensor_scalar(ssq, ssq, 1.0 / D, EPS, ALU.mult, ALU.add).then_inc(ms_done, 1)
            dve.wait_ge(root_done, 1)
            nc.vector.reciprocal(rstd, root).then_inc(rstd_done, 1)
            dve.wait_ge(rstd_done, 1)
            for t in range(2):
                nc.vector.tensor_scalar(xs[:, t], x1[:, t], rstd[:, t:t + 1], None, ALU.mult).then_inc(xs_vec, 1)
            dve.wait_ge(consts_in, 64)
            for k in range(0, KC, 2):
                dve.wait_ge(xT_done, k + 1)
                nc.vector.tensor_scalar(hT[:, k], pbank[k][:], gmix[:, k:k + 1], None, ALU.mult).then_inc(hT_vec, 1)

            dve.wait_ge(softp_done, 1)
            nc.vector.scalar_tensor_tensor(gz, gz, 0.0, gd, ALU.min, ALU.subtract).then_inc(g_done, 1)
            dve.wait_ge(g_done, 1)
            dve.wait_ge(scan_in, 16)
            for m in range(4):
                src, dst = (gz[:, m], gb[:, m]) if m < 2 else (gz[:, m, ::-1], gb[:, m, ::-1])
                nc.vector.tensor_tensor_scan(dst, scan_keep, src, 0.0, ALU.mult, ALU.add).then_inc(scan_done, 1)
            dve.wait_ge(scan_done, 4)
            gb_n = gb.rearrange("p m (n i) -> p (m n) i", i=CHUNK)
            gd_n = gd.rearrange("p m (n i) -> p (m n) i", i=CHUNK)
            half = 2 * NCH

            def spread(v, d, i):
                return v[:, d * half:(d + 1) * half, i:i + 1].broadcast_to((P, half, CHUNK))

            for d in range(2):
                ref = CHUNK // 2 - 1 if d == 0 else CHUNK // 2
                tt(gd_n[:, d * half:(d + 1) * half], gb_n[:, d * half:(d + 1) * half], spread(gb_n, d, ref),
                   ALU.subtract).then_inc(d1_done, 1)

            def per_dir(v):
                return v.rearrange("p (d m) t -> p d (m t)", d=2)

            def same_dirs(v):
                return v.rearrange("p m t -> p (m t)").unsqueeze(1).broadcast_to((P, 2, HP * T))

            dve.wait_ge(e12_done, 1)
            dve.wait_ge(unit_evicted, 3)
            dve.wait_ge(xT_done, KC)
            tt(per_dir(q_rel), per_dir(gE), same_dirs(gq), ALU.mult).then_inc(q_rel_done, 1)
            dve.wait_ge(e12_done, 2)
            for d in range(2):
                tt(gd_n[:, d * half:(d + 1) * half], spread(gb_n, d, CHUNK - 1 if d == 0 else 0),
                   gb_n[:, d * half:(d + 1) * half], ALU.subtract).then_inc(d3_done, 1)
            dve.wait_ge(e4_done, 1)
            tt(per_dir(q_exp), per_dir(gz), same_dirs(gq), ALU.mult).then_inc(q_exp_done, 1)

            dve.wait_ge(late_in, 32)
            for t in range(TT):
                dve.wait_ge(unit_evicted, 10 + t)
                nc.vector.tensor_scalar(r_exp[:, t], r_exp[:, t], 1.0, None, ALU.add).then_inc(r_step, 1)
                dve.wait_ge(r_step, 3 * t + 1)
                nc.vector.reciprocal(r_exp[:, t], r_exp[:, t]).then_inc(r_step, 1)
                dve.wait_ge(r_step, 3 * t + 2)
                tt(rg[:, t], rg[:, t], r_exp[:, t], ALU.mult).then_inc(r_step, 1)
                dve.wait_ge(r_step, 3 * t + 3)
                gain = gla_gb.unsqueeze(1).broadcast_to((P, GLA_HEADS, DV))
                rv = rg[:, t].rearrange("p (h v) -> p h v", v=DV)
                tt(rv, rv, gain, ALU.mult).then_inc(rg_done, 1)
            dve.wait_ge(dec_done, 2)
            for m in range(4):
                dve.wait_ge(kT_done, m + 1)
                nc.vector.tensor_copy(k_rows[:, m].rearrange("p t j -> p (t j)"), pbank[6 + m % 2][:]).then_inc(k_rows_done, 1)
            dve.wait_ge(sb_copied, 4)
            for par in range(2):
                for c in range(2):
                    cm = causal[64 * c:64 * c + 64].bitcast(U32).unsqueeze(1).broadcast_to((64, 8, CHUNK))
                    nc.vector.copy_predicated(st[64 * c:64 * c + 64, par * 8:par * 8 + 8, 64 * c:64 * c + 64], cm,
                                              pbank[2 + par][64 * c:64 * c + 64, :].rearrange("p (a i) -> p a i", i=CHUNK)
                                              ).then_inc(st_done, 1)
            for s in range(NCH - 1):
                dve.wait_ge(state_done, min(s // 2 * 2 + 2, NCH - 1))
                if s:
                    dve.wait_ge(state_used, 4 * s)
                for d in range(2):
                    n, nxt = (s, s + 1) if d == 0 else (NCH - 1 - s, NCH - 2 - s)
                    for hp in range(HP):
                        m = 2 * d + hp
                        new = pbank[6 + n % 2][:, d * 256 + hp * DV:d * 256 + (hp + 1) * DV]
                        if s == 0:
                            nc.vector.tensor_copy(s_prev[:, m, nxt], new).then_inc(state_used, 1)
                        else:
                            nc.vector.scalar_tensor_tensor(s_prev[:, m, nxt], s_prev[:, m, n], dec[:, m, n:n + 1], new,
                                                           ALU.mult, ALU.add).then_inc(state_used, 1)
            dve.wait_ge(oss_done, 16)
            nc.vector.tensor_scalar(oss, oss, 1.0 / DV, EPS, ALU.mult, ALU.add).then_inc(oms_done, 1)
            dve.wait_ge(oroot_done, 1)
            nc.vector.reciprocal(orstd, oroot).then_inc(orstd_done, 1)
            dve.wait_ge(orstd_done, 1)
            for t in range(TT):
                for h in range(GLA_HEADS):
                    hp, par = divmod(h, 2)
                    c0 = (t % 2) * 256 + hp * DV
                    nc.vector.scalar_tensor_tensor(o_rows[:, t, h * DV:(h + 1) * DV],
                                                   pbank[2 + 2 * par + t // 2][:, c0:c0 + DV], orstd[:, t, h:h + 1],
                                                   rg[:, t, h * DV:(h + 1) * DV], ALU.mult, ALU.mult).then_inc(y_done, 1)

            NU = PAIRS * BLOCKS
            dve.wait_ge(bias_done, 3 * NA_HEADS)
            for i in range(NU + 1):
                if i < NU:
                    pair, b = divmod(i, BLOCKS)
                    dve.wait_ge(s_done, i + 1)
                    if i >= 4:
                        dve.wait_ge(pT_done, i - 3)
                    for par in range(2):
                        tt(probs[i % 4][:, par], pbank[2 * (i % 2) + par][:, 0:NKEY], bias[:, 2 * pair + par, BIAS_VAR[b]],
                           ALU.add).then_inc(s_added, 1)
                    dve.wait_ge(s_added, 2 * (i + 1))
                    nc.vector.tensor_reduce(nmax[:, i], probs[i % 4], AX.X, ALU.max, negate=True).then_inc(nmax_done, 1)
                if i >= 1:
                    dve.wait_ge(exp_done, 2 * i)
                    nc.vector.reciprocal(rsum[:, i - 1], psum_[:, i - 1]).then_inc(rsum_done, 1)

            dve.wait_ge(g2_in, 32)
            for t in range(TT):
                dve.wait_ge(wo_done, t + 1)
                for hf in range(2):
                    cols = slice(hf * 512, (hf + 1) * 512)
                    tt(x1[:, t, cols], x1[:, t, cols], pbank[2 * (t % 2) + hf][:], ALU.add).then_inc(x1_done, 1)
                dve.wait_ge(sumsq2_done, t + 1)
                nc.vector.tensor_scalar(ssq2[:, t:t + 1], ssq2[:, t:t + 1], 1.0 / D, EPS, ALU.mult, ALU.add).then_inc(ms2_done, 1)
                dve.wait_ge(root2_done, t + 1)
                nc.vector.reciprocal(rstd2[:, t:t + 1], root2[:, t:t + 1]).then_inc(rstd2_done, 1)
                dve.wait_ge(rstd2_done, t + 1)
                nc.vector.scalar_tensor_tensor(h2[:, t], x1[:, t], rstd2[:, t:t + 1], g2b, ALU.mult, ALU.mult).then_inc(h2_done, 1)
                dve.wait_ge(h2T_done, t + 1)
                if t >= 2:
                    dve.wait_ge(lg_done, t - 1)
                nc.vector.tensor_copy(hT2[t % 2][:, 4:8].rearrange("p a b -> p (a b)"), pbank[5][:]).then_inc(h2T_vec, 1)

            n_step = [0]

            def then(ins):
                n_step[0] += 1
                ins.then_inc(route_step, 1)
                dve.wait_ge(route_step, n_step[0])

            nc.vector.memset(lg[:, :, GROUPS:8], LOWEST)
            dve.wait_ge(h2_done, TT)
            then(nc.vector.memset(ones, 1.0))
            dve.wait_ge(lg_done, TT)
            lp = pbank[6][:, 0:TT * 64].rearrange("p (t c) -> p t c", c=64)
            tt(lg[:, :, 0:GROUPS], lp[:, :, 0:GROUPS], b_r_sb[:, 0:GROUPS].unsqueeze(1).broadcast_to((P, TT, GROUPS)), ALU.add)
            then(tt(lg[:, :, 8:], lp[:, :, GROUPS:GROUPS + EXPERTS],
                    b_r_sb[:, GROUPS:].unsqueeze(1).broadcast_to((P, TT, EXPERTS)), ALU.add))
            for t in range(TT):
                m = nc.vector.max(gtop[:, t], lg[:, t, 0:8])
            then(m)
            tt(gexp, lg[:, :, 0:GROUPS], gtop[:, :, 0:1].broadcast_to((P, TT, GROUPS)), ALU.subtract).then_inc(gdiff_done, 1)
            for t in range(TT):
                m = nc.vector.max_index(itop8[:, t], gtop[:, t], lg[:, t, 0:8])
            then(m)
            then(nc.vector.tensor_copy(gidx, itop8[:, :, 0:1]))
            then(tt(ghot, iota[:, 0:GROUPS].unsqueeze(1).broadcast_to((P, TT, GROUPS)),
                    gidx.broadcast_to((P, TT, GROUPS)), ALU.is_equal))
            pv = prod.rearrange("p t (g e) -> p t g e", g=GROUPS)
            then(tt(pv, lg[:, :, 8:].rearrange("p t (g e) -> p t g e", g=GROUPS),
                    ghot.unsqueeze(3).broadcast_to((P, TT, GROUPS, PER_GROUP)), ALU.mult))
            then(nc.vector.tensor_reduce(ing, prod.rearrange("p t (g e) -> p t e g", g=GROUPS), AX.X, ALU.add))
            for t in range(TT):
                m = nc.vector.max(etop[:, t], ing[:, t])
            then(m)
            tt(ediff, etop[:, :, 1:2], etop[:, :, 0:1], ALU.subtract).then_inc(ediff_done, 1)
            for t in range(TT):
                m = nc.vector.max_index(eidx[:, t], etop[:, t], ing[:, t])
            then(m)
            then(nc.vector.tensor_copy(eid, eidx[:, :, 0:2]))
            then(nc.vector.scalar_tensor_tensor(eid, gidx.broadcast_to((P, TT, 2)), float(PER_GROUP), eid, ALU.mult, ALU.add))
            for k in range(2):
                m = tt(hot[k], iota.unsqueeze(1).broadcast_to((P, TT, EXPERTS)),
                       eid[:, :, k:k + 1].broadcast_to((P, TT, EXPERTS)), ALU.is_equal)
            then(m)
            tt(both, hot[0], hot[1], ALU.add).then_inc(both_done, 1)
            dve.wait_ge(rank_mm_done, 1)
            cum = pbank[7][:, 0:TT * EXPERTS].rearrange("p (t e) -> p t e", e=EXPERTS)
            for k in range(2):
                then(tt(prod, hot[k], cum, ALU.mult))
                then(nc.vector.tensor_reduce(rank[:, :, k:k + 1], prod, AX.X, ALU.add))
            nc.vector.tensor_reduce(most, pbank[7][:, TT * EXPERTS:(TT + 1) * EXPERTS], AX.X, ALU.max).then_inc(most_done, 1)
            nc.vector.tensor_scalar(fits, rank, float(SLOTS), None, ALU.is_lt)
            then(nc.vector.scalar_tensor_tensor(slotf, eid, float(SLOTS), rank, ALU.mult, ALU.add))
            then(nc.vector.tensor_scalar(slotf, slotf, dump_row, None, ALU.subtract))
            then(tt(slotf, slotf, fits, ALU.mult))
            nc.vector.tensor_scalar(slot, slotf, dump_row, None, ALU.add).then_inc(slots_done, 1)
            dve.wait_ge(gexp_done, 1)
            then(nc.vector.tensor_reduce(gsum, gexp, AX.X, ALU.add))
            dve.wait_ge(eexp_done, 1)
            then(nc.vector.tensor_scalar(eden, eexp, 1.0, None, ALU.add))
            then(tt(eden, eden, gsum, ALU.mult))
            then(nc.vector.reciprocal(comb[:, :, 0:1], eden))
            then(tt(comb[:, :, 1:2], comb[:, :, 0:1], eexp, ALU.mult))

            def rows_T_evict(s, c):
                dve.wait_ge(xt_done, c + 1)
                nc.vector.tensor_copy(xT[s].rearrange("p k t -> p (k t)"), pbank[3][:]).then_inc(xt_evicted, 1)

            def hidden(s, c):
                dve.wait_ge(sil_done, c + 1)
                tt(hid[s], pbank[s][:, 256:512], sil[s], ALU.mult).then_inc(hid_done, 1)

            def y_evict(s, c, stored):
                dve.wait_ge(d_done, c + 1)
                if stored is not None:
                    dve.wait_ge(y_stored[s], 32 * stored)
                nc.vector.tensor_copy(y_sb[s], pbank[5 + s][:]).then_inc(y_evicted, 1)

            rows_T_evict(0, 0)
            hidden(0, 0)
            rows_T_evict(1, 1)
            for e in range(1, 1 + RING):
                hidden(e % RING, e)
                rows_T_evict((e + 1) % RING, e + 1)
                y_evict((e - 1) % RING, e - 1, None)
            with dve.Fori(1, (EXPERTS - 2) // RING) as i:
                for j in range(RING):
                    e = RING * i + 1 + j
                    hidden((1 + j) % RING, e)
                    rows_T_evict((2 + j) % RING, e + 1)
                    y_evict(j, e - 1, i)
            last = EXPERTS - 1
            hidden(last % RING, last)
            for e in (last - 1, last):
                y_evict(e % RING, e, e // RING)

            dve.wait_ge(most_done, 1)
            general = dve.value_load(most[0:1, 0:1], min_val=0, max_val=T)
            with dve.If(general > limit):
                dve.wait_ge(d_done, EXPERTS)
                dve.wait_ge(a_g2, 16)
                for t in range(TT):
                    nc.vector.scalar_tensor_tensor(g_rows[:, t], x1[:, t], rstd2[:, t:t + 1], g_gain, ALU.mult,
                                                   ALU.mult).then_inc(a_h2, 1)
                    nc.vector.tensor_scalar(g_cw[:, t], hot[0][:, t], comb[:, t, 0:1], None, ALU.mult).then_inc(a_cw, 1)
                    dve.wait_ge(a_cw, 2 * t + 1)
                    nc.vector.scalar_tensor_tensor(g_cw[:, t], hot[1][:, t], comb[:, t, 1:2], g_cw[:, t], ALU.mult,
                                                   ALU.add).then_inc(a_cw, 1)
                nc.vector.tensor_copy(x2, x1).then_inc(a_acc, 1)
                dve.wait_ge(a_cw, 2 * TT)
                with dve.Fori(0, EXPERTS) as e:
                    dve.wait_ge(a_acc, 2 * TT * e + 1)
                    nc.vector.tensor_copy(g_col, g_cw[:, :, bass.ds(e, 1)]).then_inc(a_col, 1)
                    dve.wait_ge(a_col, e + 1)
                    for t in range(TT):
                        c = TT * e + t
                        dve.wait_ge(a_sil, c + 1)
                        tt(g_hid, pbank[2][:], g_sil, ALU.mult).then_inc(a_hid, 1)
                        dve.wait_ge(a_d, c + 1)
                        for hf in range(2):
                            acc = x2[:, t, hf * 512:(hf + 1) * 512]
                            nc.vector.scalar_tensor_tensor(acc, pbank[4 + hf][:], g_col[:, t], acc, ALU.mult,
                                                           ALU.add).then_inc(a_acc, 1)
                dve.wait_ge(a_acc, 2 * TT * EXPERTS + 1)
                for t in range(TT):
                    nc.vector.tensor_copy(x2[:, t, 0:1], x2[:, t, 0:1]).then_inc(x2_done, 1)
            with dve.If(general < limit + 1):
                for t in range(TT):
                    dve.wait_ge(gathered[t], 32)
                    nc.vector.scalar_tensor_tensor(x2[:, t], got[t][0], comb[:, t, 0:1], x1[:, t], ALU.mult,
                                                   ALU.add).then_inc(x2_half, 1)
                    dve.wait_ge(x2_half, t + 1)
                    nc.vector.scalar_tensor_tensor(x2[:, t], got[t][1], comb[:, t, 1:2], x2[:, t], ALU.mult,
                                                   ALU.add).then_inc(x2_done, 1)
            dve.wait_ge(gf_in, 16)
            for t in range(TT):
                dve.wait_ge(sumsq3_done, t + 1)
                nc.vector.tensor_scalar(ssq3[:, t:t + 1], ssq3[:, t:t + 1], 1.0 / D, EPS, ALU.mult, ALU.add).then_inc(ms3_done, 1)
                dve.wait_ge(root3_done, t + 1)
                nc.vector.reciprocal(rstd3[:, t:t + 1], root3[:, t:t + 1]).then_inc(rstd3_done, 1)
                dve.wait_ge(rstd3_done, t + 1)
                nc.vector.scalar_tensor_tensor(res[:, t], x2[:, t], rstd3[:, t:t + 1], gfb, ALU.mult, ALU.mult).then_inc(res_done, 1)

        @block.gpsimd
        def _(pool):
            nc.gpsimd.memset(zeros, 0.0).then_inc(zero_ready, 1)
            pool.wait_ge(rstd_done, 1)
            for t in range(2, TT):
                nc.gpsimd.tensor_scalar(xs[:, t], x1[:, t], rstd[:, t:t + 1], None, ALU.mult).then_inc(xs_pool, 1)
            pool.wait_ge(rpb_in, 16 * NA_HEADS)
            pool.wait_ge(mask_in, 16)
            for h in range(NA_HEADS):
                for v in range(3):
                    u0 = WIN_W - v * WIN_W // 2
                    first = rpb_run[:, h, RPB_RUN - 1 - u0:RPB_RUN - u0]
                    run = bass.AP(first.tensor, first.offset, [first.ap[0], [-1, KEY_W], [-RPB_W, ROWS]])
                    nc.gpsimd.tensor_tensor(bias[:, h, v].rearrange("p (j r) -> p j r", r=ROWS), run,
                                            mask[:, v].rearrange("p (j r) -> p j r", r=ROWS), ALU.add).then_inc(bias_done, 1)
            pool.wait_ge(bias_done, 3 * NA_HEADS)
            pool.wait_ge(e12_done, 2)
            pool.wait_ge(unit_evicted, 5)
            pool.wait_ge(zeroed, 32)

            def per_dir(v):
                return v.rearrange("p (d m) t -> p d (m t)", d=2)

            keys = gk.rearrange("p m t -> p (m t)").unsqueeze(1).broadcast_to((P, 2, HP * T))
            nc.gpsimd.tensor_tensor(per_dir(k_rel), per_dir(gz), keys, ALU.mult).then_inc(k_rel_done, 1)
            pool.wait_ge(e3_done, 1)
            nc.gpsimd.tensor_tensor(per_dir(k_dec), per_dir(gE), keys, ALU.mult).then_inc(k_dec_done, 1)
            pool.wait_ge(q_exp_done, 1)
            pool.wait_ge(k_dec_done, 1)
            nc.gpsimd.memset(st, 0.0).then_inc(st_zero, 1)
            for i in range(PAIRS * BLOCKS):
                pool.wait_ge(rsum_done, i + 1)
                for par in range(2):
                    nc.gpsimd.tensor_scalar(probs[i % 4][:, par], probs[i % 4][:, par], rsum[:, i, par:par + 1], None,
                                            ALU.mult).then_inc(p_done, 1)

            pool.wait_ge(slots_done, 1)
            pool.wait_ge(zeroed, 32)
            for t in range(TT):
                for k in range(2):
                    nc.gpsimd.indirect_dma_start(rows_in, bass.IndirectOffsetOnAxis(ap=slot[:, t, k:k + 1], axis=0),
                                                 h2[:, t], None).then_inc(scattered, 16)
            pool.wait_ge(scattered, 16 * 2 * TT)

            def rows_load(e, s):
                pool.dma_start(x_in[s][0:SLOTS], rows_in_d[e]).then_inc(rows_in_sb[s], 16)

            def rows_store(e, c, s):
                pool.wait_ge(y_evicted, c + 1)
                for half in range(2):
                    pool.dma_start(rows_out_d[e, half], y_sb[s][64 * half:64 * half + 64]).then_inc(y_stored[s], 16)

            for e in range(RING):
                rows_load(e, e)
            whole = (EXPERTS - RING) // RING * RING
            with pool.Fori(0, whole // RING) as i:
                for j in range(RING):
                    e = RING * i + j
                    rows_store(e, e, j)
                    pool.wait_ge(xt_done, e + 1)
                    rows_load(e + RING, j)
            for e in range(whole, EXPERTS):
                rows_store(e, e, e % RING)
                if e + RING < EXPERTS:
                    pool.wait_ge(xt_done, e + 1)
                    rows_load(e + RING, e % RING)
            for s in range(RING):
                pool.wait_ge(y_stored[s], 32 * len(range(s, EXPERTS, RING)))
            pool.wait_ge(most_done, 1)
            general = pool.value_load(most[0:1, 0:1], min_val=0, max_val=T)
            with pool.If(general < limit + 1):
                for t in range(TT):
                    for k in range(2):
                        nc.gpsimd.indirect_dma_start(got[t][k], None, rows_out,
                                                     bass.IndirectOffsetOnAxis(ap=slot[:, t, k:k + 1], axis=0)
                                                     ).then_inc(gathered[t], 16)


def constants():
    import numpy as np
    c = np.zeros((P, 353), np.float32)
    c[:, 0:128] = np.eye(P)
    c[:, 128:256] = np.triu(np.ones((P, P)), 1)
    j, i = np.meshgrid(np.arange(P) % CHUNK, np.arange(CHUNK), indexing="ij")
    c[:, 256:320] = j <= i
    c[:, 320:352] = np.arange(EXPERTS)
    c[:, 352] = DUMP + np.arange(P)
    mask = np.full((P, 3, KEY_W, ROWS), NEG, np.float32)
    for var, b in enumerate((0, 1, BLOCKS - 1)):
        for wl in range(BLK_W):
            w = b * BLK_W + wl
            s = min(max(w - WIN_W // 2, 0), GRID_W - WIN_W) - KEY_START[b]
            mask[wl * ROWS:(wl + 1) * ROWS, var, s:s + WIN_W] = 0
    scan = np.ones((P, T), np.float32)
    scan[:, ::CHUNK] = 0
    return c, mask.reshape(P, -1), scan


def kernel(**inputs):
    import numpy as np
    import concourse.bacc as bacc
    from concourse.bass_utils import run_bass_kernel_spmd as run

    nc = bacc.Bacc("TRN2", target_bir_lowering=False, num_devices=1)
    a = {k: np.asarray(v) for k, v in inputs.items()}
    w_g2 = np.zeros((2 * RANK, 512), np.float32)
    w_g2[0:RANK, 0:256] = a["w_g2_f"][0]
    w_g2[RANK:, 256:512] = a["w_g2_b"][0]
    c_small, c_mask, c_scan = constants()
    ins = {
        "x": a["x"],
        "rpb": np.pad(a["rpb"][0, :, ::-1, ::-1].reshape(-1), (RPB_PAD, 64)),
        "w_in": a["w_in"],
        "w_g2": w_g2,
        "b_g": np.concatenate([a["b_g_f"][0], a["b_g_b"][0]]).reshape(4, P).T,
        "gla_g": a["gla_norm_g"],
        "g_mix": a["norm_mix_g"][0].reshape(KC, P).T,
        "w_out": a["w_out"],
        "g_ffn": a["norm_ffn_g"],
        "w_r": np.concatenate([a["w_grp"][0], a["w_exp"][0]], axis=1).reshape(KC, P, -1).transpose(1, 0, 2),
        "b_r": np.concatenate([a["b_grp"], a["b_exp"]], axis=1),
        "w_gate": a["w_gate"], "w_up": a["w_up"], "w_down": a["w_down"],
        "g_fin": a["final_norm_g"].reshape(1, -1),
        "c_small": c_small, "c_mask": c_mask, "c_scan": c_scan,
    }
    arrays, args = {}, []
    for name, v in ins.items():
        v = np.ascontiguousarray(v)
        arrays["in_" + name] = v
        args.append(nc.dram_tensor("in_" + name, v.shape, mybir.dt.from_np(v.dtype), kind="ExternalInput").ap())
    args.append(nc.dram_tensor("out0", (1, T, D), F32, kind="ExternalOutput").ap())
    mixer_and_moe(nc, *args)
    return run(nc, [arrays], core_ids=[0]).results[0]["out0"]
```

```python
from contextlib import ExitStack

import concourse.bass as bass
from concourse import mybir

ALU = mybir.AluOpType
ACT = mybir.ActivationFunctionType
AX = mybir.AxisListType
F32 = mybir.dt.float32
BF16 = mybir.dt.bfloat16
U32 = mybir.dt.uint32
I32 = mybir.dt.int32

P = 128
D = 1024
T = 512
TT = T // P
KC = D // P
GRID_W = 64
ROWS = T // GRID_W
WIN_W = 16
NA_HEADS, NA_DIM = 8, 64
PAIRS = NA_HEADS // 2
BLK_W = P // ROWS
BLOCKS = GRID_W // BLK_W
KEY_W = 2 * BLK_W
NKEY = KEY_W * ROWS
KEY_START = [min(max(b * BLK_W - WIN_W // 2, 0), GRID_W - KEY_W) for b in range(BLOCKS)]
BIAS_VAR = [0, 1, 1, 2]
RPB_H, RPB_W = 2 * ROWS - 1, 2 * WIN_W - 1
RPB_RUN = RPB_W * (ROWS - 1) + KEY_W + WIN_W
RPB_PAD = WIN_W
GLA_HEADS, DK, DV = 4, 64, 128
CHUNK = 64
NCH = T // CHUNK
HP = GLA_HEADS // 2
RANK = 16
GROUPS, PER_GROUP = 4, 8
EXPERTS = GROUPS * PER_GROUP
FF = 512
FC = FF // P
SLOTS = 64
RING = 3
EPS = 1e-6
NEG = -1e30
LOWEST = -3e38
UNIT_BANKS = 2

IN_NQ, IN_NK, IN_NV, IN_GQK, IN_GV, IN_GR, IN_LR = 0, 512, 1024, 1536, 2048, 2560, 3072


def words(kib):
    return int(kib * 256)


def mixer_and_moe(nc, x, rpb, w_in, w_g2, b_g, gla_g, g_mix, w_out, g_ffn, w_r, b_r, w_gate, w_up, w_down, g_fin,
                  c_small, c_mask, c_scan, out, limit=SLOTS):
    with ExitStack() as ctx:
        arena = ctx.enter_context(nc.sbuf_tensor("arena", [P, words(207)], F32))
        pbank = [ctx.enter_context(nc.psum_tensor(f"bank{i}", [P, 512], F32)) for i in range(8)]
        upper_b = ctx.enter_context(nc.sbuf_tensor("upper_b", [P, P], BF16))
        ones_b = ctx.enter_context(nc.sbuf_tensor("ones_b", [P, P], BF16))
        both_b = ctx.enter_context(nc.sbuf_tensor("both_b", [P, TT, EXPERTS], BF16))
        rows_out = nc.dram_tensor("rows_out", [EXPERTS * SLOTS, D], F32).ap()

        def sem(name):
            return ctx.enter_context(nc.semaphore(name))

        def at(kib, *shape):
            n = 1
            for s in shape:
                n *= s
            v = arena[:, words(kib):words(kib) + n]
            if len(shape) == 2:
                return v.rearrange("p (a b) -> p a b", b=shape[1])
            if len(shape) == 3:
                return v.rearrange("p (a b c) -> p a b c", b=shape[1], c=shape[2])
            return v

        hT = at(0, KC, T)
        w_buf = [at(16, KC, 512), at(32, KC, 512)]
        bias = at(48, NA_HEADS, 3, NKEY)
        na_v = at(72, 2 * BLOCKS - 1, 512)
        gz = at(78, 4, T)
        r_exp = at(78, TT, 512)
        gd = at(86, 4, T)
        na_q = at(86, PAIRS, T)
        gE = at(94, 4, T)
        na_k = at(94, PAIRS, T)
        xs = at(102, TT, D)
        gb = at(102, 4, T)
        k_rows = at(102, 4, TT, P)
        q_rel = at(110, 4, T)
        rpb_run = at(118, NA_HEADS, RPB_RUN)
        k_rel = at(118, 4, T)
        o_junk = at(118, 16, DV)
        vT = at(110, PAIRS, T)
        k_dec = at(126, 4, T)
        o_rows = at(126, TT, 512)
        w_og = at(16, KC // 2, D)
        w_on = at(112, KC // 2, D)
        q_exp = at(134, 4, T)
        scan_keep = at(140, T)
        probs = [at(134 + 2 * i, 2, NKEY) for i in range(4)]
        hT2 = [at(136 + 4 * i, KC, P) for i in range(2)]
        h2 = [at(128 + 4 * i, D) for i in range(2)]
        lr = at(142, T)
        probsT = [at(142, 4, P), at(195, 4, P)]
        x1 = at(144, TT, D)
        gla_gb = at(163, DV)
        s_prev = at(163, 4, NCH, DV)
        yT = at(163, KC, T)
        gv = at(179, TT, 512)
        rg = at(187, TT, 512)
        junk = at(179, TT, D)
        h2_part = [[at(171 + 6 * t + 2 * i, D // 2).bitcast(BF16).rearrange("p (k q) -> p k q", k=KC) for i in range(3)]
                   for t in range(TT)]
        junk2 = [at(171 + 6 * t, D) for t in range(TT)]
        gq = at(195, HP, T)
        gk = at(199, HP, T)
        st = at(195, 16, P)
        mask = at(203, 3, NKEY)
        y_rows = [at(203 + 0.5 * i, P) for i in range(2)]
        w_lr = at(206, KC, 2 * RANK)
        g2b = at(199, D)
        gfb = at(128, D)
        wr_sb = at(197, KC, GROUPS + EXPERTS)

        small = at(160, 768)
        pos = [0]

        def take(n):
            v = small[:, pos[0]:pos[0] + n]
            pos[0] += n
            return v

        ident, upper, causal, iota = take(128), take(128), take(64), take(SLOTS)
        gmix, bg = take(8), take(4)
        b_r_sb = take(GROUPS + EXPERTS)
        ssq, root, rstd = take(TT), take(TT), take(TT)
        dec = take(4 * NCH).rearrange("p (m n) -> p m n", m=4)
        oss, oroot, orstd = (take(16).rearrange("p (t h) -> p t h", t=TT) for _ in range(3))
        nmax, psum_, rsum = (take(32).rearrange("p (u h) -> p u h", h=2) for _ in range(3))
        ssq2, root2, rstd2 = take(TT), take(TT), take(TT)
        ssq3, root3, rstd3 = take(TT), take(TT), take(TT)
        comb = take(2 * TT).rearrange("p (t k) -> p t k", k=2)
        slot = take(2 * TT).rearrange("p (t k) -> p t k", k=2).bitcast(U32)
        most = take(1).bitcast(I32)
        assert pos[0] <= 768

        rt = at(204, 768)
        rpos = [0]

        def rtake(*shape):
            n = 1
            for s in shape:
                n *= s
            v = rt[:, rpos[0]:rpos[0] + n]
            rpos[0] += n
            assert rpos[0] <= 768
            if len(shape) == 2:
                v = v.rearrange("p (a b) -> p a b", b=shape[1])
            return v

        lg = rtake(TT, 8 + EXPERTS)
        gtop, itop8, ing = rtake(TT, 8), rtake(TT, 8).bitcast(U32), rtake(TT, 8)
        gidx, ghot, gexp = rtake(TT, 1), rtake(TT, GROUPS), rtake(TT, GROUPS)
        etop, eidx = rtake(TT, 8), rtake(TT, 8).bitcast(U32)
        gsum, ediff, eexp, eden = rtake(TT, 1), rtake(TT, 1), rtake(TT, 1), rtake(TT, 1)
        eid = rtake(TT, 2)
        hot = [rtake(TT, EXPERTS), rtake(TT, EXPERTS)]
        rank, slotf = rtake(TT, 2), rtake(TT, 2)
        prod = at(203, TT, EXPERTS)
        code = at(203.5, TT, EXPERTS)

        xT = at(163, KC, SLOTS)
        hidT = at(165, 2, 2, SLOTS)
        hid = [at(166 + i, 256) for i in range(RING)]
        y_sb = [at(195 + 2 * i, 512) for i in range(RING)]
        pick = [at(201 + 0.5 * i, TT * SLOTS // 2).bitcast(BF16).rearrange("p (t s) -> p t s", t=TT)
                for i in range(RING)]
        wg_sb = [at(48 * i, 2, KC, FF) for i in range(RING)]
        wd_sb = [at(48 * i + 32, FC, D) for i in range(RING)]
        got = [[at(4 * (2 * t + k), D) for k in range(2)] for t in range(TT)]
        res = at(32, TT, D)
        x2 = at(96, TT, D)
        junk3 = at(112, TT, D)

        ident_b = at(169, P // 2).bitcast(BF16)
        g_hT = [at(64 + 4 * t, KC, P) for t in range(TT)]
        g_sil = at(132, FF)
        g_hid = at(134, FF)
        g_hidT = at(136, FC, P)
        g_cw = at(138, TT, EXPERTS)
        g_col = at(139, TT, 1)

        x_in_sb = [sem(f"x_in_sb{t}") for t in range(TT)]
        late_in = sem("late_in")
        consts_in, scan_in, mask_in, rpb_in = sem("consts_in"), sem("scan_in"), sem("mask_in"), sem("rpb_in")
        win_in = [sem(f"win_in{g}") for g in range(7)]
        og_done, og_added, wog_in, upper_ready = sem("og_done"), sem("og_added"), sem("wog_in"), sem("upper_ready")
        sumsq_done, ms_done, root_done, rstd_done = sem("sumsq_done"), sem("ms_done"), sem("root_done"), sem("rstd_done")
        xs_vec, xs_pool = sem("xs_vec"), sem("xs_pool")
        xT_done, hT_act, hT_vec = sem("xT_done"), sem("hT_act"), sem("hT_vec")
        unit_done, unit_evicted = sem("unit_done"), sem("unit_evicted")
        gates_done, z_done, abs_done, expa_done = sem("gates_done"), sem("z_done"), sem("abs_done"), sem("expa_done")
        softp_done, g_done, scan_done, d1_done = sem("softp_done"), sem("g_done"), sem("scan_done"), sem("d1_done")
        e12_done, q_rel_done, k_rel_done, d3_done = sem("e12_done"), sem("q_rel_done"), sem("k_rel_done"), sem("d3_done")
        e3_done, dec_done, e4_done = sem("e3_done"), sem("dec_done"), sem("e4_done")
        k_dec_done, q_exp_done = sem("k_dec_done"), sem("q_exp_done")
        r_step, rg_done, bias_done = sem("r_step"), sem("rg_done"), sem("bias_done")
        kT_done, k_rows_done, scores_done = sem("kT_done"), sem("k_rows_done"), sem("scores_done")
        st_zero, sb_copied, st_done = sem("st_zero"), sem("sb_copied"), sem("st_done")
        state_done, state_used = sem("state_done"), sem("state_used")
        o_done, oss_done, oms_done, oroot_done = sem("o_done"), sem("oss_done"), sem("oms_done"), sem("oroot_done")
        orstd_done, y_done, yg_done, yg_evicted = sem("orstd_done"), sem("y_done"), sem("yg_done"), sem("yg_evicted")
        v_done, v_evicted = sem("v_done"), sem("v_evicted")
        s_done, s_added, nmax_done = sem("s_done"), sem("s_added"), sem("nmax_done")
        exp_done, rsum_done, y_scaled, yt_done = sem("exp_done"), sem("rsum_done"), sem("y_scaled"), sem("yt_done")
        pT_done, pT_evicted, pv_done, yn_evicted = sem("pT_done"), sem("pT_evicted"), sem("pv_done"), sem("yn_evicted")
        wout_in, g2_in, gf_in = sem("wout_in"), sem("g2_in"), sem("gf_in")
        wo_done, x1_done, sumsq2_done, ms2_done = sem("wo_done"), sem("x1_done"), sem("sumsq2_done"), sem("ms2_done")
        root2_done, rstd2_done, h2_done = sem("root2_done"), sem("rstd2_done"), sem("h2_done")
        hi_done, rest_done, mid_done, parts_done = sem("hi_done"), sem("rest_done"), sem("mid_done"), sem("parts_done")
        h2T_done, h2T_act, h2T_vec, lg_done = sem("h2T_done"), sem("h2T_act"), sem("h2T_vec"), sem("lg_done")
        route_step, gdiff_done, gexp_done, ediff_done = sem("route_step"), sem("gdiff_done"), sem("gexp_done"), sem("ediff_done")
        code_done, picked = sem("code_done"), sem("picked")
        eexp_done, both_done, rank_mm_done, slots_done = sem("eexp_done"), sem("both_done"), sem("rank_mm_done"), sem("slots_done")
        most_done = sem("most_done")
        wgu_in = [sem(f"wgu_in{i}") for i in range(RING)]
        wd_in = [sem(f"wd_in{i}") for i in range(RING)]
        y_stored = [sem(f"y_stored{i}") for i in range(RING)]
        xt_done, xt_evicted, gu_done, sil_done = sem("xt_done"), sem("xt_evicted"), sem("gu_done"), sem("sil_done")
        hid_done, ht_done, ht_evicted, d_done, y_evicted = (sem("hid_done"), sem("ht_done"), sem("ht_evicted"),
                                                            sem("d_done"), sem("y_evicted"))
        gathered = [sem(f"gathered{t}") for t in range(TT)]
        x2_half, x2_done, sumsq3_done, ms3_done = sem("x2_half"), sem("x2_done"), sem("sumsq3_done"), sem("ms3_done")
        root3_done, rstd3_done, res_done, out_stored = sem("root3_done"), sem("rstd3_done"), sem("res_done"), sem("out_stored")
        a_col, a_ident = sem("a_col"), sem("a_ident")
        a_T, a_hT, a_w, a_gu, a_sil, a_hid, a_ht, a_hte, a_d, a_acc, a_cw = (
            sem("a_T"), sem("a_hT"), sem("a_w"), sem("a_gu"), sem("a_sil"), sem("a_hid"), sem("a_ht"),
            sem("a_hte"), sem("a_d"), sem("a_acc"), sem("a_cw"))

        x_d = x.rearrange("b (t p) d -> (b t) p d", p=P)
        out_d = out.rearrange("b (t p) d -> (b t) p d", p=P)
        win_d = w_in.rearrange("l (k p) n -> (l p) k n", p=P)
        wout_d = w_out.rearrange("l (k p) n -> (l p) k n", p=P)
        wg_d = w_gate.rearrange("l e (p k) f -> (l e) p k f", k=KC)
        wu_d = w_up.rearrange("l e (p k) f -> (l e) p k f", k=KC)
        wd_d = w_down.rearrange("l e (k p) d -> (l e) p k d", p=P)
        rows_out_d = rows_out.rearrange("(e t) (h d) -> e h t d", t=SLOTS, h=2)

        def h2_by_chunk(t):
            return h2[t % 2].rearrange("p (q k) -> p k q", k=KC)

        block = ctx.enter_context(nc.Block())

        groups = [("lr", None, IN_LR), ("gqk", 0, IN_GQK), ("gv", 1, IN_GV), ("gr", 0, IN_GR),
                  ("nq", 1, IN_NQ), ("nk", 0, IN_NK), ("nv", 1, IN_NV)]

        @block.sync
        def _(sp):
            for t in range(TT):
                sp.dma_start(x1[:, t], x_d[t]).then_inc(x_in_sb[t], 16)
                if t == 0:
                    sp.dma_start(small[:, 0:384], c_small).then_inc(consts_in, 16)
            sp.dma_start(gmix, g_mix).then_inc(consts_in, 16)
            sp.dma_start(bg, b_g).then_inc(consts_in, 16)
            sp.dma_start(w_lr, win_d[:, :, IN_LR:IN_LR + 2 * RANK]).then_inc(win_in[0], 16)
            sp.dma_start(gE[:, 0], w_g2).then_inc(consts_in, 16)
            for g in (1, 2):
                sp.dma_start(w_buf[groups[g][1]], win_d[:, :, groups[g][2]:groups[g][2] + 512]).then_inc(win_in[g], 16)
            for h in range(NA_HEADS):
                run = bass.AP(rpb.tensor, h * RPB_H * RPB_W, [[1, BLK_W], [RPB_W, ROWS], [1, RPB_RUN]])
                sp.dma_start(rpb_run[:, h], run).then_inc(rpb_in, 16)
            sp.dma_start(mask.rearrange("p a b -> p (a b)"), c_mask).then_inc(mask_in, 16)
            sp.dma_start(scan_keep, c_scan).then_inc(scan_in, 16)
            sp.dma_start(gla_gb, gla_g.broadcast_to((P, DV))).then_inc(late_in, 16)
            sp.dma_start(b_r_sb, b_r.broadcast_to((P, GROUPS + EXPERTS))).then_inc(late_in, 16)
            for g in range(3, 7):
                sp.wait_ge(unit_done, 1 + 4 * (g - 2))
                sp.dma_start(w_buf[groups[g][1]], win_d[:, :, groups[g][2]:groups[g][2] + 512]).then_inc(win_in[g], 16)
            sp.wait_ge(unit_done, 21)
            sp.dma_start(w_og, wout_d[:, KC // 2:]).then_inc(wog_in, 16)
            sp.wait_ge(o_done, TT)
            sp.dma_start(g2b, g_ffn.broadcast_to((P, D))).then_inc(g2_in, 16)
            sp.dma_start(wr_sb, w_r).then_inc(g2_in, 16)
            sp.wait_ge(yg_done, GLA_HEADS)
            sp.dma_start(w_on, wout_d[:, 0:KC // 2]).then_inc(wout_in, 16)

            def load_gu(e, s):
                sp.dma_start(wg_sb[s][:, 0], wg_d[e]).then_inc(wgu_in[s], 16)
                sp.dma_start(wg_sb[s][:, 1], wu_d[e]).then_inc(wgu_in[s], 16)

            def load_d(e, s):
                sp.dma_start(wd_sb[s], wd_d[e]).then_inc(wd_in[s], 16)

            sp.wait_ge(unit_done, 25)
            sp.dma_start(wg_sb[0][:, 0], wg_d[0]).then_inc(wgu_in[0], 16)
            load_d(0, 0)
            sp.wait_ge(og_done, 2 * TT)
            sp.dma_start(wg_sb[0][:, 1], wu_d[0]).then_inc(wgu_in[0], 16)
            sp.wait_ge(pv_done, 4 * PAIRS)
            load_gu(1, 1)
            load_d(1, 1)
            sp.dma_start(wg_sb[2][:, 0], wg_d[2]).then_inc(wgu_in[2], 16)
            sp.wait_ge(wo_done, TT)
            sp.dma_start(wg_sb[2][:, 1], wu_d[2]).then_inc(wgu_in[2], 16)
            sp.wait_ge(lg_done, TT)
            sp.wait_ge(parts_done, TT)
            load_d(2, 2)

            def step(e, c, s):
                sp.wait_ge(gu_done, c - 2)
                load_gu(e, s)
                sp.wait_ge(d_done, c - 2)
                load_d(e, s)

            with sp.Fori(1, EXPERTS // RING) as i:
                for j in range(RING):
                    step(RING * i + j, RING * i + j, j)
            for e in range(EXPERTS // RING * RING, EXPERTS):
                step(e, e, e % RING)

            sp.wait_ge(d_done, EXPERTS - 2)
            sp.dma_start(gfb, g_fin.broadcast_to((P, D))).then_inc(gf_in, 16)
            sp.wait_ge(most_done, 1)
            general = sp.value_load(most[0:1, 0:1], min_val=0, max_val=T)
            with sp.If(general > limit):
                sp.wait_ge(d_done, EXPERTS)
                with sp.Fori(0, EXPERTS) as e:
                    sp.wait_ge(a_acc, TT * 2 * e + 1)
                    sp.dma_start(wg_sb[0][:, 0], wg_d[e]).then_inc(a_w, 16)
                    sp.dma_start(wg_sb[0][:, 1], wu_d[e]).then_inc(a_w, 16)
                    sp.dma_start(wd_sb[0], wd_d[e]).then_inc(a_w, 16)

            for t in range(TT):
                sp.wait_ge(res_done, t + 1)
                sp.dma_start(out_d[t], res[:, t]).then_inc(out_stored, 16)
            sp.wait_ge(out_stored, 16 * TT)

        @block.tensor
        def _(pe):
            pe.wait_ge(consts_in, 16 * 4)
            for t in range(TT):
                if t % 2 == 0:
                    pe.wait_ge(xs_vec, t // 2 + 1)
                else:
                    pe.wait_ge(xs_pool, t // 2 + 1)
                for k in range(KC):
                    m = pe.transpose(pbank[k][:, t * P:(t + 1) * P], xs[:, t, k * P:(k + 1) * P], ident)
                    if t == TT - 1:
                        m.then_inc(xT_done, 1)
            pe.wait_ge(hT_act, KC // 2)
            pe.wait_ge(hT_vec, KC // 2)
            count = [0]

            def unit(lhs, rhs):
                n = count[0]
                if n >= UNIT_BANKS:
                    pe.wait_ge(unit_evicted, n - UNIT_BANKS + 1)
                for k in range(KC):
                    m = pe.matmul(pbank[n % UNIT_BANKS][:], lhs(k), rhs(k), start=(k == 0), stop=(k == KC - 1))
                m.then_inc(unit_done, 1)
                count[0] += 1

            def weights_stationary(g, m):
                w = w_buf[groups[g][1]]
                unit(lambda k: w[:, k, m * P:(m + 1) * P], lambda k: hT[:, k])

            def tokens_stationary(g, t):
                w = w_buf[groups[g][1]]
                unit(lambda k: hT[:, k, t * P:(t + 1) * P], lambda k: w[:, k])

            pe.wait_ge(win_in[0], 16)
            for k in range(KC):
                j = 32 * (k % 4)
                m = pe.matmul(pbank[0][j:j + 32], w_lr[:, k], hT[:, k], start=(k < 4), stop=(k >= 4))
            m.then_inc(unit_done, 1)
            count[0] += 1
            pe.wait_ge(win_in[1], 16)
            weights_stationary(1, 0)
            pe.wait_ge(unit_evicted, 1)
            for m in range(4):
                pe.matmul(pbank[2 + m][:], gE[:, 0, m * P:(m + 1) * P], lr,
                          start=True, stop=True).then_inc(gates_done, 1)
            for m in range(1, 4):
                weights_stationary(1, m)
            for g in (2, 3):
                pe.wait_ge(win_in[g], 16)
                for t in range(TT):
                    tokens_stationary(g, t)

            pe.wait_ge(k_dec_done, 1)
            for m in range(4):
                if m >= 2:
                    pe.wait_ge(k_rows_done, m - 1)
                for t in range(TT):
                    mm = pe.transpose(pbank[6 + m % 2][:, t * P:(t + 1) * P], k_dec[:, m, t * P:(t + 1) * P], ident)
                mm.then_inc(kT_done, 1)
            pe.wait_ge(q_rel_done, 1)
            pe.wait_ge(k_rel_done, 1)
            for d in range(2):
                for n in range(NCH):
                    for hp in range(HP):
                        for par in range(2):
                            rows = slice(64 * par, 64 * par + 64)
                            c = (hp * (NCH // 2) + n // 2) * CHUNK
                            mm = pe.matmul(pbank[2 + 2 * d + par][64 * (n % 2):64 * (n % 2) + 64, c:c + CHUNK],
                                           k_rel[rows, 2 * d + hp, n * CHUNK:(n + 1) * CHUNK],
                                           q_rel[rows, 2 * d + hp, n * CHUNK:(n + 1) * CHUNK], start=True, stop=True)
                mm.then_inc(scores_done, 1)

            pe.wait_ge(win_in[4], 16)
            for s2 in range(4):
                weights_stationary(4, s2)
                if s2 == 0:
                    pe.wait_ge(k_rows_done, 4)
                else:
                    pe.wait_ge(state_used, 8 * s2)
                for s in (2 * s2, 2 * s2 + 1):
                    if s == NCH - 1:
                        continue
                    for d in range(2):
                        n = s if d == 0 else NCH - 1 - s
                        rows = slice(64 * (n % 2), 64 * (n % 2) + 64)
                        for hp in range(HP):
                            for par in range(2):
                                h = 2 * hp + par
                                mm = pe.matmul(
                                    pbank[6 + n % 2][64 * par:64 * par + 64, d * 256 + hp * DV:d * 256 + (hp + 1) * DV],
                                    k_rows[rows, 2 * d + hp, n // 2, par * DK:(par + 1) * DK],
                                    gv[rows, n // 2, h * DV:(h + 1) * DV], start=True, stop=True)
                    mm.then_inc(state_done, 1)
            pe.wait_ge(win_in[5], 16)
            for m in range(4):
                weights_stationary(5, m)
            pe.wait_ge(st_done, 4)
            pe.wait_ge(state_used, 28)
            pe.wait_ge(q_exp_done, 1)
            for t in range(TT):
                for hp in range(HP):
                    for par in range(2):
                        h = 2 * hp + par
                        rows = slice(64 * par, 64 * par + 64)
                        c0 = (t % 2) * 256 + hp * DV
                        bank = pbank[2 + 2 * par + t // 2]
                        pe.matmul(bank[:, c0:c0 + DV], st[:, par * 8 + hp * 4 + t], gv[:, t, h * DV:(h + 1) * DV],
                                  start=True, stop=False)
                        for c in range(2):
                            n = 2 * t + c
                            dirs = [d for d in range(2) if not (d == 0 and n == 0) and not (d == 1 and n == NCH - 1)]
                            for d in dirs:
                                mm = pe.matmul(bank[64 * c:64 * c + 64, c0:c0 + DV],
                                               q_exp[rows, 2 * d + hp, n * CHUNK:(n + 1) * CHUNK],
                                               s_prev[rows, 2 * d + hp, n], start=False, stop=(d == dirs[-1]))
                mm.then_inc(o_done, 1)
            pe.wait_ge(win_in[6], 16)
            for m in range(4):
                weights_stationary(6, m)
            pe.wait_ge(unit_evicted, 25)
            for i in range(2 * BLOCKS - 1):
                if i >= 2:
                    pe.wait_ge(v_evicted, i - 1)
                for m in range(PAIRS):
                    mm = pe.transpose(pbank[6 + i % 2][:, m * P:(m + 1) * P], vT[:, m, i * 64:i * 64 + P], ident)
                mm.then_inc(v_done, 1)
            pe.wait_ge(v_evicted, 2 * BLOCKS - 1)
            NU = PAIRS * BLOCKS

            def na_scores(i):
                pair, b = divmod(i, BLOCKS)
                if i >= 2:
                    pe.wait_ge(s_added, 2 * (i - 1))
                for par in range(2):
                    rows = slice(64 * par, 64 * par + 64)
                    k0 = KEY_START[b] * ROWS
                    mm = pe.matmul(pbank[2 + 2 * (i % 2) + par][:, 0:NKEY], na_q[rows, pair, b * P:(b + 1) * P],
                                   na_k[rows, pair, k0:k0 + NKEY], start=True, stop=True)
                mm.then_inc(s_done, 1)

            pe.wait_ge(y_done, 16)
            na_scores(0)
            na_scores(1)
            for h in range(GLA_HEADS):
                if h >= 2:
                    pe.wait_ge(yg_evicted, h - 1)
                for t in range(TT):
                    mm = pe.transpose(pbank[6 + h % 2][:, t * P:(t + 1) * P], o_rows[:, t, h * DV:(h + 1) * DV], ident)
                mm.then_inc(yg_done, 1)

            for i in range(2, NU + 4):
                if i < NU:
                    na_scores(i)
                if 0 <= i - 2 < NU:
                    u = i - 2
                    pe.wait_ge(exp_done, 2 * (u + 1))
                    if u >= 1:
                        pe.wait_ge(pT_evicted, u)
                    for par in range(2):
                        for c in range(2):
                            a = 2 * par + c
                            mm = pe.transpose(pbank[6][:, a * P:(a + 1) * P],
                                              probs[u % 4][:, par, c * P:(c + 1) * P], ident)
                    mm.then_inc(pT_done, 1)
                if 0 <= i - 3 < NU:
                    u = i - 3
                    pair, b = divmod(u, BLOCKS)
                    pe.wait_ge(pT_evicted, u + 1)
                    if u >= 1:
                        pe.wait_ge(y_scaled, u)
                    v0 = KEY_START[b] * ROWS // 64
                    for par in range(2):
                        h = 2 * pair + par
                        for c in range(2):
                            mm = pe.matmul(pbank[1][:, par * NA_DIM:(par + 1) * NA_DIM], probsT[u % 2][:, 2 * par + c],
                                           na_v[:, v0 + 2 * c, h * NA_DIM:(h + 1) * NA_DIM], start=(c == 0), stop=(c == 1))
                    mm.then_inc(pv_done, 1)
                if i >= 4:
                    u = i - 4
                    pair, b = divmod(u, BLOCKS)
                    pe.wait_ge(y_scaled, u + 1)
                    if b == 0 and pair >= 1:
                        pe.wait_ge(yn_evicted, pair)
                    pe.transpose(pbank[7][:, b * P:(b + 1) * P], y_rows[u % 2], ident).then_inc(yt_done, 1)
                if i % 2 == 0 and i // 2 - 1 < 2 * TT:
                    j = i // 2 - 1
                    if j == 0:
                        pe.wait_ge(wog_in, 16)
                        pe.wait_ge(yg_evicted, GLA_HEADS)
                    else:
                        pe.wait_ge(og_added, j)
                    t, half = divmod(j, 2)
                    for k in range(KC // 2):
                        mm = pe.matmul(pbank[0][:], yT[:, KC // 2 + k, t * P:(t + 1) * P],
                                       w_og[:, k, half * 512:(half + 1) * 512], start=(k == 0), stop=(k == KC // 2 - 1))
                    mm.then_inc(og_done, 1)

            def out_proj(t):
                if t >= 2:
                    pe.wait_ge(x1_done, 2 * (t - 1))
                for half in range(2):
                    for k in range(KC // 2):
                        mm = pe.matmul(pbank[2 * (t % 2) + half][:], yT[:, k, t * P:(t + 1) * P],
                                       w_on[:, k, half * 512:(half + 1) * 512], start=(k == 0), stop=(k == KC // 2 - 1))
                mm.then_inc(wo_done, 1)

            def router(t):
                pe.wait_ge(h2_done, t + 1)
                if t >= 1:
                    pe.wait_ge(h2T_act, t)
                    pe.wait_ge(h2T_vec, t)
                for k in range(KC):
                    mm = pe.transpose(pbank[4 + k // 4][:, (k % 4) * P:(k % 4 + 1) * P], h2[t % 2][:, k * P:(k + 1) * P],
                                      ident)
                mm.then_inc(h2T_done, 1)
                pe.wait_ge(h2T_act, t + 1)
                pe.wait_ge(h2T_vec, t + 1)
                if t >= 2:
                    pe.wait_ge(both_done, t - 1)
                for k in range(KC):
                    mm = pe.matmul(pbank[6 + t % 2][:, 0:GROUPS + EXPERTS], hT2[t % 2][:, k], wr_sb[:, k],
                                   start=(k == 0), stop=(k == KC - 1))
                mm.then_inc(lg_done, 1)

            pe.wait_ge(yn_evicted, PAIRS)
            pe.wait_ge(wout_in, 16)
            pe.wait_ge(g2_in, 32)
            out_proj(0)
            out_proj(1)
            router(0)
            out_proj(2)
            router(1)
            out_proj(3)
            router(2)
            router(3)
            pe.wait_ge(both_done, TT)
            pe.wait_ge(upper_ready, 2)
            for t in range(TT + 1):
                for s in range(min(t + 1, TT)):
                    mm = pe.matmul(pbank[6][:, t * EXPERTS:(t + 1) * EXPERTS], (upper_b if s == t else ones_b)[:],
                                   both_b[:, s], start=(s == 0), stop=(s == min(t, TT - 1)))
            mm.then_inc(rank_mm_done, 1)

            def pick_rows(s, c):
                pe.wait_ge(picked, c + 1)
                for k in range(KC):
                    for t in range(TT):
                        for i in range(3):
                            mm = pe.matmul(pbank[3][:, k * SLOTS:(k + 1) * SLOTS], h2_part[t][i][:, k], pick[s][:, t],
                                           start=(t == 0 and i == 0), stop=(t == TT - 1 and i == 2))
                mm.then_inc(xt_done, 1)

            def gate_up(s, q, c):
                pe.wait_ge(xt_evicted, c + 1)
                pe.wait_ge(wgu_in[s], 32 * q + 32)
                for k in range(KC):
                    for half in range(2):
                        mm = pe.matmul(pbank[s][64 * half:64 * half + 64, :].rearrange("p (g f) -> p g f", g=2),
                                       xT[:, k], wg_sb[s][:, :, k, half * 256:(half + 1) * 256],
                                       start=(k == 0), stop=(k == KC - 1))
                mm.then_inc(gu_done, 1)

            def hidden_T(s, c):
                pe.wait_ge(hid_done, c + 1)
                pe.nop(nofuse=True)
                for cc in range(2):
                    mm = pe.transpose(pbank[4][:, cc * P:(cc + 1) * P], hid[s][:, cc * P:(cc + 1) * P], ident)
                mm.then_inc(ht_done, 1)

            def down(s, q, c):
                pe.wait_ge(ht_evicted, c + 1)
                pe.wait_ge(wd_in[s], 16 * q + 16)
                for kc in range(FC):
                    for half in range(2):
                        mm = pe.matmul(pbank[5 + s][64 * half:64 * half + 64, :], hidT[:, kc % 2, kc // 2],
                                       wd_sb[s][:, kc, half * 512:(half + 1) * 512],
                                       start=(kc == 0), stop=(kc == FC - 1))
                mm.then_inc(d_done, 1)

            pe.wait_ge(parts_done, TT)
            pick_rows(0, 0)
            gate_up(0, 0, 0)
            pick_rows(1, 1)
            with pe.Fori(0, (EXPERTS - 2) // RING) as i:
                for j in range(RING):
                    e = RING * i + 1 + j
                    gate_up((1 + j) % RING, i + (1 + j) // RING, e)
                    hidden_T(j, e - 1)
                    pick_rows((2 + j) % RING, e + 1)
                    down(j, i, e - 1)
            last = EXPERTS - 1
            gate_up(last % RING, last // RING, last)
            hidden_T((last - 1) % RING, last - 1)
            down((last - 1) % RING, (last - 1) // RING, last - 1)
            hidden_T(last % RING, last)
            down(last % RING, last // RING, last)

            pe.wait_ge(most_done, 1)
            general = pe.value_load(most[0:1, 0:1], min_val=0, max_val=T)
            with pe.If(general > limit):
                pe.wait_ge(a_ident, 1)
                for t in range(TT):
                    for g in range(2):
                        if 2 * t + g >= 1:
                            pe.wait_ge(a_hT, 2 * t + g)
                        for k in range(4):
                            for i in range(3):
                                mm = pe.matmul(pbank[0][:, k * P:(k + 1) * P], h2_part[t][i][:, 4 * g + k], ident_b,
                                               start=(i == 0), stop=(i == 2))
                        mm.then_inc(a_T, 1)
                pe.wait_ge(a_hT, 2 * TT)
                with pe.Fori(0, EXPERTS) as e:
                    pe.wait_ge(a_w, 48 * e + 48)
                    for t in range(TT):
                        c = TT * e + t
                        for g in range(2):
                            for k in range(KC):
                                mm = pe.matmul(pbank[1 + g][:], g_hT[t][:, k], wg_sb[0][:, g, k],
                                               start=(k == 0), stop=(k == KC - 1))
                        mm.then_inc(a_gu, 1)
                        pe.wait_ge(a_hid, c + 1)
                        pe.nop(nofuse=True)
                        for k in range(FC):
                            mm = pe.transpose(pbank[3][:, k * P:(k + 1) * P], g_hid[:, k * P:(k + 1) * P], ident)
                        mm.then_inc(a_ht, 1)
                        pe.wait_ge(a_hte, c + 1)
                        for half in range(2):
                            for k in range(FC):
                                mm = pe.matmul(pbank[4 + half][:], g_hidT[:, k], wd_sb[0][:, k, half * 512:(half + 1) * 512],
                                               start=(k == 0), stop=(k == FC - 1))
                        mm.then_inc(a_d, 1)
                        pe.wait_ge(a_acc, 2 * c + 3)

        @block.scalar
        def _(act):
            def scaled_copy(dst, src, scale):
                return nc.scalar.activation(dst, src, ACT.Identity, scale=scale)

            for t in range(TT):
                act.wait_ge(x_in_sb[t], 16)
                nc.scalar.activation(junk[:, t], x1[:, t], ACT.Square, accum_out=ssq[:, t:t + 1]).then_inc(sumsq_done, 1)
                act.wait_ge(ms_done, t + 1)
                nc.scalar.activation(root[:, t:t + 1], ssq[:, t:t + 1], ACT.Sqrt).then_inc(root_done, 1)
            act.wait_ge(consts_in, 64)
            for k in range(1, KC, 2):
                act.wait_ge(xT_done, k + 1)
                scaled_copy(hT[:, k], pbank[k][:], gmix[:, k:k + 1]).then_inc(hT_act, 1)

            def gla_q_evict(n, m):
                act.wait_ge(unit_done, n + 1)
                dst = gq[:, m] if m < HP else gk[:, m - HP]
                scaled_copy(dst, pbank[n % 2][:], DK ** -0.5 if m < HP else 1.0).then_inc(unit_evicted, 1)

            def gv_evict(n, t):
                act.wait_ge(unit_done, n + 1)
                nc.scalar.copy(gv[:, t], pbank[n % 2][:]).then_inc(unit_evicted, 1)

            act.wait_ge(sumsq_done, TT)
            act.wait_ge(unit_done, 1)
            nc.scalar.copy(lr, pbank[0][:]).then_inc(unit_evicted, 1)
            gla_q_evict(1, 0)
            for m in range(4):
                act.wait_ge(gates_done, m + 1)
                nc.scalar.activation(gz[:, m], pbank[2 + m][:], ACT.Identity, bias=bg[:, m:m + 1]).then_inc(z_done, 1)
            for m in range(1, 4):
                gla_q_evict(1 + m, m)
            act.wait_ge(z_done, 4)
            nc.scalar.activation(gd, gz, ACT.Abs).then_inc(abs_done, 1)
            act.wait_ge(abs_done, 1)
            nc.scalar.activation(gE, gd, ACT.Exp, scale=-1.0).then_inc(expa_done, 1)
            act.wait_ge(expa_done, 1)
            nc.scalar.activation(gd, gE, ACT.Ln, bias=1.0).then_inc(softp_done, 1)
            gv_evict(5, 0)
            act.wait_ge(d1_done, 2)
            nc.scalar.activation(gE, gd, ACT.Exp, scale=1.0 / 16).then_inc(e12_done, 1)
            nc.scalar.activation(gz, gd, ACT.Exp, scale=-1.0 / 16).then_inc(e12_done, 1)
            gv_evict(6, 1)
            act.wait_ge(d3_done, 2)
            act.wait_ge(q_rel_done, 1)
            nc.scalar.activation(gE, gd, ACT.Exp, scale=1.0 / 16).then_inc(e3_done, 1)
            gbn = gb.rearrange("p m (n i) -> p m n i", i=CHUNK)
            nc.scalar.activation(dec[:, 0:2], gbn[:, 0:2, :, CHUNK - 1], ACT.Exp, scale=1.0 / 16).then_inc(dec_done, 1)
            nc.scalar.activation(dec[:, 2:4], gbn[:, 2:4, :, 0], ACT.Exp, scale=1.0 / 16).then_inc(dec_done, 1)
            act.wait_ge(k_rel_done, 1)
            nc.scalar.activation(gz, gb, ACT.Exp, scale=1.0 / 16).then_inc(e4_done, 1)
            gv_evict(7, 2)
            gv_evict(8, 3)
            act.wait_ge(q_exp_done, 1)
            for t in range(TT):
                act.wait_ge(unit_done, 10 + t)
                nc.scalar.copy(rg[:, t], pbank[(9 + t) % 2][:])
                nc.scalar.activation(r_exp[:, t], pbank[(9 + t) % 2][:], ACT.Exp, scale=-1.0).then_inc(unit_evicted, 1)
            act.wait_ge(scores_done, 2)
            act.wait_ge(st_zero, 1)
            for par in range(2):
                for c in range(2):
                    nc.scalar.copy(st[64 * c:64 * c + 64, par * 8:par * 8 + 8, 64 * c:64 * c + 64],
                                   pbank[4 + par][64 * c:64 * c + 64, :].rearrange("p (a i) -> p a i", i=CHUNK)
                                   ).then_inc(sb_copied, 1)
            for m in range(4):
                act.wait_ge(unit_done, 14 + m)
                nc.scalar.activation(na_q[:, m].rearrange("p (w r) -> p w r", r=ROWS),
                                     pbank[(13 + m) % 2][:].rearrange("p (r w) -> p w r", w=GRID_W),
                                     ACT.Identity, scale=NA_DIM ** -0.5).then_inc(unit_evicted, 1)
            act.wait_ge(k_dec_done, 1)
            for m in range(4):
                act.wait_ge(unit_done, 18 + m)
                nc.scalar.copy(na_k[:, m].rearrange("p (w r) -> p w r", r=ROWS),
                               pbank[(17 + m) % 2][:].rearrange("p (r w) -> p w r", w=GRID_W)).then_inc(unit_evicted, 1)

            def o_slice(t, h):
                hp, par = divmod(h, 2)
                c0 = (t % 2) * 256 + hp * DV
                return pbank[2 + 2 * par + t // 2][:, c0:c0 + DV]

            for t in range(TT):
                act.wait_ge(o_done, t // 2 * 2 + 2)
                for h in range(GLA_HEADS):
                    nc.scalar.activation(o_junk[:, 4 * t + h], o_slice(t, h), ACT.Square,
                                         accum_out=oss[:, t, h:h + 1]).then_inc(oss_done, 1)
            act.wait_ge(oms_done, 1)
            nc.scalar.activation(oroot, oss, ACT.Sqrt).then_inc(oroot_done, 1)
            for m in range(4):
                act.wait_ge(unit_done, 22 + m)
                nc.scalar.copy(vT[:, m].rearrange("p (w r) -> p w r", r=ROWS),
                               pbank[(21 + m) % 2][:].rearrange("p (r w) -> p w r", w=GRID_W)).then_inc(unit_evicted, 1)
            act.wait_ge(rg_done, TT)
            for i in range(2 * BLOCKS - 1):
                act.wait_ge(v_done, i + 1)
                nc.scalar.copy(na_v[:, i], pbank[6 + i % 2][:]).then_inc(v_evicted, 1)
            for h in range(GLA_HEADS):
                act.wait_ge(yg_done, h + 1)
                nc.scalar.copy(yT[:, 4 + h], pbank[6 + h % 2][:]).then_inc(yg_evicted, 1)

            NU = PAIRS * BLOCKS
            for i in range(NU + 4):
                if i < NU:
                    act.wait_ge(nmax_done, i + 1)
                    for par in range(2):
                        nc.scalar.activation(probs[i % 4][:, par], probs[i % 4][:, par], ACT.Exp,
                                             bias=nmax[:, i, par:par + 1],
                                             accum_out=psum_[:, i, par:par + 1]).then_inc(exp_done, 1)
                if 0 <= i - 2 < NU:
                    u = i - 2
                    act.wait_ge(pT_done, u + 1)
                    if u >= 2:
                        act.wait_ge(pv_done, u - 1)
                    nc.scalar.copy(probsT[u % 2].rearrange("p a b -> p (a b)"), pbank[6][:]).then_inc(pT_evicted, 1)
                if i >= 4 and (i - 4) % BLOCKS == BLOCKS - 1:
                    pair = (i - 4) // BLOCKS
                    act.wait_ge(yt_done, i - 3)
                    nc.scalar.copy(yT[:, pair].rearrange("p (r w) -> p w r", w=GRID_W),
                                   pbank[7][:].rearrange("p (w r) -> p w r", r=ROWS)).then_inc(yn_evicted, 1)

            for t in range(TT):
                act.wait_ge(x1_done, 2 * (t + 1))
                nc.scalar.activation(junk2[t], x1[:, t], ACT.Square, accum_out=ssq2[:, t:t + 1]).then_inc(sumsq2_done, 1)
                act.wait_ge(ms2_done, t + 1)
                nc.scalar.activation(root2[:, t:t + 1], ssq2[:, t:t + 1], ACT.Sqrt).then_inc(root2_done, 1)
                act.wait_ge(h2T_done, t + 1)
                if t >= 2:
                    act.wait_ge(lg_done, t - 1)
                nc.scalar.copy(hT2[t % 2][:, 0:4].rearrange("p a b -> p (a b)"), pbank[4][:]).then_inc(h2T_act, 1)
                act.wait_ge(sumsq2_done, t + 1)
                nc.scalar.copy(h2_part[t][0], h2_by_chunk(t)).then_inc(hi_done, 1)
                act.wait_ge(rest_done, t + 1)
                nc.scalar.copy(h2_part[t][1], h2_by_chunk(t)).then_inc(mid_done, 1)
            act.wait_ge(gdiff_done, 1)
            nc.scalar.activation(gexp, gexp, ACT.Exp).then_inc(gexp_done, 1)
            act.wait_ge(ediff_done, 1)
            nc.scalar.activation(eexp, ediff, ACT.Exp).then_inc(eexp_done, 1)

            def silu(s, c):
                act.wait_ge(gu_done, c + 1)
                nc.scalar.activation(hid[s], pbank[s][:, 0:256], ACT.Silu).then_inc(sil_done, 1)

            def hidden_T_evict(s, c):
                act.wait_ge(ht_done, c + 1)
                nc.scalar.copy(hidT.rearrange("p c h t -> p (c h t)"), pbank[4][:, 0:256]).then_inc(ht_evicted, 1)

            silu(0, 0)
            with act.Fori(0, (EXPERTS - 2) // RING) as i:
                for j in range(RING):
                    e = RING * i + 1 + j
                    silu((1 + j) % RING, e)
                    hidden_T_evict(j, e - 1)
            last = EXPERTS - 1
            silu(last % RING, last)
            hidden_T_evict((last - 1) % RING, last - 1)
            hidden_T_evict(last % RING, last)

            act.wait_ge(most_done, 1)
            general = act.value_load(most[0:1, 0:1], min_val=0, max_val=T)
            with act.If(general > limit):
                for c in range(2 * TT):
                    act.wait_ge(a_T, c + 1)
                    nc.scalar.copy(g_hT[c // 2][:, 4 * (c % 2):4 * (c % 2) + 4].rearrange("p a b -> p (a b)"),
                                   pbank[0][:]).then_inc(a_hT, 1)
                with act.Fori(0, EXPERTS) as e:
                    for t in range(TT):
                        c = TT * e + t
                        act.wait_ge(a_gu, c + 1)
                        nc.scalar.activation(g_sil, pbank[1][:], ACT.Silu).then_inc(a_sil, 1)
                        act.wait_ge(a_ht, c + 1)
                        nc.scalar.copy(g_hidT.rearrange("p a b -> p (a b)"), pbank[3][:]).then_inc(a_hte, 1)

            for t in range(TT):
                act.wait_ge(x2_done, t + 1)
                nc.scalar.activation(junk3[:, t], x2[:, t], ACT.Square, accum_out=ssq3[:, t:t + 1]).then_inc(sumsq3_done, 1)
                act.wait_ge(ms3_done, t + 1)
                nc.scalar.activation(root3[:, t:t + 1], ssq3[:, t:t + 1], ACT.Sqrt).then_inc(root3_done, 1)

        @block.vector
        def _(dve):
            def tt(out_, a, b, op):
                return nc.vector.tensor_tensor(out_, a, b, op)

            for t in range(TT):
                dve.wait_ge(sumsq_done, t + 1)
                nc.vector.tensor_scalar(ssq[:, t:t + 1], ssq[:, t:t + 1], 1.0 / D, EPS, ALU.mult, ALU.add).then_inc(ms_done, 1)
                dve.wait_ge(root_done, t + 1)
                nc.vector.reciprocal(rstd[:, t:t + 1], root[:, t:t + 1]).then_inc(rstd_done, 1)
                if t % 2 == 0:
                    dve.wait_ge(rstd_done, t + 1)
                    nc.vector.tensor_scalar(xs[:, t], x1[:, t], rstd[:, t:t + 1], None, ALU.mult).then_inc(xs_vec, 1)
            dve.wait_ge(consts_in, 64)
            for k in range(0, KC, 2):
                dve.wait_ge(xT_done, k + 1)
                nc.vector.tensor_scalar(hT[:, k], pbank[k][:], gmix[:, k:k + 1], None, ALU.mult).then_inc(hT_vec, 1)

            dve.wait_ge(softp_done, 1)
            nc.vector.scalar_tensor_tensor(gz, gz, 0.0, gd, ALU.min, ALU.subtract).then_inc(g_done, 1)
            dve.wait_ge(g_done, 1)
            dve.wait_ge(scan_in, 16)
            for m in range(4):
                src, dst = (gz[:, m], gb[:, m]) if m < 2 else (gz[:, m, ::-1], gb[:, m, ::-1])
                nc.vector.tensor_tensor_scan(dst, scan_keep, src, 0.0, ALU.mult, ALU.add).then_inc(scan_done, 1)
            dve.wait_ge(scan_done, 4)
            gb_n = gb.rearrange("p m (n i) -> p (m n) i", i=CHUNK)
            gd_n = gd.rearrange("p m (n i) -> p (m n) i", i=CHUNK)
            half = 2 * NCH

            def spread(v, d, i):
                return v[:, d * half:(d + 1) * half, i:i + 1].broadcast_to((P, half, CHUNK))

            for d in range(2):
                ref = CHUNK // 2 - 1 if d == 0 else CHUNK // 2
                tt(gd_n[:, d * half:(d + 1) * half], gb_n[:, d * half:(d + 1) * half], spread(gb_n, d, ref),
                   ALU.subtract).then_inc(d1_done, 1)

            def per_dir(v):
                return v.rearrange("p (d m) t -> p d (m t)", d=2)

            def same_dirs(v):
                return v.rearrange("p m t -> p (m t)").unsqueeze(1).broadcast_to((P, 2, HP * T))

            dve.wait_ge(e12_done, 1)
            dve.wait_ge(unit_evicted, 3)
            dve.wait_ge(xT_done, KC)
            tt(per_dir(q_rel), per_dir(gE), same_dirs(gq), ALU.mult).then_inc(q_rel_done, 1)
            dve.wait_ge(e12_done, 2)
            for d in range(2):
                tt(gd_n[:, d * half:(d + 1) * half], spread(gb_n, d, CHUNK - 1 if d == 0 else 0),
                   gb_n[:, d * half:(d + 1) * half], ALU.subtract).then_inc(d3_done, 1)
            dve.wait_ge(e4_done, 1)
            tt(per_dir(q_exp), per_dir(gz), same_dirs(gq), ALU.mult).then_inc(q_exp_done, 1)

            dve.wait_ge(late_in, 32)
            for t in range(TT):
                dve.wait_ge(unit_evicted, 10 + t)
                nc.vector.tensor_scalar(r_exp[:, t], r_exp[:, t], 1.0, None, ALU.add).then_inc(r_step, 1)
                dve.wait_ge(r_step, 3 * t + 1)
                nc.vector.reciprocal(r_exp[:, t], r_exp[:, t]).then_inc(r_step, 1)
                dve.wait_ge(r_step, 3 * t + 2)
                tt(rg[:, t], rg[:, t], r_exp[:, t], ALU.mult).then_inc(r_step, 1)
                dve.wait_ge(r_step, 3 * t + 3)
                gain = gla_gb.unsqueeze(1).broadcast_to((P, GLA_HEADS, DV))
                rv = rg[:, t].rearrange("p (h v) -> p h v", v=DV)
                tt(rv, rv, gain, ALU.mult).then_inc(rg_done, 1)
            dve.wait_ge(dec_done, 2)
            for m in range(4):
                dve.wait_ge(kT_done, m + 1)
                nc.vector.tensor_copy(k_rows[:, m].rearrange("p t j -> p (t j)"), pbank[6 + m % 2][:]).then_inc(k_rows_done, 1)
            dve.wait_ge(sb_copied, 4)
            for par in range(2):
                for c in range(2):
                    cm = causal[64 * c:64 * c + 64].bitcast(U32).unsqueeze(1).broadcast_to((64, 8, CHUNK))
                    nc.vector.copy_predicated(st[64 * c:64 * c + 64, par * 8:par * 8 + 8, 64 * c:64 * c + 64], cm,
                                              pbank[2 + par][64 * c:64 * c + 64, :].rearrange("p (a i) -> p a i", i=CHUNK)
                                              ).then_inc(st_done, 1)
            dve.wait_ge(rg_done, TT)
            for s in range(NCH - 1):
                dve.wait_ge(state_done, min(s // 2 * 2 + 2, NCH - 1))
                if s:
                    dve.wait_ge(state_used, 4 * s)
                for d in range(2):
                    n, nxt = (s, s + 1) if d == 0 else (NCH - 1 - s, NCH - 2 - s)
                    for hp in range(HP):
                        m = 2 * d + hp
                        new = pbank[6 + n % 2][:, d * 256 + hp * DV:d * 256 + (hp + 1) * DV]
                        if s == 0:
                            nc.vector.tensor_copy(s_prev[:, m, nxt], new).then_inc(state_used, 1)
                        else:
                            nc.vector.scalar_tensor_tensor(s_prev[:, m, nxt], s_prev[:, m, n], dec[:, m, n:n + 1], new,
                                                           ALU.mult, ALU.add).then_inc(state_used, 1)
            dve.wait_ge(oss_done, 16)
            nc.vector.tensor_scalar(oss, oss, 1.0 / DV, EPS, ALU.mult, ALU.add).then_inc(oms_done, 1)
            dve.wait_ge(oroot_done, 1)
            nc.vector.reciprocal(orstd, oroot).then_inc(orstd_done, 1)
            dve.wait_ge(orstd_done, 1)
            for t in range(TT):
                for h in range(GLA_HEADS):
                    hp, par = divmod(h, 2)
                    c0 = (t % 2) * 256 + hp * DV
                    nc.vector.scalar_tensor_tensor(o_rows[:, t, h * DV:(h + 1) * DV],
                                                   pbank[2 + 2 * par + t // 2][:, c0:c0 + DV], orstd[:, t, h:h + 1],
                                                   rg[:, t, h * DV:(h + 1) * DV], ALU.mult, ALU.mult).then_inc(y_done, 1)

            NU = PAIRS * BLOCKS
            dve.wait_ge(bias_done, 3 * NA_HEADS)
            for i in range(NU + 3):
                if i < NU:
                    pair, b = divmod(i, BLOCKS)
                    dve.wait_ge(s_done, i + 1)
                    if i >= 4:
                        dve.wait_ge(pT_done, i - 3)
                    for par in range(2):
                        tt(probs[i % 4][:, par], pbank[2 + 2 * (i % 2) + par][:, 0:NKEY], bias[:, 2 * pair + par, BIAS_VAR[b]],
                           ALU.add).then_inc(s_added, 1)
                    dve.wait_ge(s_added, 2 * (i + 1))
                    nc.vector.tensor_reduce(nmax[:, i], probs[i % 4], AX.X, ALU.max, negate=True).then_inc(nmax_done, 1)
                if i % 2 and i >= 3:
                    j = i // 2 - 1
                    dve.wait_ge(og_done, j + 1)
                    xv = x1[:, j // 2, (j % 2) * 512:(j % 2 + 1) * 512]
                    tt(xv, xv, pbank[0][:], ALU.add).then_inc(og_added, 1)
                if 1 <= i <= NU:
                    dve.wait_ge(exp_done, 2 * i)
                    nc.vector.reciprocal(rsum[:, i - 1], psum_[:, i - 1]).then_inc(rsum_done, 1)
                if i >= 3:
                    u = i - 3
                    dve.wait_ge(pv_done, u + 1)
                    dve.wait_ge(rsum_done, u + 1)
                    if u >= 2:
                        dve.wait_ge(yt_done, u - 1)
                    tt(y_rows[u % 2].rearrange("p (h d) -> p h d", h=2), pbank[1][:, 0:P].rearrange("p (h d) -> p h d", h=2),
                       rsum[:, u].unsqueeze(2).broadcast_to((P, 2, NA_DIM)), ALU.mult).then_inc(y_scaled, 1)

            n_step = [0]

            def then(ins):
                n_step[0] += 1
                ins.then_inc(route_step, 1)
                dve.wait_ge(route_step, n_step[0])

            def route(t):
                dve.wait_ge(lg_done, t + 1)
                lp = pbank[6 + t % 2][:, 0:GROUPS + EXPERTS]
                tt(lg[:, t, 0:GROUPS], lp[:, 0:GROUPS], b_r_sb[:, 0:GROUPS], ALU.add)
                then(tt(lg[:, t, 8:], lp[:, GROUPS:], b_r_sb[:, GROUPS:], ALU.add))
                then(nc.vector.max(gtop[:, t], lg[:, t, 0:8]))
                then(nc.vector.max_index(itop8[:, t], gtop[:, t], lg[:, t, 0:8]))
                then(nc.vector.tensor_copy(gidx[:, t], itop8[:, t, 0:1]))
                then(nc.vector.tensor_scalar(ghot[:, t], iota[:, 0:GROUPS], gidx[:, t], None, ALU.is_equal))
                then(tt(prod[:, t].rearrange("p (g e) -> p g e", g=GROUPS), lg[:, t, 8:].rearrange("p (g e) -> p g e", g=GROUPS),
                        ghot[:, t].unsqueeze(2).broadcast_to((P, GROUPS, PER_GROUP)), ALU.mult))
                then(nc.vector.tensor_reduce(ing[:, t], prod[:, t].rearrange("p (g e) -> p e g", g=GROUPS), AX.X, ALU.add))
                then(nc.vector.max(etop[:, t], ing[:, t]))
                then(nc.vector.max_index(eidx[:, t], etop[:, t], ing[:, t]))
                then(nc.vector.tensor_copy(eid[:, t], eidx[:, t, 0:2]))
                then(nc.vector.scalar_tensor_tensor(eid[:, t], gidx[:, t].broadcast_to((P, 2)), float(PER_GROUP), eid[:, t],
                                                    ALU.mult, ALU.add))
                nc.vector.tensor_scalar(hot[0][:, t], iota[:, 0:EXPERTS], eid[:, t, 0:1], None, ALU.is_equal)
                then(nc.vector.tensor_scalar(hot[1][:, t], iota[:, 0:EXPERTS], eid[:, t, 1:2], None, ALU.is_equal))
                tt(both_b[:, t], hot[0][:, t], hot[1][:, t], ALU.add).then_inc(both_done, 1)

            nc.vector.tensor_copy(upper_b[:], upper).then_inc(upper_ready, 1)
            nc.vector.memset(ones_b[:], 1.0).then_inc(upper_ready, 1)
            nc.vector.memset(lg[:, :, GROUPS:8], LOWEST)
            dve.wait_ge(og_added, 2 * TT)
            dve.wait_ge(g2_in, 32)
            for t in range(TT):
                dve.wait_ge(wo_done, t + 1)
                for hf in range(2):
                    cols = slice(hf * 512, (hf + 1) * 512)
                    tt(x1[:, t, cols], x1[:, t, cols], pbank[2 * (t % 2) + hf][:], ALU.add).then_inc(x1_done, 1)
                dve.wait_ge(sumsq2_done, t + 1)
                nc.vector.tensor_scalar(ssq2[:, t:t + 1], ssq2[:, t:t + 1], 1.0 / D, EPS, ALU.mult, ALU.add).then_inc(ms2_done, 1)
                dve.wait_ge(root2_done, t + 1)
                nc.vector.reciprocal(rstd2[:, t:t + 1], root2[:, t:t + 1]).then_inc(rstd2_done, 1)
                dve.wait_ge(rstd2_done, t + 1)
                if t >= 2:
                    dve.wait_ge(parts_done, t - 1)
                nc.vector.scalar_tensor_tensor(h2[t % 2], x1[:, t], rstd2[:, t:t + 1], g2b, ALU.mult, ALU.mult).then_inc(h2_done, 1)
                dve.wait_ge(h2T_done, t + 1)
                if t >= 2:
                    dve.wait_ge(lg_done, t - 1)
                nc.vector.tensor_copy(hT2[t % 2][:, 4:8].rearrange("p a b -> p (a b)"), pbank[5][:]).then_inc(h2T_vec, 1)
                if t >= 1:
                    route(t - 1)
            route(TT - 1)

            dve.wait_ge(rank_mm_done, 1)
            cum = pbank[6][:, 0:TT * EXPERTS].rearrange("p (t e) -> p t e", e=EXPERTS)
            then(nc.vector.scalar_tensor_tensor(code, cum, 1.0, both_b[:], ALU.add, ALU.mult))
            then(nc.vector.tensor_scalar(code, code, 1.0, None, ALU.subtract))

            def pick_slots(s, e, c):
                nc.vector.tensor_tensor(pick[s], iota.unsqueeze(1).broadcast_to((P, TT, SLOTS)),
                                        code[:, :, bass.ds(e, 1)].broadcast_to((P, TT, SLOTS)), ALU.is_equal).then_inc(picked, 1)

            def slots_and_weights():
                nc.vector.tensor_reduce(most, pbank[6][:, TT * EXPERTS:(TT + 1) * EXPERTS], AX.X, ALU.max).then_inc(most_done, 1)
                tt(gexp, lg[:, :, 0:GROUPS], gtop[:, :, 0:1].broadcast_to((P, TT, GROUPS)), ALU.subtract).then_inc(gdiff_done, 1)
                tt(ediff, etop[:, :, 1:2], etop[:, :, 0:1], ALU.subtract).then_inc(ediff_done, 1)
                for k in range(2):
                    then(tt(prod, hot[k], cum, ALU.mult))
                    then(nc.vector.tensor_reduce(rank[:, :, k:k + 1], prod, AX.X, ALU.add))
                then(nc.vector.scalar_tensor_tensor(slotf, eid, float(SLOTS), rank, ALU.mult, ALU.add))
                nc.vector.tensor_copy(slot, slotf).then_inc(slots_done, 1)
                dve.wait_ge(gexp_done, 1)
                then(nc.vector.tensor_reduce(gsum, gexp, AX.X, ALU.add))
                dve.wait_ge(eexp_done, 1)
                then(nc.vector.tensor_scalar(eden, eexp, 1.0, None, ALU.add))
                then(tt(eden, eden, gsum, ALU.mult))
                then(nc.vector.reciprocal(comb[:, :, 0:1], eden))
                then(tt(comb[:, :, 1:2], comb[:, :, 0:1], eexp, ALU.mult))

            def rows_T_evict(s, c):
                dve.wait_ge(xt_done, c + 1)
                nc.vector.tensor_copy(xT.rearrange("p k t -> p (k t)"), pbank[3][:]).then_inc(xt_evicted, 1)

            def hidden(s, c):
                dve.wait_ge(sil_done, c + 1)
                tt(hid[s], pbank[s][:, 256:512], hid[s], ALU.mult).then_inc(hid_done, 1)

            def y_evict(s, c, stored):
                dve.wait_ge(d_done, c + 1)
                if stored is not None:
                    dve.wait_ge(y_stored[s], 32 * stored)
                nc.vector.tensor_copy(y_sb[s], pbank[5 + s][:]).then_inc(y_evicted, 1)

            pick_slots(0, 0, 0)
            pick_slots(1, 1, 1)
            rows_T_evict(0, 0)
            slots_and_weights()
            hidden(0, 0)
            rows_T_evict(1, 1)
            for e in range(1, 1 + RING):
                pick_slots((e + 1) % RING, e + 1, e + 1)
                hidden(e % RING, e)
                rows_T_evict((e + 1) % RING, e + 1)
                y_evict((e - 1) % RING, e - 1, None)
            with dve.Fori(1, (EXPERTS - 2) // RING) as i:
                for j in range(RING):
                    e = RING * i + 1 + j
                    pick_slots((2 + j) % RING, e + 1, e + 1)
                    hidden((1 + j) % RING, e)
                    rows_T_evict((2 + j) % RING, e + 1)
                    y_evict(j, e - 1, i)
            last = EXPERTS - 1
            hidden(last % RING, last)
            for e in (last - 1, last):
                y_evict(e % RING, e, e // RING)

            dve.wait_ge(most_done, 1)
            general = dve.value_load(most[0:1, 0:1], min_val=0, max_val=T)
            with dve.If(general > limit):
                nc.vector.tensor_copy(ident_b, ident).then_inc(a_ident, 1)
                dve.wait_ge(d_done, EXPERTS)
                for t in range(TT):
                    nc.vector.tensor_scalar(g_cw[:, t], hot[0][:, t], comb[:, t, 0:1], None, ALU.mult).then_inc(a_cw, 1)
                    dve.wait_ge(a_cw, 2 * t + 1)
                    nc.vector.scalar_tensor_tensor(g_cw[:, t], hot[1][:, t], comb[:, t, 1:2], g_cw[:, t], ALU.mult,
                                                   ALU.add).then_inc(a_cw, 1)
                nc.vector.tensor_copy(x2, x1).then_inc(a_acc, 1)
                dve.wait_ge(a_cw, 2 * TT)
                with dve.Fori(0, EXPERTS) as e:
                    dve.wait_ge(a_acc, 2 * TT * e + 1)
                    nc.vector.tensor_copy(g_col, g_cw[:, :, bass.ds(e, 1)]).then_inc(a_col, 1)
                    dve.wait_ge(a_col, e + 1)
                    for t in range(TT):
                        c = TT * e + t
                        dve.wait_ge(a_sil, c + 1)
                        tt(g_hid, pbank[2][:], g_sil, ALU.mult).then_inc(a_hid, 1)
                        dve.wait_ge(a_d, c + 1)
                        for hf in range(2):
                            acc = x2[:, t, hf * 512:(hf + 1) * 512]
                            nc.vector.scalar_tensor_tensor(acc, pbank[4 + hf][:], g_col[:, t], acc, ALU.mult,
                                                           ALU.add).then_inc(a_acc, 1)
                dve.wait_ge(a_acc, 2 * TT * EXPERTS + 1)
                for t in range(TT):
                    nc.vector.tensor_copy(x2[:, t, 0:1], x2[:, t, 0:1]).then_inc(x2_done, 1)
            with dve.If(general < limit + 1):
                for t in range(TT):
                    dve.wait_ge(gathered[t], 32)
                    nc.vector.scalar_tensor_tensor(x2[:, t], got[t][0], comb[:, t, 0:1], x1[:, t], ALU.mult,
                                                   ALU.add).then_inc(x2_half, 1)
                    dve.wait_ge(x2_half, t + 1)
                    nc.vector.scalar_tensor_tensor(x2[:, t], got[t][1], comb[:, t, 1:2], x2[:, t], ALU.mult,
                                                   ALU.add).then_inc(x2_done, 1)
            dve.wait_ge(gf_in, 16)
            for t in range(TT):
                dve.wait_ge(sumsq3_done, t + 1)
                nc.vector.tensor_scalar(ssq3[:, t:t + 1], ssq3[:, t:t + 1], 1.0 / D, EPS, ALU.mult, ALU.add).then_inc(ms3_done, 1)
                dve.wait_ge(root3_done, t + 1)
                nc.vector.reciprocal(rstd3[:, t:t + 1], root3[:, t:t + 1]).then_inc(rstd3_done, 1)
                dve.wait_ge(rstd3_done, t + 1)
                nc.vector.scalar_tensor_tensor(res[:, t], x2[:, t], rstd3[:, t:t + 1], gfb, ALU.mult, ALU.mult).then_inc(res_done, 1)

        @block.gpsimd
        def _(pool):
            for t in range(1, TT, 2):
                pool.wait_ge(rstd_done, t + 1)
                nc.gpsimd.tensor_scalar(xs[:, t], x1[:, t], rstd[:, t:t + 1], None, ALU.mult).then_inc(xs_pool, 1)
            pool.wait_ge(rpb_in, 16 * NA_HEADS)
            pool.wait_ge(mask_in, 16)
            for h in range(NA_HEADS):
                for v in range(3):
                    u0 = WIN_W - v * WIN_W // 2
                    first = rpb_run[:, h, RPB_RUN - 1 - u0:RPB_RUN - u0]
                    run = bass.AP(first.tensor, first.offset, [first.ap[0], [-1, KEY_W], [-RPB_W, ROWS]])
                    nc.gpsimd.tensor_tensor(bias[:, h, v].rearrange("p (j r) -> p j r", r=ROWS), run,
                                            mask[:, v].rearrange("p (j r) -> p j r", r=ROWS), ALU.add).then_inc(bias_done, 1)
            pool.wait_ge(bias_done, 3 * NA_HEADS)
            pool.wait_ge(e12_done, 2)
            pool.wait_ge(unit_evicted, 5)

            def per_dir(v):
                return v.rearrange("p (d m) t -> p d (m t)", d=2)

            keys = gk.rearrange("p m t -> p (m t)").unsqueeze(1).broadcast_to((P, 2, HP * T))
            nc.gpsimd.tensor_tensor(per_dir(k_rel), per_dir(gz), keys, ALU.mult).then_inc(k_rel_done, 1)
            pool.wait_ge(e3_done, 1)
            nc.gpsimd.tensor_tensor(per_dir(k_dec), per_dir(gE), keys, ALU.mult).then_inc(k_dec_done, 1)
            pool.wait_ge(q_exp_done, 1)
            pool.wait_ge(k_dec_done, 1)
            nc.gpsimd.memset(st, 0.0).then_inc(st_zero, 1)

            for t in range(TT):
                pool.wait_ge(hi_done, t + 1)
                pool.wait_ge(h2T_done, t + 1)
                nc.gpsimd.tensor_tensor(h2_by_chunk(t), h2_by_chunk(t), h2_part[t][0], ALU.subtract).then_inc(rest_done, 1)
                pool.wait_ge(mid_done, t + 1)
                nc.gpsimd.tensor_tensor(h2_part[t][2], h2_by_chunk(t), h2_part[t][1], ALU.subtract).then_inc(parts_done, 1)

            def rows_store(e, c, s):
                pool.wait_ge(y_evicted, c + 1)
                for half in range(2):
                    pool.dma_start(rows_out_d[e, half], y_sb[s][64 * half:64 * half + 64]).then_inc(y_stored[s], 16)

            with pool.Fori(0, EXPERTS // RING) as i:
                for j in range(RING):
                    rows_store(RING * i + j, RING * i + j, j)
            for e in range(EXPERTS // RING * RING, EXPERTS):
                rows_store(e, e, e % RING)
            pool.wait_ge(slots_done, 1)
            for s in range(RING):
                pool.wait_ge(y_stored[s], 32 * len(range(s, EXPERTS, RING)))
            pool.wait_ge(most_done, 1)
            general = pool.value_load(most[0:1, 0:1], min_val=0, max_val=T)
            with pool.If(general < limit + 1):
                for t in range(TT):
                    for k in range(2):
                        nc.gpsimd.indirect_dma_start(got[t][k], None, rows_out,
                                                     bass.IndirectOffsetOnAxis(ap=slot[:, t, k:k + 1], axis=0)
                                                     ).then_inc(gathered[t], 16)


def constants():
    import numpy as np
    c = np.zeros((P, 384), np.float32)
    c[:, 0:128] = np.eye(P)
    c[:, 128:256] = np.triu(np.ones((P, P)), 1)
    j, i = np.meshgrid(np.arange(P) % CHUNK, np.arange(CHUNK), indexing="ij")
    c[:, 256:320] = j <= i
    c[:, 320:384] = np.arange(SLOTS)
    mask = np.full((P, 3, KEY_W, ROWS), NEG, np.float32)
    for var, b in enumerate((0, 1, BLOCKS - 1)):
        for wl in range(BLK_W):
            w = b * BLK_W + wl
            s = min(max(w - WIN_W // 2, 0), GRID_W - WIN_W) - KEY_START[b]
            mask[wl * ROWS:(wl + 1) * ROWS, var, s:s + WIN_W] = 0
    scan = np.ones((P, T), np.float32)
    scan[:, ::CHUNK] = 0
    return c, mask.reshape(P, -1), scan


def kernel(**inputs):
    import numpy as np
    import concourse.bacc as bacc
    from concourse.bass_utils import run_bass_kernel_spmd as run

    nc = bacc.Bacc("TRN2", target_bir_lowering=False, num_devices=1)
    a = {k: np.asarray(v) for k, v in inputs.items()}
    w_g2 = np.zeros((2 * RANK, 512), np.float32)
    w_g2[0:RANK, 0:256] = a["w_g2_f"][0]
    w_g2[RANK:, 256:512] = a["w_g2_b"][0]
    c_small, c_mask, c_scan = constants()
    ins = {
        "x": a["x"],
        "rpb": np.pad(a["rpb"][0, :, ::-1, ::-1].reshape(-1), (RPB_PAD, 64)),
        "w_in": a["w_in"],
        "w_g2": np.tile(w_g2, (4, 1)),
        "b_g": np.concatenate([a["b_g_f"][0], a["b_g_b"][0]]).reshape(4, P).T,
        "gla_g": a["gla_norm_g"],
        "g_mix": a["norm_mix_g"][0].reshape(KC, P).T,
        "w_out": a["w_out"],
        "g_ffn": a["norm_ffn_g"],
        "w_r": np.concatenate([a["w_grp"][0], a["w_exp"][0]], axis=1).reshape(KC, P, -1).transpose(1, 0, 2),
        "b_r": np.concatenate([a["b_grp"], a["b_exp"]], axis=1),
        "w_gate": a["w_gate"], "w_up": a["w_up"], "w_down": a["w_down"],
        "g_fin": a["final_norm_g"].reshape(1, -1),
        "c_small": c_small, "c_mask": c_mask, "c_scan": c_scan,
    }
    arrays, args = {}, []
    for name, v in ins.items():
        v = np.ascontiguousarray(v)
        arrays["in_" + name] = v
        args.append(nc.dram_tensor("in_" + name, v.shape, mybir.dt.from_np(v.dtype), kind="ExternalInput").ap())
    args.append(nc.dram_tensor("out0", (1, T, D), F32, kind="ExternalOutput").ap())
    mixer_and_moe(nc, *args)
    return run(nc, [arrays], core_ids=[0]).results[0]["out0"]
```

```python
from contextlib import ExitStack

import concourse.bass as bass
from concourse import mybir

ALU = mybir.AluOpType
ACT = mybir.ActivationFunctionType
AX = mybir.AxisListType
F32 = mybir.dt.float32
BF16 = mybir.dt.bfloat16
U32 = mybir.dt.uint32
I32 = mybir.dt.int32

P = 128
D = 1024
T = 512
TT = T // P
KC = D // P
GRID_W = 64
ROWS = T // GRID_W
WIN_W = 16
NA_HEADS, NA_DIM = 8, 64
PAIRS = NA_HEADS // 2
BLK_W = P // ROWS
BLOCKS = GRID_W // BLK_W
KEY_W = 2 * BLK_W
NKEY = KEY_W * ROWS
KEY_START = [min(max(b * BLK_W - WIN_W // 2, 0), GRID_W - KEY_W) for b in range(BLOCKS)]
BIAS_VAR = [0, 1, 1, 2]
RPB_H, RPB_W = 2 * ROWS - 1, 2 * WIN_W - 1
RPB_RUN = RPB_W * (ROWS - 1) + KEY_W + WIN_W
RPB_PAD = WIN_W
GLA_HEADS, DK, DV = 4, 64, 128
CHUNK = 64
NCH = T // CHUNK
HP = GLA_HEADS // 2
RANK = 16
GROUPS, PER_GROUP = 4, 8
EXPERTS = GROUPS * PER_GROUP
FF = 512
FC = FF // P
SLOTS = 64
RING = 3
EPS = 1e-6
NEG = -1e30
LOWEST = -3e38
UNIT_BANKS = 2
V_BANKS = [6, 7, 0, 1]
GLA_BANK = [0] * 6 + [2, 3]
POOL_TILES = 2

IN_NQ, IN_NK, IN_NV, IN_GQK, IN_GV, IN_GR, IN_LR = 0, 512, 1024, 1536, 2048, 2560, 3072


def words(kib):
    return int(kib * 256)


def mixer_and_moe(nc, x, rpb, w_in, w_g2, b_g, gla_g, g_mix, w_out, g_ffn, g_ffn_T, w_r, b_r, w_gate, w_up, w_down, g_fin,
                  c_small, c_mask, c_scan, out, limit=SLOTS):
    with ExitStack() as ctx:
        arena = ctx.enter_context(nc.sbuf_tensor("arena", [P, words(207)], F32))
        pbank = [ctx.enter_context(nc.psum_tensor(f"bank{i}", [P, 512], F32)) for i in range(8)]
        upper_b = ctx.enter_context(nc.sbuf_tensor("upper_b", [P, P], BF16))
        ones_b = ctx.enter_context(nc.sbuf_tensor("ones_b", [P, P], BF16))
        both_b = ctx.enter_context(nc.sbuf_tensor("both_b", [P, TT, EXPERTS], BF16))
        rows_out = nc.dram_tensor("rows_out", [EXPERTS * SLOTS, D], F32).ap()

        def sem(name):
            return ctx.enter_context(nc.semaphore(name))

        def at(kib, *shape):
            n = 1
            for s in shape:
                n *= s
            v = arena[:, words(kib):words(kib) + n]
            if len(shape) == 2:
                return v.rearrange("p (a b) -> p a b", b=shape[1])
            if len(shape) == 3:
                return v.rearrange("p (a b c) -> p a b c", b=shape[1], c=shape[2])
            return v

        hT = at(0, KC, T)
        w_buf = [at(16, KC, 512), at(32, KC, 512)]
        bias = at(48, NA_HEADS, 3, NKEY)
        na_v = at(72, 2 * BLOCKS - 1, 512)
        gz = at(78, 4, T)
        r_exp = at(78, TT, 512)
        gd = at(86, 4, T)
        na_q = at(86, PAIRS, T)
        gE = at(94, 4, T)
        na_k = at(94, PAIRS, T)
        xs = at(102, TT, D)
        gb = at(102, 4, T)
        k_rows = at(102, 4, TT, P)
        q_rel = at(110, 4, T)
        rpb_run = at(118, NA_HEADS, RPB_RUN)
        k_rel = at(118, 4, T)
        o_junk = at(118, 16, DV)
        vT = at(110, PAIRS, T)
        k_dec = at(126, 4, T)
        o_rows = at(126, TT, 512)
        w_og = [at(102, KC // 4, D), at(179, KC // 4, D)]
        w_on = at(112, KC // 2, D)
        q_exp = at(134, 4, T)
        scan_keep = at(140, T)
        probs = [at(134 + 2 * i, 2, NKEY) for i in range(4)]
        hT2 = [at(136 + 4 * i, KC, P) for i in range(2)]
        h2 = [at(128 + 4 * i, D) for i in range(2)]
        lr = at(142, T)
        probsT = [at(142, 4, P), at(195, 4, P)]
        x1 = at(144, TT, D)
        gla_gb = at(163, DV)
        s_prev = at(163, 4, NCH, DV)
        yT = at(163, KC, T)
        gv = at(179, TT, 512)
        rg = at(187, TT, 512)
        junk = at(179, TT, D)
        h2_part = [[at(171 + 6 * t + 2 * i, D // 2).bitcast(BF16).rearrange("p (k q) -> p k q", k=KC) for i in range(3)]
                   for t in range(TT)]
        junk2 = [at(171 + 6 * t, D) for t in range(TT)]
        gq = at(195, HP, T)
        gk = at(199, HP, T)
        st = at(195, 16, P)
        mask = at(203, 3, NKEY)
        y_rows = [at(203 + 0.5 * i, P) for i in range(2)]
        w_lr = at(206, KC, 2 * RANK)
        g2b = at(199, D)
        gfb = at(128, D)
        wr_sb = at(197, KC, GROUPS + EXPERTS)

        small = at(160, 768)
        pos = [0]

        def take(n):
            v = small[:, pos[0]:pos[0] + n]
            pos[0] += n
            return v

        ident, upper, causal, iota = take(128), take(128), take(64), take(SLOTS)
        gmix, bg = take(8), take(4)
        b_r_sb = take(GROUPS + EXPERTS)
        gffn = take(KC)
        ssq, root, rstd = take(TT), take(TT), take(TT)
        dec = take(4 * NCH).rearrange("p (m n) -> p m n", m=4)
        oss, oroot, orstd = (take(16).rearrange("p (t h) -> p t h", t=TT) for _ in range(3))
        nmax, psum_, rsum = (take(32).rearrange("p (u h) -> p u h", h=2) for _ in range(3))
        ssq2, root2, rstd2 = take(TT), take(TT), take(TT)
        ssq3, root3, rstd3 = take(TT), take(TT), take(TT)
        comb = take(2 * TT).rearrange("p (t k) -> p t k", k=2)
        slot = take(2 * TT).rearrange("p (t k) -> p t k", k=2).bitcast(U32)
        most = take(1).bitcast(I32)
        assert pos[0] <= 768

        rt = at(204, 768)
        rpos = [0]

        def rtake(*shape):
            n = 1
            for s in shape:
                n *= s
            v = rt[:, rpos[0]:rpos[0] + n]
            rpos[0] += n
            assert rpos[0] <= 768
            if len(shape) == 2:
                v = v.rearrange("p (a b) -> p a b", b=shape[1])
            return v

        lg = rtake(TT, 8 + EXPERTS)
        gtop, itop8, ing = rtake(TT, 8), rtake(TT, 8).bitcast(U32), rtake(TT, 8)
        gidx, ghot, gexp = rtake(TT, 1), rtake(TT, GROUPS), rtake(TT, GROUPS)
        etop, eidx = rtake(TT, 8), rtake(TT, 8).bitcast(U32)
        gsum, ediff, eexp, eden = rtake(TT, 1), rtake(TT, 1), rtake(TT, 1), rtake(TT, 1)
        eid = rtake(TT, 2)
        hot = [rtake(TT, EXPERTS), rtake(TT, EXPERTS)]
        rank, slotf = rtake(TT, 2), rtake(TT, 2)
        prod = at(203, TT, EXPERTS)
        code = at(203.5, TT, EXPERTS)

        xT = at(163, KC, SLOTS)
        hidT = at(165, 2, 2, SLOTS)
        hid = [at(166 + i, 256) for i in range(RING)]
        y_sb = [at(195 + 2 * i, 512) for i in range(RING)]
        pick = [at(201 + 0.5 * i, TT * SLOTS // 2).bitcast(BF16).rearrange("p (t s) -> p t s", t=TT)
                for i in range(RING)]
        wg_sb = [at(48 * i, 2, KC, FF) for i in range(RING)]
        wd_sb = [at(48 * i + 32, FC, D) for i in range(RING)]
        got = [[at(4 * (2 * t + k), D) for k in range(2)] for t in range(TT)]
        res = at(32, TT, D)
        x2 = at(96, TT, D)
        junk3 = at(112, TT, D)

        ident_b = at(169, P // 2).bitcast(BF16)
        g_hT = [at(64 + 4 * t, KC, P) for t in range(TT)]
        g_sil = at(132, FF)
        g_hid = at(134, FF)
        g_hidT = at(136, FC, P)
        g_cw = at(138, TT, EXPERTS)
        g_col = at(139, TT, 1)

        x_in_sb = [sem(f"x_in_sb{t}") for t in range(TT)]
        late_in = sem("late_in")
        consts_in, bias_in = sem("consts_in"), sem("bias_in")
        win_in = [sem(f"win_in{g}") for g in range(7)]
        og_done, og_added, wog_in, router_ready = sem("og_done"), sem("og_added"), sem("wog_in"), sem("router_ready")
        sumsq_done, ms_done, root_done, rstd_done = sem("sumsq_done"), sem("ms_done"), sem("root_done"), sem("rstd_done")
        xs_done, small_in = sem("xs_done"), sem("small_in")
        xT_done, hT_act, hT_vec = sem("xT_done"), sem("hT_act"), sem("hT_vec")
        unit_done, unit_evicted = sem("unit_done"), sem("unit_evicted")
        gates_done, z_done, abs_done, expa_done = sem("gates_done"), sem("z_done"), sem("abs_done"), sem("expa_done")
        softp_done, g_done, scan_done, d1_done = sem("softp_done"), sem("g_done"), sem("scan_done"), sem("d1_done")
        e12_done, q_rel_done, k_rel_done, d3_done = sem("e12_done"), sem("q_rel_done"), sem("k_rel_done"), sem("d3_done")
        e3_done, dec_done, e4_done = sem("e3_done"), sem("dec_done"), sem("e4_done")
        k_dec_done, q_exp_done = sem("k_dec_done"), sem("q_exp_done")
        r_step, rg_done, bias_done = sem("r_step"), sem("rg_done"), sem("bias_done")
        kT_done, k_rows_done, scores_done = sem("kT_done"), sem("k_rows_done"), sem("scores_done")
        st_zero, sb_copied, st_done = sem("st_zero"), sem("sb_copied"), sem("st_done")
        state_done, state_used = sem("state_done"), sem("state_used")
        o_done, oss_done, oms_done, oroot_done = sem("o_done"), sem("oss_done"), sem("oms_done"), sem("oroot_done")
        orstd_done, y_done, yg_done, yg_evicted = sem("orstd_done"), sem("y_done"), sem("yg_done"), sem("yg_evicted")
        v_done, v_act, v_vec = sem("v_done"), sem("v_act"), sem("v_vec")
        s_done, s_added, nmax_done = sem("s_done"), sem("s_added"), sem("nmax_done")
        exp_done, rsum_done, y_scaled, yt_done = sem("exp_done"), sem("rsum_done"), sem("y_scaled"), sem("yt_done")
        pT_done, pT_evicted, pv_done, yn_evicted = sem("pT_done"), sem("pT_evicted"), sem("pv_done"), sem("yn_evicted")
        wout_in, g2_in, gf_in = sem("wout_in"), sem("g2_in"), sem("gf_in")
        wo_done, x1_done, sumsq2_done, ms2_done = sem("wo_done"), sem("x1_done"), sem("sumsq2_done"), sem("ms2_done")
        root2_done, rstd2_done, h2_done = sem("root2_done"), sem("rstd2_done"), sem("h2_done")
        xr_done, res_pool = sem("xr_done"), sem("res_pool")
        lg_evicted, gu_half_done = sem("lg_evicted"), sem("gu_half_done")
        hi_done, rest_done, mid_done, parts_done = sem("hi_done"), sem("rest_done"), sem("mid_done"), sem("parts_done")
        h2T_done, h2T_act, h2T_vec, lg_done = sem("h2T_done"), sem("h2T_act"), sem("h2T_vec"), sem("lg_done")
        route_step, cdiff_done, cexp_done = sem("route_step"), sem("cdiff_done"), sem("cexp_done")
        picked = sem("picked")
        both_done, rank_mm_done, slots_done = sem("both_done"), sem("rank_mm_done"), sem("slots_done")
        most_done = sem("most_done")
        wgu_in = [[sem(f"wgu_in{i}_{part}") for part in range(2)] for i in range(RING)]
        wd_in = [sem(f"wd_in{i}") for i in range(RING)]
        y_stored = [sem(f"y_stored{i}") for i in range(RING)]
        xt_done, xt_evicted, gu_done, sil_done = sem("xt_done"), sem("xt_evicted"), sem("gu_done"), sem("sil_done")
        hid_done, ht_done, ht_evicted, d_done, y_evicted = (sem("hid_done"), sem("ht_done"), sem("ht_evicted"),
                                                            sem("d_done"), sem("y_evicted"))
        gathered = [[sem(f"gathered{t}_{k}") for k in range(2)] for t in range(TT)]
        x2_half, x2_done, sumsq3_done, ms3_done = sem("x2_half"), sem("x2_done"), sem("sumsq3_done"), sem("ms3_done")
        root3_done, rstd3_done, res_done, out_stored = sem("root3_done"), sem("rstd3_done"), sem("res_done"), sem("out_stored")
        a_col = sem("a_col")
        a_T, a_copied, a_w, a_gu, a_sil, a_hid, a_d, a_acc, a_cw = (
            sem("a_T"), sem("a_copied"), sem("a_w"), sem("a_gu"), sem("a_sil"), sem("a_hid"), sem("a_d"), sem("a_acc"),
            sem("a_cw"))

        x_d = x.rearrange("b (t p) d -> (b t) p d", p=P)
        out_d = out.rearrange("b (t p) d -> (b t) p d", p=P)
        win_d = w_in.rearrange("l (k p) n -> (l p) k n", p=P)
        wout_d = w_out.rearrange("l (k p) n -> (l p) k n", p=P)
        wg_d = w_gate.rearrange("l e (p k) f -> (l e) p k f", k=KC)
        wu_d = w_up.rearrange("l e (p k) f -> (l e) p k f", k=KC)
        wd_d = w_down.rearrange("l e (k p) d -> (l e) p k d", p=P)
        rows_out_d = rows_out.rearrange("(e t) (h d) -> e h t d", t=SLOTS, h=2)

        def h2_by_chunk(t):
            return h2[t % 2].rearrange("p (q k) -> p k q", k=KC)

        block = ctx.enter_context(nc.Block())

        groups = [("lr", None, IN_LR), ("gqk", 0, IN_GQK), ("gv", 1, IN_GV), ("gr", 0, IN_GR),
                  ("nq", 1, IN_NQ), ("nk", 0, IN_NK), ("nv", 1, IN_NV)]

        @block.sync
        def _(sp):
            for t in range(TT):
                sp.dma_start(x1[:, t], x_d[t]).then_inc(x_in_sb[t], 16)
                if t == 0:
                    sp.dma_start(small[:, 0:384], c_small).then_inc(small_in, 16)
            sp.dma_start(gmix, g_mix).then_inc(consts_in, 16)
            sp.dma_start(bg, b_g).then_inc(consts_in, 16)
            sp.dma_start(w_lr, win_d[:, :, IN_LR:IN_LR + 2 * RANK]).then_inc(win_in[0], 16)
            sp.dma_start(gE[:, 0], w_g2).then_inc(consts_in, 16)
            for g in (1, 2):
                sp.dma_start(w_buf[groups[g][1]], win_d[:, :, groups[g][2]:groups[g][2] + 512]).then_inc(win_in[g], 16)
            for h in range(NA_HEADS):
                run = bass.AP(rpb.tensor, h * RPB_H * RPB_W, [[1, BLK_W], [RPB_W, ROWS], [1, RPB_RUN]])
                sp.dma_start(rpb_run[:, h], run).then_inc(bias_in, 16)
            sp.dma_start(mask.rearrange("p a b -> p (a b)"), c_mask).then_inc(bias_in, 16)
            sp.dma_start(scan_keep, c_scan).then_inc(late_in, 16)
            sp.dma_start(gla_gb, gla_g.broadcast_to((P, DV))).then_inc(late_in, 16)
            sp.dma_start(b_r_sb, b_r.broadcast_to((P, GROUPS + EXPERTS))).then_inc(late_in, 16)
            for g in range(3, 7):
                sp.wait_ge(unit_done, 1 + 4 * (g - 2))
                sp.dma_start(w_buf[groups[g][1]], win_d[:, :, groups[g][2]:groups[g][2] + 512]).then_inc(win_in[g], 16)
            sp.wait_ge(state_done, NCH - 1)
            sp.dma_start(w_og[0], wout_d[:, KC // 2:3 * KC // 4]).then_inc(wog_in, 16)
            sp.wait_ge(o_done, TT)
            sp.dma_start(w_og[1], wout_d[:, 3 * KC // 4:]).then_inc(wog_in, 16)
            sp.dma_start(g2b, g_ffn.broadcast_to((P, D))).then_inc(g2_in, 16)
            sp.dma_start(wr_sb, w_r).then_inc(g2_in, 16)
            sp.dma_start(gffn, g_ffn_T).then_inc(g2_in, 16)

            def load_rows(src, dst, s, part):
                ks = slice(part * KC // 2, (part + 1) * KC // 2)
                sp.dma_start(dst[:, ks], src[:, ks]).then_inc(wgu_in[s][part], 16)

            def load_g(e, s):
                for part in range(2):
                    load_rows(wg_d[e], wg_sb[s][:, 0], s, part)

            def load_u(e, s):
                for part in range(2):
                    load_rows(wu_d[e], wg_sb[s][:, 1], s, part)

            def load_d(e, s):
                sp.dma_start(wd_sb[s], wd_d[e]).then_inc(wd_in[s], 16)

            sp.wait_ge(unit_done, 25)
            load_g(0, 0)
            load_u(0, 0)
            load_d(0, 0)
            sp.wait_ge(yg_done, GLA_HEADS)
            sp.wait_ge(v_done, 2 * BLOCKS - 1)
            sp.dma_start(w_on, wout_d[:, 0:KC // 2]).then_inc(wout_in, 16)
            sp.wait_ge(pv_done, 4 * PAIRS)
            sp.wait_ge(og_done, 2 * TT)
            load_g(1, 1)
            load_u(1, 1)
            load_d(1, 1)
            load_g(2, 2)
            sp.wait_ge(wo_done, 2 * TT)
            load_u(2, 2)
            sp.wait_ge(lg_done, TT)
            sp.wait_ge(parts_done, TT + 1)
            load_d(2, 2)

            def step(e, c, s):
                for part in range(2):
                    sp.wait_ge(gu_done if part else gu_half_done, c - 2)
                    load_rows(wg_d[e], wg_sb[s][:, 0], s, part)
                    load_rows(wu_d[e], wg_sb[s][:, 1], s, part)
                sp.wait_ge(d_done, c - 2)
                load_d(e, s)

            with sp.Fori(1, EXPERTS // RING) as i:
                for j in range(RING):
                    step(RING * i + j, RING * i + j, j)
            for e in range(EXPERTS // RING * RING, EXPERTS):
                step(e, e, e % RING)

            sp.wait_ge(d_done, EXPERTS - 2)
            sp.dma_start(gfb, g_fin.broadcast_to((P, D))).then_inc(gf_in, 16)
            sp.wait_ge(most_done, 1)
            general = sp.value_load(most[0:1, 0:1], min_val=0, max_val=T)
            with sp.If(general > limit):
                sp.wait_ge(d_done, EXPERTS)
                with sp.Fori(0, EXPERTS) as e:
                    sp.wait_ge(a_acc, TT * 2 * e + 1)
                    sp.dma_start(wg_sb[0][:, 0], wg_d[e]).then_inc(a_w, 16)
                    sp.dma_start(wg_sb[0][:, 1], wu_d[e]).then_inc(a_w, 16)
                    sp.dma_start(wd_sb[0], wd_d[e]).then_inc(a_w, 16)

            for t in range(TT):
                if t < POOL_TILES:
                    sp.wait_ge(res_pool, t + 1)
                else:
                    sp.wait_ge(res_done, t + 1 - POOL_TILES)
                sp.dma_start(out_d[t], res[:, t]).then_inc(out_stored, 16)
            sp.wait_ge(out_stored, 16 * TT)

        @block.tensor
        def _(pe):
            pe.wait_ge(small_in, 16)
            for t in range(TT):
                pe.wait_ge(xs_done, t + 1)
                for k in range(KC):
                    m = pe.transpose(pbank[k][:, t * P:(t + 1) * P], xs[:, t, k * P:(k + 1) * P], ident)
                    if t == TT - 1:
                        m.then_inc(xT_done, 1)
            count = [0]

            def unit(lhs, rhs, between=None):
                n = count[0]
                if n >= UNIT_BANKS:
                    pe.wait_ge(unit_evicted, n - UNIT_BANKS + 1)
                for k in range(KC):
                    m = pe.matmul(pbank[n % UNIT_BANKS][:], lhs(k), rhs(k), start=(k == 0), stop=(k == KC - 1))
                    if k == KC - 1:
                        m.then_inc(unit_done, 1)
                    if between is not None:
                        between(k)
                count[0] += 1

            def weights_stationary(g, m, between=None):
                w = w_buf[groups[g][1]]
                unit(lambda k: w[:, k, m * P:(m + 1) * P], lambda k: hT[:, k], between)

            def tokens_stationary(g, t):
                w = w_buf[groups[g][1]]
                unit(lambda k: hT[:, k, t * P:(t + 1) * P], lambda k: w[:, k])

            pe.wait_ge(win_in[0], 16)
            for k in range(KC):
                j = 32 * (k % 4)
                pe.wait_ge(hT_act if k % 2 else hT_vec, k // 2 + 1)
                m = pe.matmul(pbank[0][j:j + 32], w_lr[:, k], hT[:, k], start=(k < 4), stop=(k >= 4))
            m.then_inc(unit_done, 1)
            count[0] += 1
            pe.wait_ge(win_in[1], 16)
            weights_stationary(1, 0)
            pe.wait_ge(unit_evicted, 1)
            pe.wait_ge(consts_in, 48)
            for m in range(4):
                pe.matmul(pbank[2 + m][:], gE[:, 0, m * P:(m + 1) * P], lr,
                          start=True, stop=True).then_inc(gates_done, 1)
            for m in range(1, 4):
                weights_stationary(1, m)
            for g in (2, 3):
                pe.wait_ge(win_in[g], 16)
                for t in range(TT):
                    tokens_stationary(g, t)

            pe.wait_ge(k_dec_done, 1)
            for m in range(4):
                if m >= 2:
                    pe.wait_ge(k_rows_done, m - 1)
                for t in range(TT):
                    mm = pe.transpose(pbank[6 + m % 2][:, t * P:(t + 1) * P], k_dec[:, m, t * P:(t + 1) * P], ident)
                mm.then_inc(kT_done, 1)
            pe.wait_ge(q_rel_done, 1)
            pe.wait_ge(k_rel_done, 1)
            def scores(k):
                d = k // (KC // 2)
                for n in range(k * 2 % NCH, k * 2 % NCH + 2):
                    for hp in range(HP):
                        for par in range(2):
                            rows = slice(64 * par, 64 * par + 64)
                            c = (hp * (NCH // 2) + n // 2) * CHUNK
                            mm = pe.matmul(pbank[2 + 2 * d + par][64 * (n % 2):64 * (n % 2) + 64, c:c + CHUNK],
                                           k_rel[rows, 2 * d + hp, n * CHUNK:(n + 1) * CHUNK],
                                           q_rel[rows, 2 * d + hp, n * CHUNK:(n + 1) * CHUNK], start=True, stop=True)
                if k % (KC // 2) == KC // 2 - 1:
                    mm.then_inc(scores_done, 1)

            pe.wait_ge(win_in[4], 16)
            for s2 in range(4):
                weights_stationary(4, s2, scores if s2 == 0 else None)
                if s2 == 0:
                    pe.wait_ge(k_rows_done, 4)
                else:
                    pe.wait_ge(state_used, 8 * s2)
                for s in (2 * s2, 2 * s2 + 1):
                    if s == NCH - 1:
                        continue
                    for d in range(2):
                        n = s if d == 0 else NCH - 1 - s
                        rows = slice(64 * (n % 2), 64 * (n % 2) + 64)
                        for hp in range(HP):
                            for par in range(2):
                                h = 2 * hp + par
                                mm = pe.matmul(
                                    pbank[6 + n % 2][64 * par:64 * par + 64, d * 256 + hp * DV:d * 256 + (hp + 1) * DV],
                                    k_rows[rows, 2 * d + hp, n // 2, par * DK:(par + 1) * DK],
                                    gv[rows, n // 2, h * DV:(h + 1) * DV], start=True, stop=True)
                    mm.then_inc(state_done, 1)
            pe.wait_ge(win_in[5], 16)
            for m in range(4):
                weights_stationary(5, m)
            pe.wait_ge(st_done, 4)
            pe.wait_ge(state_used, 28)
            pe.wait_ge(q_exp_done, 1)
            for t in range(TT):
                for hp in range(HP):
                    for par in range(2):
                        h = 2 * hp + par
                        rows = slice(64 * par, 64 * par + 64)
                        c0 = (t % 2) * 256 + hp * DV
                        bank = pbank[2 + 2 * par + t // 2]
                        pe.matmul(bank[:, c0:c0 + DV], st[:, par * 8 + hp * 4 + t], gv[:, t, h * DV:(h + 1) * DV],
                                  start=True, stop=False)
                        for c in range(2):
                            n = 2 * t + c
                            dirs = [d for d in range(2) if not (d == 0 and n == 0) and not (d == 1 and n == NCH - 1)]
                            for d in dirs:
                                mm = pe.matmul(bank[64 * c:64 * c + 64, c0:c0 + DV],
                                               q_exp[rows, 2 * d + hp, n * CHUNK:(n + 1) * CHUNK],
                                               s_prev[rows, 2 * d + hp, n], start=False, stop=(d == dirs[-1]))
                mm.then_inc(o_done, 1)
            NU = PAIRS * BLOCKS

            def na_scores(i):
                pair, b = divmod(i, BLOCKS)
                if i >= 2:
                    pe.wait_ge(s_added, 2 * (i - 1))
                for par in range(2):
                    rows = slice(64 * par, 64 * par + 64)
                    k0 = KEY_START[b] * ROWS
                    mm = pe.matmul(pbank[2 + 2 * (i % 2) + par][:, 0:NKEY], na_q[rows, pair, b * P:(b + 1) * P],
                                   na_k[rows, pair, k0:k0 + NKEY], start=True, stop=True)
                mm.then_inc(s_done, 1)

            pe.wait_ge(win_in[6], 16)
            for m in range(2):
                weights_stationary(6, m)
            pe.wait_ge(y_done, 16)
            pe.wait_ge(unit_evicted, 21)
            na_scores(0)
            na_scores(1)
            for h in range(GLA_HEADS):
                if h >= 2:
                    pe.wait_ge(yg_evicted, h - 1)
                for t in range(TT):
                    mm = pe.transpose(pbank[6 + h % 2][:, t * P:(t + 1) * P], o_rows[:, t, h * DV:(h + 1) * DV], ident)
                mm.then_inc(yg_done, 1)
            for m in range(2, 4):
                weights_stationary(6, m)
            na_scores(2)
            na_scores(3)
            pe.wait_ge(unit_evicted, 25)
            pe.wait_ge(yg_evicted, GLA_HEADS)
            for i in range(2 * BLOCKS - 1):
                if i >= 4:
                    pe.wait_ge(v_vec if i % 2 else v_act, i // 2 - 1)
                for m in range(PAIRS):
                    mm = pe.transpose(pbank[V_BANKS[i % 4]][:, m * P:(m + 1) * P], vT[:, m, i * 64:i * 64 + P], ident)
                mm.then_inc(v_done, 1)
            pe.wait_ge(v_act, BLOCKS - 1)

            def gla_share(n):
                j, part = divmod(n, 2)
                if n == 0:
                    pe.wait_ge(wog_in, 32)
                if part == 0:
                    if GLA_BANK[j]:
                        pe.wait_ge(s_added, 2 * (NU - 1))
                    elif j >= 1:
                        pe.wait_ge(og_added, j)
                t, half = divmod(j, 2)
                for k in (2 * part, 2 * part + 1):
                    mm = pe.matmul(pbank[GLA_BANK[j]][:], yT[:, KC // 2 + k, t * P:(t + 1) * P],
                                   w_og[part][:, k % 2, half * 512:(half + 1) * 512], start=(k == 0), stop=(k == KC // 2 - 1))
                if part == 1:
                    mm.then_inc(og_done, 1)

            for i in range(2, NU + 4):
                if 4 <= i < NU:
                    na_scores(i)
                if 4 <= i < NU + 2:
                    gla_share(i - 4)
                if 0 <= i - 2 < NU:
                    u = i - 2
                    pe.wait_ge(exp_done, 2 * (u + 1))
                    if u >= 1:
                        pe.wait_ge(pT_evicted, u)
                    for par in range(2):
                        for c in range(2):
                            a = 2 * par + c
                            mm = pe.transpose(pbank[6][:, a * P:(a + 1) * P],
                                              probs[u % 4][:, par, c * P:(c + 1) * P], ident)
                    mm.then_inc(pT_done, 1)
                if 0 <= i - 3 < NU:
                    u = i - 3
                    pair, b = divmod(u, BLOCKS)
                    pe.wait_ge(pT_evicted, u + 1)
                    if u == 0:
                        pe.wait_ge(v_act, BLOCKS)
                        pe.wait_ge(v_vec, BLOCKS - 1)
                    else:
                        pe.wait_ge(y_scaled, u)
                    v0 = KEY_START[b] * ROWS // 64
                    for par in range(2):
                        h = 2 * pair + par
                        for c in range(2):
                            mm = pe.matmul(pbank[1][:, par * NA_DIM:(par + 1) * NA_DIM], probsT[u % 2][:, 2 * par + c],
                                           na_v[:, v0 + 2 * c, h * NA_DIM:(h + 1) * NA_DIM], start=(c == 0), stop=(c == 1))
                    mm.then_inc(pv_done, 1)
                if i >= 4:
                    u = i - 4
                    pair, b = divmod(u, BLOCKS)
                    pe.wait_ge(y_scaled, u + 1)
                    if b == 0 and pair >= 1:
                        pe.wait_ge(yn_evicted, pair)
                    pe.transpose(pbank[7][:, b * P:(b + 1) * P], y_rows[u % 2], ident).then_inc(yt_done, 1)
                if i >= NU + 2:
                    gla_share(i - 4)

            def out_proj(t, half):
                if t >= 2:
                    pe.wait_ge(x1_done, 2 * (t - 2) + half + 1)
                for k in range(KC // 2):
                    mm = pe.matmul(pbank[2 * (t % 2) + half][:], yT[:, k, t * P:(t + 1) * P],
                                   w_on[:, k, half * 512:(half + 1) * 512], start=(k == 0), stop=(k == KC // 2 - 1))
                mm.then_inc(wo_done, 1)

            def x1_T(t):
                pe.wait_ge(x1_done, 2 * (t + 1))
                if t >= 1:
                    pe.wait_ge(h2T_act, t)
                    pe.wait_ge(h2T_vec, t)
                for k in range(KC):
                    mm = pe.transpose(pbank[4 + k // 4][:, (k % 4) * P:(k % 4 + 1) * P], x1[:, t, k * P:(k + 1) * P], ident)
                mm.then_inc(h2T_done, 1)

            def router(t):
                pe.wait_ge(h2T_act, t + 1)
                pe.wait_ge(h2T_vec, t + 1)
                if t >= 2:
                    pe.wait_ge(lg_evicted, t - 1)
                for k in range(KC):
                    mm = pe.matmul(pbank[6 + t % 2][:, 0:GROUPS + EXPERTS], hT2[t % 2][:, k], wr_sb[:, k],
                                   start=(k == 0), stop=(k == KC - 1))
                mm.then_inc(lg_done, 1)

            pe.wait_ge(yn_evicted, PAIRS)
            pe.wait_ge(wout_in, 16)
            pe.wait_ge(og_added, 6)
            def keep_clock(n):
                for _ in range(n):
                    pe.matmul(pbank[1][:, 0:P], ident, ident, start=True, stop=True)

            for t in range(2):
                if t == 1:
                    pe.wait_ge(og_added, 2 * TT)
                for half in range(2):
                    out_proj(t, half)
            x1_T(0)
            out_proj(2, 0)
            pe.wait_ge(router_ready, 3)
            router(0)
            x1_T(1)
            out_proj(2, 1)
            out_proj(3, 0)
            router(1)
            x1_T(2)
            out_proj(3, 1)
            router(2)
            keep_clock(4)
            x1_T(3)
            keep_clock(4)
            router(3)
            keep_clock(10)
            pe.wait_ge(both_done, TT)
            for t in range(TT + 1):
                for s in range(min(t + 1, TT)):
                    mm = pe.matmul(pbank[6][:, t * EXPERTS:(t + 1) * EXPERTS], (upper_b if s == t else ones_b)[:],
                                   both_b[:, s], start=(s == 0), stop=(s == min(t, TT - 1)))
            mm.then_inc(rank_mm_done, 1)
            keep_clock(5)

            def pick_rows(s, c):
                pe.wait_ge(picked, c + 1)
                for k in range(KC):
                    for t in range(TT):
                        for i in range(3):
                            mm = pe.matmul(pbank[3][:, k * SLOTS:(k + 1) * SLOTS], h2_part[t][i][:, k], pick[s][:, t],
                                           start=(t == 0 and i == 0), stop=(t == TT - 1 and i == 2))
                mm.then_inc(xt_done, 1)

            def gate_up(s, q, c):
                pe.wait_ge(xt_evicted, c + 1)
                for k in range(KC):
                    if k % (KC // 2) == 0:
                        pe.wait_ge(wgu_in[s][k // (KC // 2)], 32 * q + 32)
                    for half in range(2):
                        mm = pe.matmul(pbank[s][64 * half:64 * half + 64, :].rearrange("p (g f) -> p g f", g=2),
                                       xT[:, k], wg_sb[s][:, :, k, half * 256:(half + 1) * 256],
                                       start=(k == 0), stop=(k == KC - 1))
                    if k == KC // 2 - 1:
                        mm.then_inc(gu_half_done, 1)
                mm.then_inc(gu_done, 1)

            def hidden_T(s, c):
                pe.wait_ge(hid_done, c + 1)
                pe.nop(nofuse=True)
                for cc in range(2):
                    mm = pe.transpose(pbank[4][:, cc * P:(cc + 1) * P], hid[s][:, cc * P:(cc + 1) * P], ident)
                mm.then_inc(ht_done, 1)

            def down(s, q, c):
                pe.wait_ge(ht_evicted, c + 1)
                pe.wait_ge(wd_in[s], 16 * q + 16)
                for kc in range(FC):
                    for half in range(2):
                        mm = pe.matmul(pbank[5 + s][64 * half:64 * half + 64, :], hidT[:, kc % 2, kc // 2],
                                       wd_sb[s][:, kc, half * 512:(half + 1) * 512],
                                       start=(kc == 0), stop=(kc == FC - 1))
                mm.then_inc(d_done, 1)

            pe.wait_ge(parts_done, TT + 1)
            pick_rows(0, 0)
            with pe.Fori(0, (EXPERTS - 2) // RING) as i:
                for s in range(RING):
                    e = RING * i + s
                    gate_up(s, i, e)
                    pick_rows((s + 1) % RING, e + 1)
                    hidden_T(s, e)
                    down(s, i, e)
            for e in (EXPERTS - 2, EXPERTS - 1):
                gate_up(e % RING, e // RING, e)
                if e < EXPERTS - 1:
                    pick_rows((e + 1) % RING, e + 1)
                hidden_T(e % RING, e)
                down(e % RING, e // RING, e)

            pe.wait_ge(most_done, 1)
            general = pe.value_load(most[0:1, 0:1], min_val=0, max_val=T)
            with pe.If(general > limit):
                pe.wait_ge(a_col, 1)
                for t in range(TT):
                    for g in range(2):
                        if 2 * t + g >= 1:
                            pe.wait_ge(a_copied, 2 * t + g)
                        for k in range(4):
                            for i in range(3):
                                mm = pe.matmul(pbank[0][:, k * P:(k + 1) * P], h2_part[t][i][:, 4 * g + k], ident_b,
                                               start=(i == 0), stop=(i == 2))
                        mm.then_inc(a_T, 1)
                pe.wait_ge(a_copied, 2 * TT)
                with pe.Fori(0, EXPERTS) as e:
                    pe.wait_ge(a_w, 48 * e + 48)
                    for t in range(TT):
                        c = TT * e + t
                        for g in range(2):
                            for k in range(KC):
                                mm = pe.matmul(pbank[1 + g][:], g_hT[t][:, k], wg_sb[0][:, g, k],
                                               start=(k == 0), stop=(k == KC - 1))
                        mm.then_inc(a_gu, 1)
                        pe.wait_ge(a_hid, c + 1)
                        pe.nop(nofuse=True)
                        for k in range(FC):
                            mm = pe.transpose(pbank[3][:, k * P:(k + 1) * P], g_hid[:, k * P:(k + 1) * P], ident)
                        mm.then_inc(a_T, 1)
                        pe.wait_ge(a_copied, c + 2 * TT + 1)
                        for half in range(2):
                            for k in range(FC):
                                mm = pe.matmul(pbank[4 + half][:], g_hidT[:, k], wd_sb[0][:, k, half * 512:(half + 1) * 512],
                                               start=(k == 0), stop=(k == FC - 1))
                        mm.then_inc(a_d, 1)
                        pe.wait_ge(a_acc, 2 * c + 3)

        @block.scalar
        def _(act):
            def scaled_copy(dst, src, scale):
                return nc.scalar.activation(dst, src, ACT.Identity, scale=scale)

            for t in range(TT):
                act.wait_ge(x_in_sb[t], 16)
                nc.scalar.activation(junk[:, t], x1[:, t], ACT.Square, accum_out=ssq[:, t:t + 1]).then_inc(sumsq_done, 1)
                act.wait_ge(ms_done, t + 1)
                nc.scalar.activation(root[:, t:t + 1], ssq[:, t:t + 1], ACT.Sqrt).then_inc(root_done, 1)
            act.wait_ge(consts_in, 48)
            for k in range(1, KC, 2):
                act.wait_ge(xT_done, k + 1)
                scaled_copy(hT[:, k], pbank[k][:], gmix[:, k:k + 1]).then_inc(hT_act, 1)

            def gla_q_evict(n, m):
                act.wait_ge(unit_done, n + 1)
                dst = gq[:, m] if m < HP else gk[:, m - HP]
                scaled_copy(dst, pbank[n % 2][:], DK ** -0.5 if m < HP else 1.0).then_inc(unit_evicted, 1)

            def gv_evict(n, t):
                act.wait_ge(unit_done, n + 1)
                nc.scalar.copy(gv[:, t], pbank[n % 2][:]).then_inc(unit_evicted, 1)

            act.wait_ge(sumsq_done, TT)
            act.wait_ge(unit_done, 1)
            nc.scalar.copy(lr, pbank[0][:]).then_inc(unit_evicted, 1)
            gla_q_evict(1, 0)
            for m in range(4):
                act.wait_ge(gates_done, m + 1)
                nc.scalar.activation(gz[:, m], pbank[2 + m][:], ACT.Identity, bias=bg[:, m:m + 1]).then_inc(z_done, 1)
            for m in range(1, 4):
                gla_q_evict(1 + m, m)
            act.wait_ge(z_done, 4)
            nc.scalar.activation(gd, gz, ACT.Abs).then_inc(abs_done, 1)
            act.wait_ge(abs_done, 1)
            nc.scalar.activation(gE, gd, ACT.Exp, scale=-1.0).then_inc(expa_done, 1)
            act.wait_ge(expa_done, 1)
            nc.scalar.activation(gd, gE, ACT.Ln, bias=1.0).then_inc(softp_done, 1)
            gv_evict(5, 0)
            act.wait_ge(d1_done, 2)
            nc.scalar.activation(gE, gd, ACT.Exp, scale=1.0 / 16).then_inc(e12_done, 1)
            nc.scalar.activation(gz, gd, ACT.Exp, scale=-1.0 / 16).then_inc(e12_done, 1)
            gv_evict(6, 1)
            act.wait_ge(d3_done, 2)
            act.wait_ge(q_rel_done, 1)
            nc.scalar.activation(gE, gd, ACT.Exp, scale=1.0 / 16).then_inc(e3_done, 1)
            gbn = gb.rearrange("p m (n i) -> p m n i", i=CHUNK)
            nc.scalar.activation(dec[:, 0:2], gbn[:, 0:2, :, CHUNK - 1], ACT.Exp, scale=1.0 / 16).then_inc(dec_done, 1)
            nc.scalar.activation(dec[:, 2:4], gbn[:, 2:4, :, 0], ACT.Exp, scale=1.0 / 16).then_inc(dec_done, 1)
            act.wait_ge(k_rel_done, 1)
            nc.scalar.activation(gz, gb, ACT.Exp, scale=1.0 / 16).then_inc(e4_done, 1)
            gv_evict(7, 2)
            gv_evict(8, 3)
            act.wait_ge(q_exp_done, 1)
            for t in range(TT):
                act.wait_ge(unit_done, 10 + t)
                nc.scalar.copy(rg[:, t], pbank[(9 + t) % 2][:])
                nc.scalar.activation(r_exp[:, t], pbank[(9 + t) % 2][:], ACT.Exp, scale=-1.0).then_inc(unit_evicted, 1)
            act.wait_ge(dec_done, 2)
            act.wait_ge(e4_done, 1)
            for m in range(4):
                act.wait_ge(kT_done, m + 1)
                nc.scalar.copy(k_rows[:, m].rearrange("p t j -> p (t j)"), pbank[6 + m % 2][:]).then_inc(k_rows_done, 1)
            act.wait_ge(scores_done, 2)
            act.wait_ge(st_zero, 1)
            for par in range(2):
                for c in range(2):
                    nc.scalar.copy(st[64 * c:64 * c + 64, par * 8:par * 8 + 8, 64 * c:64 * c + 64],
                                   pbank[4 + par][64 * c:64 * c + 64, :].rearrange("p (a i) -> p a i", i=CHUNK)
                                   ).then_inc(sb_copied, 1)
            for m in range(4):
                act.wait_ge(unit_done, 14 + m)
                nc.scalar.activation(na_q[:, m].rearrange("p (w r) -> p w r", r=ROWS),
                                     pbank[(13 + m) % 2][:].rearrange("p (r w) -> p w r", w=GRID_W),
                                     ACT.Identity, scale=NA_DIM ** -0.5).then_inc(unit_evicted, 1)
            act.wait_ge(k_dec_done, 1)
            for m in range(4):
                act.wait_ge(unit_done, 18 + m)
                nc.scalar.copy(na_k[:, m].rearrange("p (w r) -> p w r", r=ROWS),
                               pbank[(17 + m) % 2][:].rearrange("p (r w) -> p w r", w=GRID_W)).then_inc(unit_evicted, 1)

            def o_slice(t, h):
                hp, par = divmod(h, 2)
                c0 = (t % 2) * 256 + hp * DV
                return pbank[2 + 2 * par + t // 2][:, c0:c0 + DV]

            for t in range(TT):
                act.wait_ge(o_done, t // 2 * 2 + 2)
                for h in range(GLA_HEADS):
                    nc.scalar.activation(o_junk[:, 4 * t + h], o_slice(t, h), ACT.Square,
                                         accum_out=oss[:, t, h:h + 1]).then_inc(oss_done, 1)
            act.wait_ge(oms_done, 1)
            nc.scalar.activation(oroot, oss, ACT.Sqrt).then_inc(oroot_done, 1)
            def vT_evict(m):
                act.wait_ge(unit_done, 22 + m)
                nc.scalar.copy(vT[:, m].rearrange("p (w r) -> p w r", r=ROWS),
                               pbank[(21 + m) % 2][:].rearrange("p (r w) -> p w r", w=GRID_W)).then_inc(unit_evicted, 1)

            def na_exp(i):
                act.wait_ge(nmax_done, i + 1)
                for par in range(2):
                    nc.scalar.activation(probs[i % 4][:, par], probs[i % 4][:, par], ACT.Exp, bias=nmax[:, i, par:par + 1],
                                         accum_out=psum_[:, i, par:par + 1]).then_inc(exp_done, 1)

            vT_evict(0)
            vT_evict(1)
            for h in range(GLA_HEADS):
                act.wait_ge(yg_done, h + 1)
                nc.scalar.copy(yT[:, 4 + h], pbank[6 + h % 2][:]).then_inc(yg_evicted, 1)
            na_exp(0)
            na_exp(1)
            vT_evict(2)
            vT_evict(3)
            act.wait_ge(rg_done, TT)
            for i in range(0, 2 * BLOCKS - 1, 2):
                act.wait_ge(v_done, i + 1)
                nc.scalar.copy(na_v[:, i], pbank[V_BANKS[i % 4]][:]).then_inc(v_act, 1)

            NU = PAIRS * BLOCKS
            for i in range(2, NU + 4):
                if i - 2 < NU:
                    u = i - 2
                    act.wait_ge(pT_done, u + 1)
                    if u >= 2:
                        act.wait_ge(pv_done, u - 1)
                    nc.scalar.copy(probsT[u % 2].rearrange("p a b -> p (a b)"), pbank[6][:]).then_inc(pT_evicted, 1)
                if i < NU:
                    na_exp(i)
                if i >= 4 and (i - 4) % BLOCKS == BLOCKS - 1:
                    pair = (i - 4) // BLOCKS
                    act.wait_ge(yt_done, i - 3)
                    nc.scalar.copy(yT[:, pair].rearrange("p (r w) -> p w r", w=GRID_W),
                                   pbank[7][:].rearrange("p (w r) -> p w r", r=ROWS)).then_inc(yn_evicted, 1)

            def square(t):
                act.wait_ge(x1_done, 2 * (t + 1))
                nc.scalar.activation(junk2[t], x1[:, t], ACT.Square, accum_out=ssq2[:, t:t + 1]).then_inc(sumsq2_done, 1)

            def square_root(t):
                act.wait_ge(ms2_done, t + 1)
                nc.scalar.activation(root2[:, t:t + 1], ssq2[:, t:t + 1], ACT.Sqrt).then_inc(root2_done, 1)

            def x1_T_evict(t):
                act.wait_ge(h2T_done, t + 1)
                if t >= 2:
                    act.wait_ge(lg_done, t - 1)
                nc.scalar.copy(hT2[t % 2][:, 0:4].rearrange("p a b -> p (a b)"), pbank[4][:]).then_inc(h2T_act, 1)

            def hi(t):
                act.wait_ge(sumsq2_done, t + 1)
                act.wait_ge(h2_done, t + 1)
                nc.scalar.copy(h2_part[t][0], h2_by_chunk(t)).then_inc(hi_done, 1)

            def mid(t):
                act.wait_ge(rest_done, t + 1)
                nc.scalar.copy(h2_part[t][1], h2_by_chunk(t)).then_inc(mid_done, 1)

            for stage, t in ((square, 0), (square_root, 0), (square, 1), (x1_T_evict, 0), (hi, 0), (square_root, 1),
                             (x1_T_evict, 1), (mid, 0), (hi, 1), (square, 2), (square_root, 2), (mid, 1), (x1_T_evict, 2),
                             (hi, 2), (mid, 2), (square, 3), (x1_T_evict, 3), (square_root, 3), (hi, 3), (mid, 3)):
                stage(t)
            act.wait_ge(cdiff_done, 1)
            nc.scalar.activation(gexp, gexp, ACT.Exp).then_inc(cexp_done, 1)
            act.wait_ge(cdiff_done, 2)
            nc.scalar.activation(eexp, ediff, ACT.Exp).then_inc(cexp_done, 1)

            def silu(s, c):
                act.wait_ge(gu_done, c + 1)
                nc.scalar.activation(hid[s], pbank[s][:, 0:256], ACT.Silu).then_inc(sil_done, 1)

            def hidden_T_evict(s, c):
                act.wait_ge(ht_done, c + 1)
                nc.scalar.copy(hidT.rearrange("p c h t -> p (c h t)"), pbank[4][:, 0:256]).then_inc(ht_evicted, 1)

            def rows_store(e, c, s):
                act.wait_ge(y_evicted, c + 1)
                for half in range(2):
                    act.dma_start(rows_out_d[e, half], y_sb[s][64 * half:64 * half + 64]).then_inc(y_stored[s], 16)

            with act.Fori(0, (EXPERTS - 2) // RING) as i:
                for s in range(RING):
                    silu(s, RING * i + s)
                    hidden_T_evict(s, RING * i + s)
                    rows_store(RING * i + s, RING * i + s, s)
            for e in (EXPERTS - 2, EXPERTS - 1):
                silu(e % RING, e)
                hidden_T_evict(e % RING, e)
                rows_store(e, e, e % RING)

            act.wait_ge(most_done, 1)
            general = act.value_load(most[0:1, 0:1], min_val=0, max_val=T)
            with act.If(general > limit):
                for c in range(2 * TT):
                    act.wait_ge(a_T, c + 1)
                    nc.scalar.copy(g_hT[c // 2][:, 4 * (c % 2):4 * (c % 2) + 4].rearrange("p a b -> p (a b)"),
                                   pbank[0][:]).then_inc(a_copied, 1)
                with act.Fori(0, EXPERTS) as e:
                    for t in range(TT):
                        c = TT * e + t
                        act.wait_ge(a_gu, c + 1)
                        nc.scalar.activation(g_sil, pbank[1][:], ACT.Silu).then_inc(a_sil, 1)
                        act.wait_ge(a_T, c + 2 * TT + 1)
                        nc.scalar.copy(g_hidT.rearrange("p a b -> p (a b)"), pbank[3][:]).then_inc(a_copied, 1)

            for t in range(TT):
                act.wait_ge(x2_done, t + 1)
                nc.scalar.activation(junk3[:, t], x2[:, t], ACT.Square, accum_out=ssq3[:, t:t + 1]).then_inc(sumsq3_done, 1)
                act.wait_ge(ms3_done, t + 1)
                nc.scalar.activation(root3[:, t:t + 1], ssq3[:, t:t + 1], ACT.Sqrt).then_inc(root3_done, 1)
                if t < POOL_TILES:
                    act.wait_ge(rstd3_done, t + 1)
                    act.wait_ge(sumsq3_done, t + 1)
                    nc.scalar.activation(junk3[:, t], x2[:, t], ACT.Identity, scale=rstd3[:, t:t + 1]).then_inc(xr_done, 1)

        @block.vector
        def _(dve):
            def tt(out_, a, b, op):
                return nc.vector.tensor_tensor(out_, a, b, op)

            for t in range(TT):
                dve.wait_ge(sumsq_done, t + 1)
                nc.vector.tensor_scalar(ssq[:, t:t + 1], ssq[:, t:t + 1], 1.0 / D, EPS, ALU.mult, ALU.add).then_inc(ms_done, 1)
                dve.wait_ge(root_done, t + 1)
                nc.vector.reciprocal(rstd[:, t:t + 1], root[:, t:t + 1]).then_inc(rstd_done, 1)
                dve.wait_ge(rstd_done, t + 1)
                nc.vector.tensor_scalar(xs[:, t], x1[:, t], rstd[:, t:t + 1], None, ALU.mult).then_inc(xs_done, 1)
            dve.wait_ge(small_in, 16)
            dve.wait_ge(consts_in, 48)
            for k in range(0, KC, 2):
                dve.wait_ge(xT_done, k + 1)
                nc.vector.tensor_scalar(hT[:, k], pbank[k][:], gmix[:, k:k + 1], None, ALU.mult).then_inc(hT_vec, 1)

            dve.wait_ge(softp_done, 1)
            nc.vector.scalar_tensor_tensor(gz, gz, 0.0, gd, ALU.min, ALU.subtract).then_inc(g_done, 1)
            dve.wait_ge(g_done, 1)
            dve.wait_ge(late_in, 48)
            for m in range(4):
                src, dst = (gz[:, m], gb[:, m]) if m < 2 else (gz[:, m, ::-1], gb[:, m, ::-1])
                nc.vector.tensor_tensor_scan(dst, scan_keep, src, 0.0, ALU.mult, ALU.add).then_inc(scan_done, 1)
            dve.wait_ge(scan_done, 4)
            gb_n = gb.rearrange("p m (n i) -> p (m n) i", i=CHUNK)
            gd_n = gd.rearrange("p m (n i) -> p (m n) i", i=CHUNK)
            half = 2 * NCH

            def spread(v, d, i):
                return v[:, d * half:(d + 1) * half, i:i + 1].broadcast_to((P, half, CHUNK))

            for d in range(2):
                ref = CHUNK // 2 - 1 if d == 0 else CHUNK // 2
                tt(gd_n[:, d * half:(d + 1) * half], gb_n[:, d * half:(d + 1) * half], spread(gb_n, d, ref),
                   ALU.subtract).then_inc(d1_done, 1)

            def per_dir(v):
                return v.rearrange("p (d m) t -> p d (m t)", d=2)

            def same_dirs(v):
                return v.rearrange("p m t -> p (m t)").unsqueeze(1).broadcast_to((P, 2, HP * T))

            dve.wait_ge(e12_done, 1)
            dve.wait_ge(unit_evicted, 3)
            dve.wait_ge(xT_done, KC)
            tt(per_dir(q_rel), per_dir(gE), same_dirs(gq), ALU.mult).then_inc(q_rel_done, 1)
            dve.wait_ge(e12_done, 2)
            for d in range(2):
                tt(gd_n[:, d * half:(d + 1) * half], spread(gb_n, d, CHUNK - 1 if d == 0 else 0),
                   gb_n[:, d * half:(d + 1) * half], ALU.subtract).then_inc(d3_done, 1)
            dve.wait_ge(e4_done, 1)
            tt(per_dir(q_exp), per_dir(gz), same_dirs(gq), ALU.mult).then_inc(q_exp_done, 1)

            for t in range(TT):
                dve.wait_ge(unit_evicted, 10 + t)
                nc.vector.tensor_scalar(r_exp[:, t], r_exp[:, t], 1.0, None, ALU.add).then_inc(r_step, 1)
                dve.wait_ge(r_step, 3 * t + 1)
                nc.vector.reciprocal(r_exp[:, t], r_exp[:, t]).then_inc(r_step, 1)
                dve.wait_ge(r_step, 3 * t + 2)
                tt(rg[:, t], rg[:, t], r_exp[:, t], ALU.mult).then_inc(r_step, 1)
                dve.wait_ge(r_step, 3 * t + 3)
                gain = gla_gb.unsqueeze(1).broadcast_to((P, GLA_HEADS, DV))
                rv = rg[:, t].rearrange("p (h v) -> p h v", v=DV)
                tt(rv, rv, gain, ALU.mult).then_inc(rg_done, 1)
            dve.wait_ge(sb_copied, 4)
            for par in range(2):
                for c in range(2):
                    cm = causal[64 * c:64 * c + 64].bitcast(U32).unsqueeze(1).broadcast_to((64, 8, CHUNK))
                    nc.vector.copy_predicated(st[64 * c:64 * c + 64, par * 8:par * 8 + 8, 64 * c:64 * c + 64], cm,
                                              pbank[2 + par][64 * c:64 * c + 64, :].rearrange("p (a i) -> p a i", i=CHUNK)
                                              ).then_inc(st_done, 1)
            dve.wait_ge(rg_done, TT)
            for s in range(NCH - 1):
                dve.wait_ge(state_done, min(s // 2 * 2 + 2, NCH - 1))
                if s:
                    dve.wait_ge(state_used, 4 * s)
                for d in range(2):
                    n, nxt = (s, s + 1) if d == 0 else (NCH - 1 - s, NCH - 2 - s)
                    for hp in range(HP):
                        m = 2 * d + hp
                        new = pbank[6 + n % 2][:, d * 256 + hp * DV:d * 256 + (hp + 1) * DV]
                        if s == 0:
                            nc.vector.tensor_copy(s_prev[:, m, nxt], new).then_inc(state_used, 1)
                        else:
                            nc.vector.scalar_tensor_tensor(s_prev[:, m, nxt], s_prev[:, m, n], dec[:, m, n:n + 1], new,
                                                           ALU.mult, ALU.add).then_inc(state_used, 1)
            dve.wait_ge(oss_done, 16)
            nc.vector.tensor_scalar(oss, oss, 1.0 / DV, EPS, ALU.mult, ALU.add).then_inc(oms_done, 1)
            dve.wait_ge(oroot_done, 1)
            nc.vector.reciprocal(orstd, oroot).then_inc(orstd_done, 1)
            dve.wait_ge(orstd_done, 1)
            for t in range(TT):
                for h in range(GLA_HEADS):
                    hp, par = divmod(h, 2)
                    c0 = (t % 2) * 256 + hp * DV
                    nc.vector.scalar_tensor_tensor(o_rows[:, t, h * DV:(h + 1) * DV],
                                                   pbank[2 + 2 * par + t // 2][:, c0:c0 + DV], orstd[:, t, h:h + 1],
                                                   rg[:, t, h * DV:(h + 1) * DV], ALU.mult, ALU.mult).then_inc(y_done, 1)

            NU = PAIRS * BLOCKS
            nc.vector.tensor_copy(upper_b[:], upper).then_inc(router_ready, 1)
            nc.vector.memset(ones_b[:], 1.0).then_inc(router_ready, 1)
            dve.wait_ge(g2_in, 48)
            tt(wr_sb, wr_sb, gffn.unsqueeze(2).broadcast_to((P, KC, GROUPS + EXPERTS)), ALU.mult).then_inc(router_ready, 1)
            dve.wait_ge(bias_done, 3 * NA_HEADS)
            for i in range(NU + 5):
                if i == 2:
                    for v in range(1, 2 * BLOCKS - 1, 2):
                        dve.wait_ge(v_done, v + 1)
                        nc.vector.tensor_copy(na_v[:, v], pbank[V_BANKS[v % 4]][:]).then_inc(v_vec, 1)
                if i % 2 == 0 and i >= 6:
                    j = i // 2 - 3
                    dve.wait_ge(og_done, j + 1)
                    xv = x1[:, j // 2, (j % 2) * 512:(j % 2 + 1) * 512]
                    tt(xv, xv, pbank[GLA_BANK[j]][:], ALU.add).then_inc(og_added, 1)
                if i < NU:
                    pair, b = divmod(i, BLOCKS)
                    dve.wait_ge(s_done, i + 1)
                    if i >= 4:
                        dve.wait_ge(pT_done, i - 3)
                    for par in range(2):
                        tt(probs[i % 4][:, par], pbank[2 + 2 * (i % 2) + par][:, 0:NKEY], bias[:, 2 * pair + par, BIAS_VAR[b]],
                           ALU.add).then_inc(s_added, 1)
                    dve.wait_ge(s_added, 2 * (i + 1))
                    nc.vector.tensor_reduce(nmax[:, i], probs[i % 4], AX.X, ALU.max, negate=True).then_inc(nmax_done, 1)
                if 1 <= i <= NU:
                    dve.wait_ge(exp_done, 2 * i)
                    nc.vector.reciprocal(rsum[:, i - 1], psum_[:, i - 1]).then_inc(rsum_done, 1)
                if 3 <= i < NU + 3:
                    u = i - 3
                    dve.wait_ge(pv_done, u + 1)
                    dve.wait_ge(rsum_done, u + 1)
                    if u >= 2:
                        dve.wait_ge(yt_done, u - 1)
                    tt(y_rows[u % 2].rearrange("p (h d) -> p h d", h=2), pbank[1][:, 0:P].rearrange("p (h d) -> p h d", h=2),
                       rsum[:, u].unsqueeze(2).broadcast_to((P, 2, NA_DIM)), ALU.mult).then_inc(y_scaled, 1)

            n_step = [0]

            def then(ins):
                n_step[0] += 1
                ins.then_inc(route_step, 1)
                dve.wait_ge(route_step, n_step[0])

            def route(t0, t1):
                dve.wait_ge(lg_done, t1)
                n = t1 - t0
                ts = slice(t0, t1)
                for t in range(t0, t1):
                    lp = pbank[6 + t % 2][:, 0:GROUPS + EXPERTS]
                    nc.vector.scalar_tensor_tensor(lg[:, t, 0:GROUPS], lp[:, 0:GROUPS], rstd2[:, t:t + 1],
                                                   b_r_sb[:, 0:GROUPS], ALU.mult, ALU.add)
                    nc.vector.scalar_tensor_tensor(lg[:, t, 8:], lp[:, GROUPS:], rstd2[:, t:t + 1],
                                                   b_r_sb[:, GROUPS:], ALU.mult, ALU.add).then_inc(lg_evicted, 1)
                dve.wait_ge(lg_evicted, t1)
                for t in range(t0, t1):
                    m = nc.vector.max(gtop[:, t], lg[:, t, 0:8])
                then(m)
                for t in range(t0, t1):
                    m = nc.vector.max_index(itop8[:, t], gtop[:, t], lg[:, t, 0:8])
                then(m)
                then(nc.vector.tensor_copy(gidx[:, ts], itop8[:, ts, 0:1]))
                then(tt(ghot[:, ts], iota[:, 0:GROUPS].unsqueeze(1).broadcast_to((P, n, GROUPS)),
                        gidx[:, ts].broadcast_to((P, n, GROUPS)), ALU.is_equal))
                for t in range(t0, t1):
                    m = tt(prod[:, t].rearrange("p (g e) -> p g e", g=GROUPS), lg[:, t, 8:].rearrange("p (g e) -> p g e", g=GROUPS),
                           ghot[:, t].unsqueeze(2).broadcast_to((P, GROUPS, PER_GROUP)), ALU.mult)
                then(m)
                for t in range(t0, t1):
                    m = nc.vector.tensor_reduce(ing[:, t], prod[:, t].rearrange("p (g e) -> p e g", g=GROUPS), AX.X, ALU.add)
                then(m)
                for t in range(t0, t1):
                    m = nc.vector.max(etop[:, t], ing[:, t])
                then(m)
                for t in range(t0, t1):
                    m = nc.vector.max_index(eidx[:, t], etop[:, t], ing[:, t])
                then(m)
                then(nc.vector.tensor_copy(eid[:, ts], eidx[:, ts, 0:2]))
                then(nc.vector.scalar_tensor_tensor(eid[:, ts], gidx[:, ts].broadcast_to((P, n, 2)), float(PER_GROUP),
                                                    eid[:, ts], ALU.mult, ALU.add))
                for k in range(2):
                    m = tt(hot[k][:, ts], iota[:, 0:EXPERTS].unsqueeze(1).broadcast_to((P, n, EXPERTS)),
                           eid[:, ts, k:k + 1].broadcast_to((P, n, EXPERTS)), ALU.is_equal)
                then(m)
                tt(both_b[:, ts], hot[0][:, ts], hot[1][:, ts], ALU.add).then_inc(both_done, n)

            nc.vector.memset(lg[:, :, GROUPS:8], LOWEST)
            dve.wait_ge(og_added, 2 * TT)

            def residual(t):
                for half in range(2):
                    dve.wait_ge(wo_done, 2 * t + half + 1)
                    xv = x1[:, t, half * 512:(half + 1) * 512]
                    tt(xv, xv, pbank[2 * (t % 2) + half][:], ALU.add).then_inc(x1_done, 1)

            def norm2(t):
                dve.wait_ge(sumsq2_done, t + 1)
                nc.vector.tensor_scalar(ssq2[:, t:t + 1], ssq2[:, t:t + 1], 1.0 / D, EPS, ALU.mult, ALU.add).then_inc(ms2_done, 1)
                dve.wait_ge(root2_done, t + 1)
                nc.vector.reciprocal(rstd2[:, t:t + 1], root2[:, t:t + 1]).then_inc(rstd2_done, 1)
                dve.wait_ge(rstd2_done, t + 1)
                if t >= 2:
                    dve.wait_ge(parts_done, t - 1)
                nc.vector.scalar_tensor_tensor(h2[t % 2], x1[:, t], rstd2[:, t:t + 1], g2b, ALU.mult, ALU.mult).then_inc(h2_done, 1)

            def x1_T_evict(t):
                dve.wait_ge(h2T_done, t + 1)
                if t >= 2:
                    dve.wait_ge(lg_done, t - 1)
                nc.vector.tensor_copy(hT2[t % 2][:, 4:8].rearrange("p a b -> p (a b)"), pbank[5][:]).then_inc(h2T_vec, 1)

            residual(0)
            norm2(0)
            residual(1)
            x1_T_evict(0)
            norm2(1)
            x1_T_evict(1)
            residual(2)
            norm2(2)
            x1_T_evict(2)
            route(0, 2)
            residual(3)
            x1_T_evict(3)
            norm2(3)
            route(2, 4)
            dve.wait_ge(mid_done, TT)
            ks = slice(KC // 2, KC)
            tt(h2_part[TT - 1][2][:, ks], h2_by_chunk(TT - 1)[:, ks], h2_part[TT - 1][1][:, ks],
               ALU.subtract).then_inc(parts_done, 1)

            dve.wait_ge(rank_mm_done, 1)
            cum = pbank[6][:, 0:TT * EXPERTS].rearrange("p (t e) -> p t e", e=EXPERTS)
            then(nc.vector.scalar_tensor_tensor(code, cum, 1.0, both_b[:], ALU.add, ALU.mult))
            then(nc.vector.tensor_scalar(code, code, 1.0, None, ALU.subtract))

            def pick_slots(s, e, c):
                nc.vector.tensor_tensor(pick[s], iota.unsqueeze(1).broadcast_to((P, TT, SLOTS)),
                                        code[:, :, bass.ds(e, 1)].broadcast_to((P, TT, SLOTS)), ALU.is_equal).then_inc(picked, 1)

            def slots_and_weights():
                nc.vector.tensor_reduce(most, pbank[6][:, TT * EXPERTS:(TT + 1) * EXPERTS], AX.X, ALU.max).then_inc(most_done, 1)
                tt(gexp, lg[:, :, 0:GROUPS], gtop[:, :, 0:1].broadcast_to((P, TT, GROUPS)), ALU.subtract).then_inc(cdiff_done, 1)
                tt(ediff, etop[:, :, 1:2], etop[:, :, 0:1], ALU.subtract).then_inc(cdiff_done, 1)
                for k in range(2):
                    then(tt(prod, hot[k], cum, ALU.mult))
                    then(nc.vector.tensor_reduce(rank[:, :, k:k + 1], prod, AX.X, ALU.add))
                then(nc.vector.scalar_tensor_tensor(slotf, eid, float(SLOTS), rank, ALU.mult, ALU.add))
                nc.vector.tensor_copy(slot, slotf).then_inc(slots_done, 1)
                dve.wait_ge(cexp_done, 1)
                then(nc.vector.tensor_reduce(gsum, gexp, AX.X, ALU.add))
                dve.wait_ge(cexp_done, 2)
                then(nc.vector.tensor_scalar(eden, eexp, 1.0, None, ALU.add))
                then(tt(eden, eden, gsum, ALU.mult))
                then(nc.vector.reciprocal(comb[:, :, 0:1], eden))
                then(tt(comb[:, :, 1:2], comb[:, :, 0:1], eexp, ALU.mult))

            def rows_T_evict(s, c):
                dve.wait_ge(xt_done, c + 1)
                nc.vector.tensor_copy(xT.rearrange("p k t -> p (k t)"), pbank[3][:]).then_inc(xt_evicted, 1)

            def hidden(s, c):
                dve.wait_ge(sil_done, c + 1)
                tt(hid[s], pbank[s][:, 256:512], hid[s], ALU.mult).then_inc(hid_done, 1)

            def y_evict(s, c, stored):
                dve.wait_ge(d_done, c + 1)
                if stored is not None:
                    dve.wait_ge(y_stored[s], 32 * stored)
                nc.vector.tensor_copy(y_sb[s], pbank[5 + s][:]).then_inc(y_evicted, 1)

            pick_slots(0, 0, 0)
            rows_T_evict(0, 0)
            pick_slots(1, 1, 1)
            slots_and_weights()
            for e in range(RING):
                if e:
                    pick_slots((e + 1) % RING, e + 1, e + 1)
                hidden(e, e)
                rows_T_evict((e + 1) % RING, e + 1)
                y_evict(e, e, None)
            with dve.Fori(1, (EXPERTS - 2) // RING) as i:
                for s in range(RING):
                    e = RING * i + s
                    pick_slots((s + 1) % RING, e + 1, e + 1)
                    hidden(s, e)
                    rows_T_evict((s + 1) % RING, e + 1)
                    y_evict(s, e, i)
            for e in (EXPERTS - 2, EXPERTS - 1):
                if e < EXPERTS - 1:
                    pick_slots((e + 1) % RING, e + 1, e + 1)
                hidden(e % RING, e)
                if e < EXPERTS - 1:
                    rows_T_evict((e + 1) % RING, e + 1)
                y_evict(e % RING, e, e // RING)

            def final_norm(t):
                dve.wait_ge(sumsq3_done, t + 1)
                nc.vector.tensor_scalar(ssq3[:, t:t + 1], ssq3[:, t:t + 1], 1.0 / D, EPS, ALU.mult, ALU.add).then_inc(ms3_done, 1)
                dve.wait_ge(root3_done, t + 1)
                nc.vector.reciprocal(rstd3[:, t:t + 1], root3[:, t:t + 1]).then_inc(rstd3_done, 1)
                dve.wait_ge(rstd3_done, t + 1)
                if t >= POOL_TILES:
                    nc.vector.scalar_tensor_tensor(res[:, t], x2[:, t], rstd3[:, t:t + 1], gfb, ALU.mult,
                                                   ALU.mult).then_inc(res_done, 1)

            dve.wait_ge(gf_in, 16)
            dve.wait_ge(most_done, 1)
            general = dve.value_load(most[0:1, 0:1], min_val=0, max_val=T)
            with dve.If(general > limit):
                nc.vector.tensor_copy(ident_b, ident).then_inc(a_col, 1)
                dve.wait_ge(d_done, EXPERTS)
                for t in range(TT):
                    nc.vector.tensor_scalar(g_cw[:, t], hot[0][:, t], comb[:, t, 0:1], None, ALU.mult).then_inc(a_cw, 1)
                    dve.wait_ge(a_cw, 2 * t + 1)
                    nc.vector.scalar_tensor_tensor(g_cw[:, t], hot[1][:, t], comb[:, t, 1:2], g_cw[:, t], ALU.mult,
                                                   ALU.add).then_inc(a_cw, 1)
                nc.vector.tensor_copy(x2, x1).then_inc(a_acc, 1)
                dve.wait_ge(a_cw, 2 * TT)
                with dve.Fori(0, EXPERTS) as e:
                    dve.wait_ge(a_acc, 2 * TT * e + 1)
                    nc.vector.tensor_copy(g_col, g_cw[:, :, bass.ds(e, 1)]).then_inc(a_col, 1)
                    dve.wait_ge(a_col, e + 2)
                    for t in range(TT):
                        c = TT * e + t
                        dve.wait_ge(a_sil, c + 1)
                        tt(g_hid, pbank[2][:], g_sil, ALU.mult).then_inc(a_hid, 1)
                        dve.wait_ge(a_d, c + 1)
                        for hf in range(2):
                            acc = x2[:, t, hf * 512:(hf + 1) * 512]
                            nc.vector.scalar_tensor_tensor(acc, pbank[4 + hf][:], g_col[:, t], acc, ALU.mult,
                                                           ALU.add).then_inc(a_acc, 1)
                dve.wait_ge(a_acc, 2 * TT * EXPERTS + 1)
                for t in range(TT):
                    nc.vector.tensor_copy(x2[:, t, 0:1], x2[:, t, 0:1]).then_inc(x2_done, 1)
                for t in range(TT):
                    final_norm(t)
            with dve.If(general < limit + 1):
                for t in range(TT):
                    dve.wait_ge(gathered[t][0], 16)
                    nc.vector.scalar_tensor_tensor(x2[:, t], got[t][0], comb[:, t, 0:1], x1[:, t], ALU.mult,
                                                   ALU.add).then_inc(x2_half, 1)
                    dve.wait_ge(x2_half, t + 1)
                    dve.wait_ge(gathered[t][1], 16)
                    nc.vector.scalar_tensor_tensor(x2[:, t], got[t][1], comb[:, t, 1:2], x2[:, t], ALU.mult,
                                                   ALU.add).then_inc(x2_done, 1)
                    if t >= 1:
                        final_norm(t - 1)
                final_norm(TT - 1)

        @block.gpsimd
        def _(pool):
            pool.wait_ge(bias_in, 16 * NA_HEADS + 16)
            for h in range(NA_HEADS):
                for v in range(3):
                    u0 = WIN_W - v * WIN_W // 2
                    first = rpb_run[:, h, RPB_RUN - 1 - u0:RPB_RUN - u0]
                    run = bass.AP(first.tensor, first.offset, [first.ap[0], [-1, KEY_W], [-RPB_W, ROWS]])
                    nc.gpsimd.tensor_tensor(bias[:, h, v].rearrange("p (j r) -> p j r", r=ROWS), run,
                                            mask[:, v].rearrange("p (j r) -> p j r", r=ROWS), ALU.add).then_inc(bias_done, 1)
            pool.wait_ge(bias_done, 3 * NA_HEADS)
            pool.wait_ge(e12_done, 2)
            pool.wait_ge(unit_evicted, 5)

            def per_dir(v):
                return v.rearrange("p (d m) t -> p d (m t)", d=2)

            keys = gk.rearrange("p m t -> p (m t)").unsqueeze(1).broadcast_to((P, 2, HP * T))
            nc.gpsimd.tensor_tensor(per_dir(k_rel), per_dir(gz), keys, ALU.mult).then_inc(k_rel_done, 1)
            pool.wait_ge(e3_done, 1)
            nc.gpsimd.tensor_tensor(per_dir(k_dec), per_dir(gE), keys, ALU.mult).then_inc(k_dec_done, 1)
            pool.wait_ge(q_exp_done, 1)
            pool.wait_ge(k_dec_done, 1)
            nc.gpsimd.memset(st, 0.0).then_inc(st_zero, 1)

            for t in range(TT):
                pool.wait_ge(hi_done, t + 1)
                nc.gpsimd.tensor_tensor(h2_by_chunk(t), h2_by_chunk(t), h2_part[t][0], ALU.subtract).then_inc(rest_done, 1)
                pool.wait_ge(mid_done, t + 1)
                ks = slice(0, KC if t < TT - 1 else KC // 2)
                nc.gpsimd.tensor_tensor(h2_part[t][2][:, ks], h2_by_chunk(t)[:, ks], h2_part[t][1][:, ks],
                                        ALU.subtract).then_inc(parts_done, 1)

            pool.wait_ge(slots_done, 1)
            for s in range(RING):
                pool.wait_ge(y_stored[s], 32 * len(range(s, EXPERTS, RING)))
            pool.wait_ge(most_done, 1)
            general = pool.value_load(most[0:1, 0:1], min_val=0, max_val=T)
            with pool.If(general < limit + 1):
                for t in range(TT):
                    for k in range(2):
                        nc.gpsimd.indirect_dma_start(got[t][k], None, rows_out,
                                                     bass.IndirectOffsetOnAxis(ap=slot[:, t, k:k + 1], axis=0)
                                                     ).then_inc(gathered[t][k], 16)
            pool.wait_ge(gf_in, 16)
            for t in range(POOL_TILES):
                pool.wait_ge(xr_done, t + 1)
                nc.gpsimd.tensor_tensor(res[:, t], junk3[:, t], gfb, ALU.mult).then_inc(res_pool, 1)


def constants():
    import numpy as np
    c = np.zeros((P, 384), np.float32)
    c[:, 0:128] = np.eye(P)
    c[:, 128:256] = np.triu(np.ones((P, P)), 1)
    j, i = np.meshgrid(np.arange(P) % CHUNK, np.arange(CHUNK), indexing="ij")
    c[:, 256:320] = j <= i
    c[:, 320:384] = np.arange(SLOTS)
    mask = np.full((P, 3, KEY_W, ROWS), NEG, np.float32)
    for var, b in enumerate((0, 1, BLOCKS - 1)):
        for wl in range(BLK_W):
            w = b * BLK_W + wl
            s = min(max(w - WIN_W // 2, 0), GRID_W - WIN_W) - KEY_START[b]
            mask[wl * ROWS:(wl + 1) * ROWS, var, s:s + WIN_W] = 0
    scan = np.ones((P, T), np.float32)
    scan[:, ::CHUNK] = 0
    return c, mask.reshape(P, -1), scan


def kernel(**inputs):
    import numpy as np
    import concourse.bacc as bacc
    from concourse.bass_utils import run_bass_kernel_spmd as run

    nc = bacc.Bacc("TRN2", target_bir_lowering=False, num_devices=1)
    a = {k: np.asarray(v) for k, v in inputs.items()}
    w_g2 = np.zeros((2 * RANK, 512), np.float32)
    w_g2[0:RANK, 0:256] = a["w_g2_f"][0]
    w_g2[RANK:, 256:512] = a["w_g2_b"][0]
    c_small, c_mask, c_scan = constants()
    ins = {
        "x": a["x"],
        "rpb": np.pad(a["rpb"][0, :, ::-1, ::-1].reshape(-1), (RPB_PAD, 64)),
        "w_in": a["w_in"],
        "w_g2": np.tile(w_g2, (4, 1)),
        "b_g": np.concatenate([a["b_g_f"][0], a["b_g_b"][0]]).reshape(4, P).T,
        "gla_g": a["gla_norm_g"],
        "g_mix": a["norm_mix_g"][0].reshape(KC, P).T,
        "w_out": a["w_out"],
        "g_ffn": a["norm_ffn_g"],
        "g_ffn_T": a["norm_ffn_g"][0].reshape(KC, P).T,
        "w_r": np.concatenate([a["w_grp"][0], a["w_exp"][0]], axis=1).reshape(KC, P, -1).transpose(1, 0, 2),
        "b_r": np.concatenate([a["b_grp"], a["b_exp"]], axis=1),
        "w_gate": a["w_gate"], "w_up": a["w_up"], "w_down": a["w_down"],
        "g_fin": a["final_norm_g"].reshape(1, -1),
        "c_small": c_small, "c_mask": c_mask, "c_scan": c_scan,
    }
    arrays, args = {}, []
    for name, v in ins.items():
        v = np.ascontiguousarray(v)
        arrays["in_" + name] = v
        args.append(nc.dram_tensor("in_" + name, v.shape, mybir.dt.from_np(v.dtype), kind="ExternalInput").ap())
    args.append(nc.dram_tensor("out0", (1, T, D), F32, kind="ExternalOutput").ap())
    mixer_and_moe(nc, *args)
    return run(nc, [arrays], core_ids=[0]).results[0]["out0"]
```
